# Optimizing a Trainium2 kernel written in Bass

```python
import math
import jax, jax.numpy as jnp
from jax import lax
import numpy as np

D_MODEL = 1024
BATCH = 1
SEQ = 256
DEPTH = 2

ROPE_THETA = 10000.0
NORM_EPS = 1e-6
Q_BLOCK = 128

MOBA_HEADS = 8
MOBA_HEAD_DIM = 64
MOBA_BLOCK = 256
MOBA_TOPK = 3
MOBA_Q_CHUNK = 32

DIFF_HEADS = 4
DIFF_HEAD_DIM = 64
DIFF_V_DIM = 2 * DIFF_HEAD_DIM

MOBA_W = MOBA_HEADS * MOBA_HEAD_DIM
DIFF_QK_W = DIFF_HEADS * 2 * DIFF_HEAD_DIM
DIFF_V_W = DIFF_HEADS * DIFF_V_DIM
EVEN_IN = 3 * MOBA_W + 2 * DIFF_QK_W + DIFF_V_W
EVEN_MIX = MOBA_W + DIFF_V_W
EVEN_SPLITS = (MOBA_W, 2 * MOBA_W, 3 * MOBA_W, 3 * MOBA_W + DIFF_QK_W, 3 * MOBA_W + 2 * DIFF_QK_W)

MLA_HEADS = 16
MLA_Q_RANK = 256
MLA_KV_RANK = 128
MLA_NOPE = 64
MLA_ROPE = 32
MLA_V = 64
ODD_IN = MLA_Q_RANK + MLA_KV_RANK + MLA_ROPE
ODD_MIX = MLA_HEADS * MLA_V

N_GROUPS = 4
EXPERTS_PER_GROUP = 8
N_EXPERTS = N_GROUPS * EXPERTS_PER_GROUP
EXPERT_TOPK = 2
EXPERT_FF = 256

N_EVEN = (DEPTH + 1) // 2
N_ODD = DEPTH // 2

kernel_name = "hybrid_moba_diffattn_mla_hiermoe"

def rms_norm(x, g):
    xf = x.astype(jnp.float32)
    y = xf * lax.rsqrt(jnp.mean(xf * xf, axis=-1, keepdims=True) + NORM_EPS)
    return (y * g.astype(jnp.float32)).astype(x.dtype)

def rope_tables(seq, dim):
    inv = 1.0 / (ROPE_THETA ** (jnp.arange(0, dim, 2, dtype=jnp.float32) / dim))
    ang = jnp.arange(seq, dtype=jnp.float32)[:, None] * inv[None, :]
    return jnp.cos(ang), jnp.sin(ang)

def apply_rope(x, cos, sin):
    shp = (1, cos.shape[0]) + (1,) * (x.ndim - 3) + (cos.shape[1],)
    c = cos.reshape(shp).astype(x.dtype)
    s = sin.reshape(shp).astype(x.dtype)
    h = x.shape[-1] // 2
    x1, x2 = x[..., :h], x[..., h:]
    return jnp.concatenate([x1 * c - x2 * s, x1 * s + x2 * c], axis=-1)

def causal_attention(q, k, v, scale):
    B, S, H, dk = q.shape
    nq = S // Q_BLOCK
    qb = q.reshape(B, nq, Q_BLOCK, H, dk).transpose(1, 0, 3, 2, 4)
    kt = k.transpose(0, 2, 1, 3)
    vt = v.transpose(0, 2, 1, 3)
    kpos = jnp.arange(S)

    def step(args):
        q_blk, i = args
        qpos = i * Q_BLOCK + jnp.arange(Q_BLOCK)
        s = jnp.einsum('bhqd,bhkd->bhqk', q_blk, kt).astype(jnp.float32) * scale
        s = jnp.where(kpos[None, :] <= qpos[:, None], s, -jnp.inf)
        p = jax.nn.softmax(s, axis=-1).astype(v.dtype)
        return jnp.einsum('bhqk,bhkd->bqhd', p, vt)

    o = lax.map(step, (qb, jnp.arange(nq)))
    return o.transpose(1, 0, 2, 3, 4).reshape(B, S, H, v.shape[-1])

def diff_attention(q1, q2, k1, k2, v, lam):
    B, S, H, d = q1.shape
    scale = d ** -0.5
    nq = S // Q_BLOCK

    def to_blocks(q):
        return q.reshape(B, nq, Q_BLOCK, H, d).transpose(1, 0, 3, 2, 4)

    k1t = k1.transpose(0, 2, 1, 3)
    k2t = k2.transpose(0, 2, 1, 3)
    vt = v.transpose(0, 2, 1, 3)
    kpos = jnp.arange(S)

    def step(args):
        q1b, q2b, i = args
        qpos = i * Q_BLOCK + jnp.arange(Q_BLOCK)
        causal = kpos[None, :] <= qpos[:, None]
        s1 = jnp.where(causal, jnp.einsum('bhqd,bhkd->bhqk', q1b, k1t).astype(jnp.float32) * scale, -jnp.inf)
        s2 = jnp.where(causal, jnp.einsum('bhqd,bhkd->bhqk', q2b, k2t).astype(jnp.float32) * scale, -jnp.inf)
        a = jax.nn.softmax(s1, axis=-1) - lam * jax.nn.softmax(s2, axis=-1)
        return jnp.einsum('bhqk,bhkd->bqhd', a.astype(v.dtype), vt)

    o = lax.map(step, (to_blocks(q1), to_blocks(q2), jnp.arange(nq)))
    return o.transpose(1, 0, 2, 3, 4).reshape(B, S, H, v.shape[-1])

def moba_attention(q, k, v):
    B, S, H, d = q.shape
    L = MOBA_BLOCK
    nb = -(-S // L)
    pad = nb * L - S
    kp = jnp.pad(k, ((0, 0), (0, pad), (0, 0), (0, 0)))
    vp = jnp.pad(v, ((0, 0), (0, pad), (0, 0), (0, 0)))
    kb = kp.reshape(B, nb, L, H, d).transpose(0, 3, 1, 2, 4)
    vb = vp.reshape(B, nb, L, H, d).transpose(0, 3, 1, 2, 4)
    kmean = jnp.mean(kb.astype(jnp.float32), axis=3).astype(k.dtype)
    topk_n = max(1, min(MOBA_TOPK, nb - 1))
    nc = S // MOBA_Q_CHUNK
    qc = q.reshape(B, nc, MOBA_Q_CHUNK, H, d).transpose(1, 0, 3, 2, 4)
    scale = d ** -0.5
    bidx = jnp.arange(nb)
    b_ar = jnp.arange(B)[:, None, None, None]
    h_ar = jnp.arange(H)[None, :, None, None]

    def step(args):
        q_blk, c = args
        qpos = c * MOBA_Q_CHUNK + jnp.arange(MOBA_Q_CHUNK)
        own = qpos[0] // L
        g = jnp.einsum('bhqd,bhnd->bhqn', q_blk, kmean).astype(jnp.float32)
        past = bidx[None, :] < (qpos // L)[:, None]
        g = jnp.where(past, g, -jnp.inf)
        gv, sel = lax.top_k(g, topk_n)
        valid = jnp.isfinite(gv)
        k_sel = kb[b_ar, h_ar, sel]
        v_sel = vb[b_ar, h_ar, sel]
        s_sel = jnp.einsum('bhqd,bhqnld->bhqnl', q_blk, k_sel).astype(jnp.float32) * scale
        s_sel = jnp.where(valid[..., None], s_sel, -jnp.inf).reshape(B, H, MOBA_Q_CHUNK, topk_n * L)
        k_own = lax.dynamic_index_in_dim(kb, own, axis=2, keepdims=False)
        v_own = lax.dynamic_index_in_dim(vb, own, axis=2, keepdims=False)
        s_own = jnp.einsum('bhqd,bhld->bhql', q_blk, k_own).astype(jnp.float32) * scale
        own_pos = own * L + jnp.arange(L)
        s_own = jnp.where(own_pos[None, :] <= qpos[:, None], s_own, -jnp.inf)
        p = jax.nn.softmax(jnp.concatenate([s_sel, s_own], axis=-1), axis=-1).astype(v.dtype)
        p_sel = p[..., :topk_n * L].reshape(B, H, MOBA_Q_CHUNK, topk_n, L)
        p_own = p[..., topk_n * L:]
        return (jnp.einsum('bhqnl,bhqnld->bqhd', p_sel, v_sel)
                + jnp.einsum('bhql,bhld->bqhd', p_own, v_own))

    o = lax.map(step, (qc, jnp.arange(nc)))
    return o.transpose(1, 0, 2, 3, 4).reshape(B, S, H, d)

def even_mixer(h, w_in, lq1, lk1, lq2, lk2, subln_g, w_out, lam_init, cos, sin):
    B, S, _ = h.shape
    z = h @ w_in
    mq, mk, mv, dq, dk, dv = jnp.split(z, EVEN_SPLITS, axis=-1)
    mq = apply_rope(mq.reshape(B, S, MOBA_HEADS, MOBA_HEAD_DIM), cos, sin)
    mk = apply_rope(mk.reshape(B, S, MOBA_HEADS, MOBA_HEAD_DIM), cos, sin)
    mv = mv.reshape(B, S, MOBA_HEADS, MOBA_HEAD_DIM)
    o_a = moba_attention(mq, mk, mv).reshape(B, S, MOBA_W)

    dq = apply_rope(dq.reshape(B, S, DIFF_HEADS, 2, DIFF_HEAD_DIM), cos, sin)
    dk = apply_rope(dk.reshape(B, S, DIFF_HEADS, 2, DIFF_HEAD_DIM), cos, sin)
    dv = dv.reshape(B, S, DIFF_HEADS, DIFF_V_DIM)
    f32 = jnp.float32
    lam = (jnp.exp(jnp.sum(lq1.astype(f32) * lk1.astype(f32)))
           - jnp.exp(jnp.sum(lq2.astype(f32) * lk2.astype(f32))) + lam_init)
    o_b = diff_attention(dq[..., 0, :], dq[..., 1, :], dk[..., 0, :], dk[..., 1, :], dv, lam)
    o_b = (rms_norm(o_b, subln_g) * (1.0 - lam_init)).reshape(B, S, DIFF_V_W)
    return jnp.concatenate([o_a, o_b], axis=-1) @ w_out

def mla_mixer(h, w_in, q_norm_g, kv_norm_g, w_q_up, w_kv_up, w_out, cos, sin):
    B, S, _ = h.shape
    z = h @ w_in
    cq, ckv, kr = jnp.split(z, (MLA_Q_RANK, MLA_Q_RANK + MLA_KV_RANK), axis=-1)
    q = (rms_norm(cq, q_norm_g) @ w_q_up).reshape(B, S, MLA_HEADS, MLA_NOPE + MLA_ROPE)
    q = jnp.concatenate([q[..., :MLA_NOPE], apply_rope(q[..., MLA_NOPE:], cos, sin)], axis=-1)
    kv = (rms_norm(ckv, kv_norm_g) @ w_kv_up).reshape(B, S, MLA_HEADS, MLA_NOPE + MLA_V)
    k_rope = apply_rope(kr[:, :, None, :], cos, sin)
    k = jnp.concatenate([kv[..., :MLA_NOPE],
                         jnp.broadcast_to(k_rope, (B, S, MLA_HEADS, MLA_ROPE))], axis=-1)
    v = kv[..., MLA_NOPE:]
    o = causal_attention(q, k, v, (MLA_NOPE + MLA_ROPE) ** -0.5)
    return o.reshape(B, S, ODD_MIX) @ w_out

def hier_moe(h, w_group, b_group, w_expert, b_expert, w_gate, w_up, w_down):
    B, S, D = h.shape
    t = h.reshape(-1, D)
    N = t.shape[0]
    gp = jax.nn.softmax((t @ w_group).astype(jnp.float32) + b_group.astype(jnp.float32), axis=-1)
    grp = jnp.argmax(gp, axis=-1)
    pg = jnp.take_along_axis(gp, grp[:, None], axis=1)[:, 0]
    el = ((t @ w_expert).astype(jnp.float32) + b_expert.astype(jnp.float32)).reshape(N, N_GROUPS, EXPERTS_PER_GROUP)
    el_g = jnp.take_along_axis(el, grp[:, None, None], axis=1)[:, 0]
    pv, pi = lax.top_k(jax.nn.softmax(el_g, axis=-1), EXPERT_TOPK)
    w = pg[:, None] * pv / jnp.sum(pv, axis=-1, keepdims=True)
    eid = grp[:, None] * EXPERTS_PER_GROUP + pi
    gates = jnp.zeros((N, N_EXPERTS), jnp.float32).at[jnp.arange(N)[:, None], eid].add(w)

    def expert_step(acc, params):
        wg, wu, wd, ge = params
        hh = jax.nn.silu(t @ wg) * (t @ wu)
        return acc + ge[:, None].astype(t.dtype) * (hh @ wd), None

    out, _ = lax.scan(expert_step, jnp.zeros_like(t), (w_gate, w_up, w_down, gates.T))
    return out.reshape(B, S, D)

def setup_inputs(seed: int = 0) -> dict:
    key = jax.random.key(seed)
    ks = jax.random.split(key, 32)
    D = D_MODEL

    def nrm(k, shape, scale):
        return jax.random.normal(k, shape, jnp.float32) * scale

    return {
        "x": nrm(ks[0], (BATCH, SEQ, D), 1.0),
        "attn_norm": 1.0 + nrm(ks[1], (DEPTH, D), 0.02),
        "ev_w_in": nrm(ks[2], (N_EVEN, D, EVEN_IN), D ** -0.5),
        "ev_lambda_q1": nrm(ks[3], (N_EVEN, DIFF_HEAD_DIM), 0.1),
        "ev_lambda_k1": nrm(ks[4], (N_EVEN, DIFF_HEAD_DIM), 0.1),
        "ev_lambda_q2": nrm(ks[5], (N_EVEN, DIFF_HEAD_DIM), 0.1),
        "ev_lambda_k2": nrm(ks[6], (N_EVEN, DIFF_HEAD_DIM), 0.1),
        "ev_subln": 1.0 + nrm(ks[7], (N_EVEN, DIFF_V_DIM), 0.02),
        "ev_w_out": nrm(ks[8], (N_EVEN, EVEN_MIX, D), EVEN_MIX ** -0.5),
        "od_w_in": nrm(ks[9], (N_ODD, D, ODD_IN), D ** -0.5),
        "od_q_norm": 1.0 + nrm(ks[10], (N_ODD, MLA_Q_RANK), 0.02),
        "od_kv_norm": 1.0 + nrm(ks[11], (N_ODD, MLA_KV_RANK), 0.02),
        "od_w_q_up": nrm(ks[12], (N_ODD, MLA_Q_RANK, MLA_HEADS * (MLA_NOPE + MLA_ROPE)), MLA_Q_RANK ** -0.5),
        "od_w_kv_up": nrm(ks[13], (N_ODD, MLA_KV_RANK, MLA_HEADS * (MLA_NOPE + MLA_V)), MLA_KV_RANK ** -0.5),
        "od_w_out": nrm(ks[14], (N_ODD, ODD_MIX, D), ODD_MIX ** -0.5),
        "ffn_norm": 1.0 + nrm(ks[15], (DEPTH, D), 0.02),
        "moe_w_group": nrm(ks[16], (DEPTH, D, N_GROUPS), D ** -0.5),
        "moe_b_group": nrm(ks[17], (DEPTH, N_GROUPS), 0.01),
        "moe_w_expert": nrm(ks[18], (DEPTH, D, N_EXPERTS), D ** -0.5),
        "moe_b_expert": nrm(ks[19], (DEPTH, N_EXPERTS), 0.01),
        "moe_w_gate": nrm(ks[20], (DEPTH, N_EXPERTS, D, EXPERT_FF), D ** -0.5),
        "moe_w_up": nrm(ks[21], (DEPTH, N_EXPERTS, D, EXPERT_FF), D ** -0.5),
        "moe_w_down": nrm(ks[22], (DEPTH, N_EXPERTS, EXPERT_FF, D), EXPERT_FF ** -0.5),
        "final_norm": 1.0 + nrm(ks[23], (D,), 0.02),
    }

def reference(x, attn_norm, ev_w_in, ev_lambda_q1, ev_lambda_k1, ev_lambda_q2, ev_lambda_k2,
              ev_subln, ev_w_out, od_w_in, od_q_norm, od_kv_norm, od_w_q_up, od_w_kv_up, od_w_out,
              ffn_norm, moe_w_group, moe_b_group, moe_w_expert, moe_b_expert, moe_w_gate,
              moe_w_up, moe_w_down, final_norm):
    S = x.shape[1]
    cos_h, sin_h = rope_tables(S, MOBA_HEAD_DIM)
    cos_r, sin_r = rope_tables(S, MLA_ROPE)
    for layer in range(DEPTH):
        j = layer // 2
        h = rms_norm(x, attn_norm[layer])
        if layer % 2 == 0:
            lam_init = 0.8 - 0.6 * math.exp(-0.3 * layer)
            x = x + even_mixer(h, ev_w_in[j], ev_lambda_q1[j], ev_lambda_k1[j], ev_lambda_q2[j],
                               ev_lambda_k2[j], ev_subln[j], ev_w_out[j], lam_init, cos_h, sin_h)
        else:
            x = x + mla_mixer(h, od_w_in[j], od_q_norm[j], od_kv_norm[j], od_w_q_up[j],
                              od_w_kv_up[j], od_w_out[j], cos_r, sin_r)
        x = x + hier_moe(rms_norm(x, ffn_norm[layer]), moe_w_group[layer], moe_b_group[layer],
                         moe_w_expert[layer], moe_b_expert[layer], moe_w_gate[layer],
                         moe_w_up[layer], moe_w_down[layer])
    return rms_norm(x, final_norm)


_drawn_inputs = setup_inputs


def setup_inputs(seed=0):
    import zlib

    import numpy as np

    out = dict(_drawn_inputs(seed))
    spreads = {}
    factors = {'ev_lambda_q2': 8.0,
     'od_q_norm': 5.362,
     'od_kv_norm': 2.848,
     'moe_b_group': 3.764,
     'moe_b_expert': 3.341,
     'final_norm': 2.904}
    for name, (base, spread) in spreads.items():
        noise = np.random.default_rng([zlib.crc32(name.encode()), seed]).standard_normal(out[name].shape)
        drawn = base * np.exp(spread * noise) if base else spread * noise
        out[name] = __import__('jax').numpy.asarray(drawn.astype(out[name].dtype))
    for name, factor in factors.items():
        out[name] = (out[name] * factor).astype(out[name].dtype)
    return out
```

```python
import math
from contextlib import ExitStack

import concourse.bass as bass
from concourse import mybir

F32 = mybir.dt.float32
I32 = mybir.dt.int32
ALU = mybir.AluOpType
ACT = mybir.ActivationFunctionType
AX = mybir.AxisListType

P = 128
EPS = 1e-6
BIG = 1e30
SLOTS = 32
LANES = 4
IDX_OFF = 64.0


def trunk(nc, x, attn_norm, ev_w_in, ev_lambda_q1, ev_lambda_k1, ev_lambda_q2, ev_lambda_k2, ev_subln, ev_w_out,
          od_w_in, od_q_norm, od_kv_norm, od_w_q_up, od_w_kv_up, od_w_out, ffn_norm, moe_w_group, moe_b_group,
          moe_w_expert, moe_b_expert, moe_w_gate, moe_w_up, moe_w_down, final_norm, rope_tab, out):
    _, S, D = x.shape
    T = S // P
    C = D // P
    LAYERS = attn_norm.shape[0]
    NG = moe_w_group.shape[2]
    NE = moe_w_expert.shape[2]
    EPG = NE // NG
    FF = moe_w_gate.shape[3]
    FC = FF // P
    QUARTS = NE // LANES
    HD = ev_lambda_q1.shape[1]
    HALF = HD // 2
    DV = ev_subln.shape[1]
    DH = ev_w_in.shape[2] // 512
    QR, KR = od_q_norm.shape[1], od_kv_norm.shape[1]
    ODN = od_w_in.shape[2]
    RR = ODN - QR - KR
    NH1 = 16
    QH = od_w_q_up.shape[2] // NH1
    NOPE = QH - RR
    LAM_INIT = 0.8 - 0.6 * math.exp(-0.3 * 0)
    SCALE = [HD ** -0.5, QH ** -0.5]
    assert T == 2 and C == 8 and FC == 2 and DH == 6 and QH == 96 and NE * 8 == S

    ctx = ExitStack()
    with ctx:
        def sb(name, shape, dt=F32):
            return ctx.enter_context(nc.sbuf_tensor(name, shape, dt))

        def sem(name):
            return ctx.enter_context(nc.semaphore(name))

        ps = [ctx.enter_context(nc.psum_tensor(f"ps{i}", [P, 512], F32)) for i in range(8)]

        gu_e = [[None] * LANES for _ in range(2)]
        gu0 = sb("gu_set0", [P, LANES, 2, C, FF])
        gu1a = sb("gu_set1a", [P, 2, 2, C, FF])
        gu1b = sb("gu_set1b", [P, 2, 2, C, FF])
        for e in range(LANES):
            gu_e[0][e] = gu0[:, e]
            gu_e[1][e] = (gu1a if e < 2 else gu1b)[:, e % 2]
        down = sb("down", [P, LANES, FC, D])
        stream_raw = [down[:, 2 * s:2 * s + 2].rearrange("p e c n -> p (e c n)") for s in range(2)]
        qk_raw = gu1b[:].rearrange("p a b c f -> p (a b c f)")
        qT0 = qk_raw[:, 0:8 * S].rearrange("p (b s) -> p b s", b=8)
        kP0 = qk_raw[:, 8 * S:24 * S].rearrange("p (b r s) -> p b r s", b=8, r=2)
        qT1 = qk_raw[:, 0:NH1 * S].rearrange("p (h s) -> p h s", h=NH1)
        kT1 = qk_raw[:, NH1 * S:2 * NH1 * S].rearrange("p (h s) -> p h s", h=NH1)

        xs = sb("xs", [P, T, D])
        hT = sb("hT", [P, C, S])
        oT = hT
        vh = sb("vh", [P, T, D])
        hp = vh
        scr = sb("scr", [P, 3072])
        rot = [scr[:, 512 * i:512 * i + 512] for i in range(2)]
        tmp_cos, tmp_sin = scr[:, 1024:1536], scr[:, 1536:2048]
        prob = [scr[:, 384 * i:384 * i + 384] for i in range(4)]
        probT = [scr[:, 2048 + 384 * i:2432 + 384 * i] for i in range(2)]
        junk = [scr[:, D * t:D * t + D] for t in range(T)]
        on = scr[:, 0:D]
        z1 = scr[:, 2048:2048 + T * ODN].rearrange("p (t n) -> p t n", t=T)
        xgT = scr[:, 0:C * P].rearrange("p (c s) -> p c s", c=C)
        ysb = scr[:, 0:D]
        hid = scr[:, 1024:1280].rearrange("p (c f) -> p c f", c=FC)
        hidT = scr[:, 1280:1536].rearrange("p (c s) -> p c s", c=FC)
        comb = scr[:, 1536:1792]
        pick = scr[:, 1792:2048].rearrange("p (t e s) -> p t e s", t=T, e=LANES)
        sil = scr[:, 1792:2048]
        pickg = scr[:, 2048:2304].rearrange("p (t e s) -> p t e s", t=T, e=LANES)
        kr_in = scr[:, 2880:3072].rearrange("p (t n) -> p t n", t=T)
        lamv = scr[:, 2816:3072].rearrange("p (k n) -> p k n", k=4)

        gain = sb("gain", [P, D])
        lat = gain
        cqT = lat[:, 0:2 * S].rearrange("p (c s) -> p c s", c=2)
        ckvT = lat[:, 2 * S:3 * S]
        krT = lat[:, 3 * S:4 * S]
        mask = sb("mask", [P, 2 * P])
        ident = sb("ident", [P, P])
        tri = sb("tri", [P, P])
        ones = sb("ones", [P, P])
        wr = sb("wr", [P, C, NG + NE])
        br = sb("br", [P, LAYERS, NG + NE])
        gcol = sb("gcol", [P, 2 * LAYERS, C])
        rope = sb("rope", [P, T, 96])
        rope0 = sb("rope0", [P, T, 2, HALF])
        gsub = sb("gsub", [P, 1])
        gq = sb("gq", [P, 2])
        gkv = sb("gkv", [P, 1])
        idx = sb("idx", [P, NE])
        idxn = sb("idxn", [P, NE])
        thr = sb("thr", [1, QUARTS, 7])
        before = sb("before", [1, QUARTS + 1, QUARTS])
        bounds = sb("bounds", [1, LAYERS, QUARTS + 2], I32)
        st = sb("st", [P, 144])
        ss, ms, rstd = st[:, 0:2], st[:, 2:4], st[:, 4:6]
        mx = st[:, 8:16].rearrange("p (u t) -> p u t", t=2)
        nm = st[:, 16:24].rearrange("p (u t) -> p u t", t=2)
        sm = st[:, 24:32].rearrange("p (u t) -> p u t", t=2)
        rs = st[:, 32:40].rearrange("p (u t) -> p u t", t=2)
        nlam = st[:, 40:41]
        lsum = st[:, 42:44]
        lexp = st[:, 44:46]
        sso, mso, rso = st[:, 48:56], st[:, 56:64], st[:, 64:72]
        ss1 = st[:, 72:76].rearrange("p (t k) -> p t k", t=T)
        ms1 = st[:, 76:80].rearrange("p (t k) -> p t k", t=T)
        rs1 = st[:, 80:84].rearrange("p (t k) -> p t k", t=T)
        cmax, rnd = st[0:1, 88:96], st[0:1, 96:104]
        bfl = st[0:1, 104:113]
        gm, gs_, gw = st[:, 116:118], st[:, 118:120], st[:, 120:122]
        m1, m2 = st[:, 122:124], st[:, 124:126]
        ex2, den, w1, w2 = st[:, 126:128], st[:, 128:130], st[:, 130:132], st[:, 132:134]
        sel1 = st[:, 134:136]
        neg_one = st[:, 136:137]
        rt = scr[:, 1024:1024 + 6 * T * NE].rearrange("p (k t e) -> p k t e", k=6, t=T)
        lg, lge, t0, oh1, oh2, routed = (rt[:, k] for k in range(6))
        pos = sb("pos", [P, T, NE])[:, :, :]
        gate = sb("gate", [P, T, NE])[:, :, :]
        lgg = sb("lgg", [P, 3, T, NG])
        cnt_ge = sb("cnt_ge", [1, QUARTS + 1, QUARTS])

        def bc(ap, shape, axis):
            for a in axis:
                ap = ap.unsqueeze(a)
            return ap.to_broadcast(shape)

        x_loaded, smalls_loaded = sem("x_loaded"), sem("smalls_loaded")
        stream_loaded = [sem("stream_loaded0"), sem("stream_loaded1")]
        gu_loaded = [sem("gu_loaded0"), sem("gu_loaded1")]
        down_loaded, gain_loaded, wr_loaded = sem("down_loaded"), sem("gain_loaded"), sem("wr_loaded")
        consts, kzero, ident_made = sem("consts"), sem("kzero"), sem("ident_made")
        pool_step = sem("pool_step")
        chain, achain = sem("dve_chain"), sem("act_chain")
        N5 = range(2 * LAYERS + 1)
        xr = [[sem(f"x_ready{n}_{t}") for t in range(T)] for n in N5]
        xT_ready = [sem(f"xT_ready{n}") for n in N5]
        hT_ready = [sem(f"hT_ready{n}") for n in N5]
        ss_ready = [sem(f"ss_ready{n}") for n in N5]
        rec_ready = [sem(f"rec_ready{n}") for n in N5]
        rstd_ready = [sem(f"rstd_ready{n}") for n in N5]
        z_ready, z_roped, v_ready = sem("z_ready"), sem("z_roped"), sem("v_ready")
        zrT_ready, qk_evac = sem("zrT_ready"), sem("qk_evac")
        L2 = range(LAYERS)
        s_ready = [sem(f"s_ready{i}") for i in L2]
        m_ready = [sem(f"m_ready{i}") for i in L2]
        e_ready = [sem(f"e_ready{i}") for i in L2]
        p_ready = [sem(f"p_ready{i}") for i in L2]
        pT_ready = [sem(f"pT_ready{i}") for i in L2]
        pT_evac = [sem(f"pT_evac{i}") for i in L2]
        pv_done = [sem(f"pv_done{i}") for i in L2]
        oT_evac = [sem(f"oT_evac{i}") for i in L2]
        sso_ready, mso_ready, rso_ready = sem("sso_ready"), sem("mso_ready"), sem("rso_ready")
        on_ready, onT_ready, lam_sum, lam_exp = sem("on_ready"), sem("onT_ready"), sem("lam_sum"), sem("lam_exp")
        wo_half = [sem(f"wo_half{i}") for i in L2]
        wo_ready = [sem(f"wo_ready{i}") for i in L2]
        z1_ready, z1_sb, ss1_ready = sem("z1_ready"), sem("z1_sb"), sem("ss1_ready")
        ms1_ready, rs1_ready, zn_ready = sem("ms1_ready"), sem("rs1_ready"), sem("zn_ready")
        cT_ready, cT_evac, kr_spread = sem("cT_ready"), sem("cT_evac"), sem("kr_spread")
        qmm_ready, kvmm_ready = sem("qmm_ready"), sem("kvmm_ready")
        q_roped, kv_evac, qrT_ready, qT_evac = sem("q_roped"), sem("kv_evac"), sem("qrT_ready"), sem("qT_evac")
        lg_ready = [sem(f"logits_ready{i}") for i in L2]
        gexp = [sem(f"group_exp{i}") for i in L2]
        eexp = [sem(f"expert_exp{i}") for i in L2]
        gmax_ready = [sem(f"group_max{i}") for i in L2]
        emax_ready = [sem(f"expert_max{i}") for i in L2]
        routed_ready = [sem(f"routed{i}") for i in L2]
        pos_ready = [sem(f"pos_ready{i}") for i in L2]
        hp_ready = [sem(f"hp_ready{i}") for i in L2]
        bounds_ready = [sem(f"bounds_ready{i}") for i in L2]
        pick_made = [sem(f"pick_made{i}") for i in L2]
        pick_ready = [sem(f"pick_ready{i}") for i in L2]
        xg_ready = [[sem(f"xg_ready{i}_{h}") for h in range(2)] for i in L2]
        xgT_a = [sem(f"xgT_act{i}") for i in L2]
        xgT_d = [sem(f"xgT_dve{i}") for i in L2]
        cT = [sem(f"comb_transposed{i}") for i in L2]
        comb_sb = [sem(f"comb_sb{i}") for i in L2]
        a_done = [sem(f"gate_up_done{i}") for i in L2]
        silu_done = [sem(f"silu_done{i}") for i in L2]
        hid_ready = [sem(f"hid_ready{i}") for i in L2]
        hidT_ready = [sem(f"hidT_ready{i}") for i in L2]
        hidT_sb = [sem(f"hidT_sb{i}") for i in L2]
        b_done = [sem(f"down_done{i}") for i in L2]
        y_a = [sem(f"y_act{i}") for i in L2]
        y_d = [sem(f"y_dve{i}") for i in L2]
        comb_done = [sem(f"comb_done{i}") for i in L2]
        y_out, stored = sem("y_out"), sem("stored")

        rope_items = [2 * n + t for n in (0, 1, 3, 4) for t in range(T)]
        v_items = [2 * n + t for n in (2, 5) for t in range(T)]
        proj0 = []
        for i in range(2 * DH + 2):
            if i < 2 * DH:
                proj0.append(("z", i))
            if i - 2 in rope_items:
                proj0.append(("T", rope_items.index(i - 2)))
        proj1, kv_list = [], []
        rest = [("v", j) for j in range(4)] + [("k", j) for j in range(8)]
        for r in range(8 + 2):
            if r < 8:
                proj1.append(("q", r))
            if r >= 2:
                proj1.append(("T", r - 2))
                proj1 += rest[:2] if r > 2 else rest[:1]
                rest = rest[2:] if r > 2 else rest[1:]
        proj1 += rest
        mm1 = [it for it in proj1 if it[0] != "T"]
        kv_list = [it for it in mm1 if it[0] != "q"]
        NSTEP = 16

        def unit(layer, s):
            if not 0 <= s < NSTEP:
                return None
            if layer == 1 or s < 8:
                return s
            return 8 + (s - 9) // 2 if s % 2 else None

        def diff(layer, s):
            return layer == 0 and s >= 8

        WO_BANK = [[0, 1, 6, 7], [2, 3, 6, 7]]

        x_dram = x[0].rearrange("(t p) d -> p t d", p=P)
        out_dram = out[0].rearrange("(t p) d -> p t d", p=P)
        gate_dram = moe_w_gate.rearrange("l e (p c) f -> l e p (c f)", c=C)
        up_dram = moe_w_up.rearrange("l e (p c) f -> l e p (c f)", c=C)
        down_dram = moe_w_down.rearrange("l e (p c) n -> l e p (c n)", c=FC)

        def load_router(eng, l):
            eng.dma_start(wr[:, :, 0:NG], moe_w_group[l].rearrange("(p c) g -> p c g", c=C)).then_inc(wr_loaded, 16)
            eng.dma_start(wr[:, :, NG:], moe_w_expert[l].rearrange("(p c) g -> p c g", c=C)).then_inc(wr_loaded, 16)

        block = ctx.enter_context(nc.Block())

        @block.sync
        def _(sp):
            def load_stream(slot, dst, src):
                sp.dma_start(dst, src).then_inc(stream_loaded[slot], 16)

            def load_gu(l, st_, e, expert):
                sp.dma_start(gu_e[st_][e][:, 0].rearrange("p c f -> p (c f)"), gate_dram[l, expert]
                             ).then_inc(gu_loaded[st_], 16)
                sp.dma_start(gu_e[st_][e][:, 1].rearrange("p c f -> p (c f)"), up_dram[l, expert]
                             ).then_inc(gu_loaded[st_], 16)

            def load_down(l, q):
                for e in range(LANES):
                    sp.dma_start(down[:, e].rearrange("p c n -> p (c n)"), down_dram[l, q * LANES + e]
                                 ).then_inc(down_loaded, 16)

            w_in = ev_w_in[0].rearrange("(p c) n -> p c n", c=C)
            w_in_sb = [s.rearrange("p (c n) -> p c n", c=C) for s in stream_raw]
            w_out_sb = [s.rearrange("p (c n) -> p c n", c=C // 2) for s in stream_raw]

            def load_w_out(w, half, slot):
                v = w[0].rearrange("(c p) n -> p c n", p=P)
                load_stream(slot, w_out_sb[slot], v[:, 4 * half:4 * half + 4, :])

            for t in range(T):
                sp.dma_start(xs[:, t, :], x_dram[:, t, :]).then_inc(x_loaded, 16)
            for n in range(DH):
                if n >= 2:
                    sp.wait_ge(z_ready, 2 * (n - 1))
                load_stream(n % 2, w_in_sb[n % 2], w_in[:, :, 512 * n:512 * n + 512])
                if n >= 1:
                    if n <= 4:
                        load_gu(0, 0, n - 1, n - 1)
            sp.wait_ge(z_ready, 2 * 5)
            load_w_out(ev_w_out, 0, 0)
            load_gu(0, 1, 0, LANES)
            sp.wait_ge(z_ready, 2 * 6)
            load_w_out(ev_w_out, 1, 1)
            load_gu(0, 1, 1, LANES + 1)

            def experts(l):
                sp.wait_ge(s_ready[l], NSTEP)
                load_gu(l, 1, 2, LANES + 2)
                load_gu(l, 1, 3, LANES + 3)
                sp.wait_ge(wo_ready[l], 4)
                load_down(l, 0)
                sp.wait_ge(bounds_ready[l], 1)
                with sp.Fori(0, QUARTS // 2 - 1) as i:
                    for half in range(2):
                        q = 2 * i + 2 + half
                        jobs = sp.value_load(bounds[0:1, l, bass.ds(q - 1, 1)], min_val=1, max_val=8 * QUARTS)
                        sp.wait_ge(a_done[l], jobs)
                        for e in range(LANES):
                            load_gu(l, half, e, q * LANES + e)
                        sp.wait_ge(b_done[l], jobs)
                        load_down(l, q - 1)
                q = QUARTS - 1
                jobs = sp.value_load(bounds[0:1, l, q:q + 1], min_val=1, max_val=8 * QUARTS)
                sp.wait_ge(b_done[l], jobs)
                load_down(l, q)

            experts(0)
            jobs = sp.value_load(bounds[0:1, 0, QUARTS - 1:QUARTS], min_val=1, max_val=8 * QUARTS)
            sp.wait_ge(a_done[0], jobs)
            load_gu(1, 0, 0, 0)
            jobs = sp.value_load(bounds[0:1, 0, QUARTS:QUARTS + 1], min_val=1, max_val=8 * QUARTS)
            sp.wait_ge(b_done[0], jobs)
            load_stream(0, stream_raw[0][:, 0:C * ODN].rearrange("p (c n) -> p c n", c=C),
                        od_w_in[0].rearrange("(p c) n -> p c n", c=C))
            load_stream(1, stream_raw[1][:, 0:2 * QH * NH1].rearrange("p (c n) -> p c n", c=2),
                        od_w_q_up[0].rearrange("(c p) n -> p c n", p=P))
            load_gu(1, 0, 1, 1)
            sp.wait_ge(z1_ready, 2)
            load_stream(0, stream_raw[0][:, 0:2 * P * NH1 // 2], od_w_kv_up[0])
            load_gu(1, 0, 2, 2)
            load_gu(1, 0, 3, 3)
            sp.wait_ge(qmm_ready, 8)
            load_w_out(od_w_out, 0, 1)
            sp.wait_ge(kvmm_ready, len(kv_list))
            load_w_out(od_w_out, 1, 0)
            load_gu(1, 1, 0, LANES)
            load_gu(1, 1, 1, LANES + 1)
            load_router(sp, 1)
            sp.wait_ge(kr_spread, 1)
            sp.dma_start(gain[:, :], ffn_norm[1].partition_broadcast(P)).then_inc(gain_loaded, 16)
            experts(1)
            sp.dma_start(gain[:, :], final_norm.partition_broadcast(P)).then_inc(gain_loaded, 16)
            for t in range(T):
                sp.wait_ge(y_out, t + 1)
                sp.dma_start(out_dram[:, t, :], xs[:, t, :]).then_inc(stored, 16)
            sp.wait_ge(stored, 16 * T)

        @block.gpsimd
        def _(pool):
            g = nc.gpsimd
            steps = [0]

            def then(ins):
                steps[0] += 1
                ins.then_inc(pool_step, 1)
                pool.wait_ge(pool_step, steps[0])

            then(g.memset(ident[:, :], 0.0))
            then(g.affine_select(out=ident[:, :], in_=ident[:, :], compare_op=ALU.not_equal, fill=1.0, base=0,
                                 pattern=[[-1, P]], channel_multiplier=1))
            g.nop().then_inc(ident_made, 1)
            then(g.memset(kP0[64:128, :, 0, :], 0.0))
            then(g.memset(kP0[0:64, :, 1, :], 0.0))
            g.nop().then_inc(kzero, 1)
            then(g.memset(mask[:, :], 0.0))
            then(g.affine_select(out=mask[:, P:2 * P], in_=mask[:, P:2 * P], compare_op=ALU.is_ge,
                                 fill=-BIG, base=0, pattern=[[-1, P]], channel_multiplier=1))
            then(g.memset(tri[:, :], 1.0))
            then(g.affine_select(out=tri[:, :], in_=tri[:, :], compare_op=ALU.is_gt, fill=0.0, base=0,
                                 pattern=[[1, P]], channel_multiplier=-1))
            then(g.memset(ones[:, :], 1.0))
            then(g.memset(before[:, :, :], 1.0))
            then(g.affine_select(out=before[:, :, :], in_=before[:, :, :], compare_op=ALU.is_gt, fill=0.0, base=0,
                                 pattern=[[1, QUARTS + 1], [-1, QUARTS]], channel_multiplier=0))
            then(g.iota(idx[:, :], pattern=[[1, NE]], base=0, channel_multiplier=0,
                        allow_small_or_imprecise_dtypes=True))
            then(g.iota(idxn[:, :], pattern=[[1, NE]], base=-int(IDX_OFF), channel_multiplier=0,
                        allow_small_or_imprecise_dtypes=True))
            then(g.iota(thr[:, :, :], pattern=[[0, QUARTS], [SLOTS, 7]], base=SLOTS, channel_multiplier=0,
                        allow_small_or_imprecise_dtypes=True))
            g.nop().then_inc(consts, 1)
            pool.wait_ge(cT_evac, 1)
            g.tensor_copy(kT1[NOPE:QH, :, :], bc(krT[NOPE:QH, :], [RR, NH1, S], [1])).then_inc(kr_spread, 1)

        @block.tensor
        def _(pe):
            mm, tr = nc.tensor.matmul, nc.tensor.transpose

            def transpose_x(n):
                for t in range(T):
                    if n == 0:
                        pe.wait_ge(x_loaded, 32)
                        pe.wait_ge(ident_made, 1)
                    else:
                        pe.wait_ge(xr[n][t], 2)
                    v = xs[:, t, :].rearrange("s (p c) -> s c p", c=C)
                    for h in range(2):
                        for j in range(4):
                            i = tr(ps[2 * t + h][:, P * j:P * j + P], v[:, 4 * h + j, :], ident[:, :])
                        i.then_inc(xT_ready[n], 1)

            def project0():
                w = [s.rearrange("p (c n) -> p c n", c=C) for s in stream_raw]
                for what, i in proj0:
                    if what == "z":
                        n, t = divmod(i, T)
                        if t == 0:
                            pe.wait_ge(stream_loaded[n % 2], 16 * (n // 2 + 1))
                        if n == 0:
                            pe.wait_ge(hT_ready[0], 2 * t + 2)
                        if i >= 4 and i - 4 in rope_items:
                            pe.wait_ge(z_roped, rope_items.index(i - 4) + 1)
                        elif i >= 4:
                            pe.wait_ge(v_ready, v_items.index(i - 4) + 1)
                        for c in range(C):
                            m = mm(ps[4 + i % 4][:, :], hT[:, c, P * t:P * t + P], w[n % 2][:, c, :],
                                   start=(c == 0), stop=(c == C - 1))
                        m.then_inc(z_ready, 1)
                    else:
                        pe.wait_ge(z_roped, i + 1)
                        if i >= 2:
                            pe.wait_ge(qk_evac, i - 1)
                        else:
                            pe.wait_ge(hT_ready[0], 4)
                        for j in range(4):
                            m = tr(ps[i % 2][:, P * j:P * j + P], rot[i % 2][:, P * j:P * j + P], ident[:, :])
                        m.then_inc(zrT_ready, 1)

            def attention(l):
                for s in range(NSTEP + 3):
                    if s < NSTEP:
                        if s == 0 and l == 0:
                            pe.wait_ge(v_ready, 4)
                            pe.wait_ge(z_roped, 8)
                            pe.wait_ge(qk_evac, 8)
                        if s == 0 and l == 1:
                            pe.wait_ge(kv_evac, len(kv_list))
                            pe.wait_ge(qT_evac, 8)
                            pe.wait_ge(kr_spread, 1)
                        if s >= 2:
                            pe.wait_ge(m_ready[l], s - 1)
                        if l == 0:
                            q, k, K = qT0[:, s // 2, :], kP0[:, s // 2, s % 2, :], P
                        else:
                            q, k, K = qT1[:, s, :], kT1[:, s, :], QH
                        mm(ps[4 + s % 2][:, 0:P], q[0:K, 0:P], k[0:K, 0:P], start=True, stop=True)
                        mm(ps[4 + s % 2][:, P:3 * P], q[0:K, P:S], k[0:K, 0:S], start=True, stop=True
                           ).then_inc(s_ready[l], 1)
                    u = unit(l, s - 2)
                    if u is not None:
                        pe.wait_ge(p_ready[l], u + 1)
                        if u >= 2:
                            pe.wait_ge(pT_evac[l], u - 1)
                        src = prob[(s - 2 - diff(l, s - 2)) % 4]
                        for j in range(3):
                            m = tr(ps[6 + u % 2][:, P * j:P * j + P], src[:, P * j:P * j + P], ident[:, :])
                        m.then_inc(pT_ready[l], 1)
                    u = unit(l, s - 3)
                    if u is not None:
                        pe.wait_ge(pT_evac[l], u + 1)
                        pT = probT[u % 2]
                        if diff(l, s - 3):
                            h = u - 8
                            o, a = ps[2 + h // 2], 256 * (h % 2)
                            v = vh[:, :, 512 + P * h:512 + P * h + P]
                            mm(o[:, a:a + P], pT[:, 0:P], v[:, 0, :], start=True, stop=True)
                            mm(o[:, a + P:a + 2 * P], pT[:, P:2 * P], v[:, 0, :], start=True, stop=False)
                            mm(o[:, a + P:a + 2 * P], pT[:, 2 * P:3 * P], v[:, 1, :], start=False, stop=True
                               ).then_inc(pv_done[l], 1)
                        else:
                            pair, r = divmod(u, 2)
                            if pair >= 2:
                                pe.wait_ge(oT_evac[l], pair - 1)
                            o = ps[pair % 2][64 * r:64 * r + 64, :]
                            v = vh[:, :, 64 * u:64 * u + 64]
                            mm(o[:, 0:S], v[:, 0, :], pT[:, 0:S], start=True, stop=False)
                            mm(o[:, P:S], v[:, 1, :], pT[:, 2 * P:3 * P], start=False, stop=True
                               ).then_inc(pv_done[l], 1)

            def project_out(l, half, slot, loads):
                w = stream_raw[slot].rearrange("p (c n) -> p c n", c=4)
                pe.wait_ge(stream_loaded[slot], 16 * loads)
                pe.wait_ge(oT_evac[l], 4 if half == 0 else (6 if l == 0 else 8))
                if half == 0:
                    pe.wait_ge(pT_evac[l], 12 if l == 0 else 16)
                for t in range(T):
                    for n in range(2):
                        for c in range(4):
                            m = mm(ps[WO_BANK[l][2 * t + n]][:, :], oT[:, 4 * half + c, P * t:P * t + P],
                                   w[:, c, 512 * n:512 * n + 512], start=(half == 0 and c == 0),
                                   stop=(half == 1 and c == 3), skip_group_check=True)
                        m.then_inc((wo_half if half == 0 else wo_ready)[l], 1)

            def project1():
                pe.wait_ge(stream_loaded[0], 16 * 5)
                w = stream_raw[0][:, 0:C * ODN].rearrange("p (c n) -> p c n", c=C)
                for t in range(T):
                    pe.wait_ge(hT_ready[2], 2 * t + 2)
                    for c in range(C):
                        m = mm(ps[4 + t][:, 0:ODN], hT[:, c, P * t:P * t + P], w[:, c, :],
                               start=(c == 0), stop=(c == C - 1))
                    m.then_inc(z1_ready, 1)
                pe.wait_ge(zn_ready, 1)
                for t in range(T):
                    for c in range(2):
                        tr(ps[6][:, S * c + P * t:S * c + P * t + P], z1[:, t, P * c:P * c + P], ident[:, :])
                    tr(ps[7][:, P * t:P * t + P], z1[:, t, QR:QR + KR], ident[:, :])
                    m = tr(ps[7][0:QH, S + P * t:S + P * t + P], kr_in[:, t, :], ident[:, :])
                m.then_inc(cT_ready, 1)
                pe.wait_ge(cT_evac, 2)
                wq = stream_raw[1][:, 0:2 * QH * NH1].rearrange("p (c n) -> p c n", c=2)
                wkv = stream_raw[0][:, 0:P * NH1].rearrange("p (h k d) -> p h k d", h=NH1, k=2)
                done = {"q": 0, "kv": 0}
                for what, i in proj1:
                    if what == "T":
                        pe.wait_ge(q_roped, i + 1)
                        if i >= 2:
                            pe.wait_ge(qT_evac, i - 1)
                        for j in range(4):
                            m = tr(ps[4 + i % 2][0:QH, P * j:P * j + P], rot[i % 2][:, QH * j:QH * j + QH],
                                   ident[:, :])
                        m.then_inc(qrT_ready, 1)
                        continue
                    j = mm1.index((what, i))
                    if j >= 4:
                        w4, i4 = mm1[j - 4]
                        if w4 == "q":
                            pe.wait_ge(q_roped, i4 + 1)
                        else:
                            pe.wait_ge(kv_evac, kv_list.index((w4, i4)) + 1)
                    b = ps[j % 4]
                    if what == "q":
                        if i == 0:
                            pe.wait_ge(stream_loaded[1], 16 * 5)
                        g, t = divmod(i, T)
                        for c in range(2):
                            m = mm(b[:, 0:4 * QH], cqT[:, c, P * t:P * t + P], wq[:, c, 4 * QH * g:4 * QH * g + 4 * QH],
                                   start=(c == 0), stop=(c == 1))
                        m.then_inc(qmm_ready, 1)
                    elif what == "v":
                        if i == 0:
                            pe.wait_ge(stream_loaded[0], 16 * 6)
                        n, t = divmod(i, T)
                        mm(b[:, :], ckvT[:, P * t:P * t + P], wkv[:, 8 * n:8 * n + 8, 1, :], start=True, stop=True
                           ).then_inc(kvmm_ready, 1)
                    else:
                        for r in range(2):
                            m = mm(b[0:NOPE, S * r:S * r + S], wkv[:, 2 * i + r, 0, :], ckvT, start=True, stop=True)
                        m.then_inc(kvmm_ready, 1)

            def route(l):
                pe.wait_ge(wr_loaded, 32 * (l + 1))
                for t in range(T):
                    pe.wait_ge(hT_ready[2 * l + 1], 2 * t + 2)
                    for c in range(C):
                        m = mm(ps[4][:, 64 * t:64 * t + NG + NE], hT[:, c, P * t:P * t + P], wr[:, c, :],
                               start=(c == 0), stop=(c == C - 1))
                    m.then_inc(lg_ready[l], 1)
                for t in range(T):
                    for n in range(2):
                        mm(ps[2 * t + n][:, :], ident[:, :], xs[:, t, 512 * n:512 * n + 512], start=True, stop=False,
                           skip_group_check=True)
                pe.wait_ge(routed_ready[l], 1)
                mm(ps[5][:, 0:NE], tri[:, :], routed[:, 0, :], start=True, stop=True)
                mm(ps[5][:, NE:2 * NE], ones[:, :], routed[:, 0, :], start=True, stop=False)
                mm(ps[5][:, NE:2 * NE], tri[:, :], routed[:, 1, :], start=False, stop=True)
                mm(ps[5][:, 2 * NE:3 * NE], ones[:, :], routed[:, 0, :], start=True, stop=False)
                mm(ps[5][:, 2 * NE:3 * NE], ones[:, :], routed[:, 1, :], start=False, stop=True
                   ).then_inc(pos_ready[l], 1)

            def experts(l):
                pe.wait_ge(bounds_ready[l], 1)
                pe.wait_ge(hp_ready[l], 2)
                with pe.Fori(0, QUARTS // 2) as i:
                    for half in range(2):
                        q = 2 * i + half
                        first = pe.value_load(bounds[0:1, l, bass.ds(q, 1)], min_val=0, max_val=8 * QUARTS)
                        end = pe.value_load(bounds[0:1, l, bass.ds(q + 1, 1)], min_val=1, max_val=8 * QUARTS)
                        with pe.Fori(first, end) as job:
                            pe.wait_ge(pick_ready[l], job + 1)
                            for c in range(C):
                                for t in range(T):
                                    m = mm(ps[4 + c // 4][:, P * (c % 4):P * (c % 4) + P], hp[:, t, P * c:P * c + P],
                                           pick[:, t].rearrange("p e s -> p (e s)"), start=(t == 0), stop=(t == 1))
                                if c % 4 == 3:
                                    m.then_inc(xg_ready[l][c // 4], 1)
                            for t in range(T):
                                m = tr(ps[7][:, 256 + P * t:256 + P * t + P], pickg[:, t].rearrange("p e s -> p (e s)"),
                                       ident[:, :])
                            m.then_inc(cT[l], 1)
                            pe.wait_ge(gu_loaded[half], 16 * 2 * LANES * (QUARTS // 2 * l + 1) + i * (16 * 2 * LANES))
                            pe.wait_ge(xgT_a[l], job + 1)
                            for c in range(C):
                                if c == 4:
                                    pe.wait_ge(xgT_d[l], job + 1)
                                for e in range(LANES):
                                    m = mm(ps[6][SLOTS * e:SLOTS * e + SLOTS, :], xgT[:, c, SLOTS * e:SLOTS * e + SLOTS],
                                           gu_e[half][e][:, :, c, :], start=(c == 0), stop=(c == C - 1))
                            m.then_inc(a_done[l], 1)
                            pe.wait_ge(hid_ready[l], job + 1)
                            for c in range(FC):
                                m = tr(ps[7][:, P * c:P * c + P], hid[:, c, :], ident[:, :])
                            m.then_inc(hidT_ready[l], 1)
                            pe.wait_ge(down_loaded, 16 * LANES * (QUARTS * l + 1 + half) + i * (16 * 2 * LANES))
                            pe.wait_ge(hidT_sb[l], job + 1)
                            for n in range(2):
                                for c in range(FC):
                                    for e in range(LANES):
                                        m = mm(ps[4 + n][SLOTS * e:SLOTS * e + SLOTS, :],
                                               hidT[:, c, SLOTS * e:SLOTS * e + SLOTS],
                                               down[:, e, c, 512 * n:512 * n + 512], start=(c == 0),
                                               stop=(c == FC - 1))
                            m.then_inc(b_done[l], 1)
                            pe.wait_ge(comb_sb[l], job + 1)
                            for n in range(2):
                                pe.wait_ge((y_a, y_d)[n][l], job + 1)
                                for t in range(T):
                                    m = mm(ps[2 * t + n][:, :], comb[:, P * t:P * t + P],
                                           ysb[:, 512 * n:512 * n + 512], start=False, stop=False,
                                           skip_group_check=True)
                            m.then_inc(comb_done[l], 1)

            transpose_x(0)
            project0()
            attention(0)
            project_out(0, 0, 0, 4)
            pe.wait_ge(on_ready, 2)
            for b in range(2):
                for j in range(4):
                    m = tr(ps[4 + b][:, P * j:P * j + P], on[:, 512 * b + P * j:512 * b + P * j + P], ident[:, :])
                m.then_inc(onT_ready, 1)
            project_out(0, 1, 1, 4)
            transpose_x(1)
            route(0)
            experts(0)
            transpose_x(2)
            project1()
            attention(1)
            project_out(1, 0, 1, 6)
            project_out(1, 1, 0, 7)
            transpose_x(3)
            route(1)
            experts(1)

        @block.scalar
        def _(act):
            A = nc.scalar.activation

            def square_sums(n):
                for t in range(T):
                    if n == 0:
                        act.wait_ge(x_loaded, 32)
                    else:
                        act.wait_ge(xr[n][t], 2)
                        act.wait_ge(xr[n][1], 2)
                    A(junk[t], xs[:, t, :], ACT.Square, accum_out=ss[:, t:t + 1]).then_inc(ss_ready[n], 1)

            def root(n):
                act.wait_ge(rec_ready[n], 1)
                A(rstd, ms, ACT.Sqrt).then_inc(rstd_ready[n], 1)

            def project0():
                for what, i in proj0:
                    if what == "z" and i in v_items:
                        n, t = divmod(i, T)
                        act.wait_ge(z_ready, i + 1)
                        A(vh[:, t, 512 * (n // 5):512 * (n // 5) + 512], ps[4 + i % 4][:, :], ACT.Identity,
                          scale=rstd[:, t:t + 1]).then_inc(v_ready, 1)
                    elif what == "T":
                        n, t = divmod(rope_items[i], T)
                        act.wait_ge(zrT_ready, i + 1)
                        b0 = 4 * (n // 3)
                        src = ps[i % 2][:, :].rearrange("p (b s) -> p b s", b=4)
                        if n % 3 == 0:
                            nc.scalar.copy(qT0[:, b0:b0 + 4, P * t:P * t + P], src).then_inc(qk_evac, 1)
                        else:
                            act.wait_ge(kzero, 1)
                            nc.scalar.copy(kP0[0:64, b0:b0 + 4, 0, P * t:P * t + P], src[0:64])
                            nc.scalar.copy(kP0[64:128, b0:b0 + 4, 1, P * t:P * t + P], src[64:128]
                                           ).then_inc(qk_evac, 1)

            def attention(l):
                for s in range(NSTEP + 4):
                    if s < NSTEP:
                        act.wait_ge(m_ready[l], s + 1)
                        k = s % 4
                        A(prob[k][:, 0:P], prob[k][:, 0:P], ACT.Exp, bias=nm[:, k, 0:1], scale=SCALE[l],
                          accum_out=sm[:, k, 0:1])
                        A(prob[k][:, P:3 * P], prob[k][:, P:3 * P], ACT.Exp, bias=nm[:, k, 1:2], scale=SCALE[l],
                          accum_out=sm[:, k, 1:2]).then_inc(e_ready[l], 1)
                    u = unit(l, s - 2)
                    if u is not None:
                        act.wait_ge(pT_ready[l], u + 1)
                        if u >= 2:
                            act.wait_ge(pv_done[l], u - 1)
                        nc.scalar.copy(probT[u % 2], ps[6 + u % 2][:, 0:3 * P]).then_inc(pT_evac[l], 1)
                    u = unit(l, s - 4)
                    if u is not None and diff(l, s - 4):
                        if u % 2:
                            b = (u - 8) // 2
                            act.wait_ge(pv_done[l], u + 1)
                            if b:
                                act.wait_ge(sso_ready, b)
                            for j in range(4):
                                m = A(tmp_sin[:, P * j:P * j + P], ps[2 + b][:, P * j:P * j + P], ACT.Square,
                                      accum_out=sso[:, 4 * b + j:4 * b + j + 1])
                            m.then_inc(sso_ready, 1)
                    elif u is not None and u % 2:
                        act.wait_ge(pv_done[l], u + 1)
                        nc.scalar.copy(oT[:, u // 2, :], ps[u // 2 % 2][:, 0:S]).then_inc(oT_evac[l], 1)

            def project1():
                act.wait_ge(rstd_ready[2], 1)
                for t in range(T):
                    act.wait_ge(z1_ready, t + 1)
                    A(z1[:, t, :], ps[4 + t][:, 0:ODN], ACT.Identity, scale=rstd[:, t:t + 1]).then_inc(z1_sb, 1)
                    act.wait_ge(z1_sb, t + 1)
                    j1 = (tmp_cos, tmp_sin)[t]
                    A(j1[:, 0:QR], z1[:, t, 0:QR], ACT.Square, accum_out=ss1[:, t, 0:1])
                    A(j1[:, QR:QR + KR], z1[:, t, QR:QR + KR], ACT.Square, accum_out=ss1[:, t, 1:2]
                      ).then_inc(ss1_ready, 1)
                act.wait_ge(ms1_ready, 1)
                A(rs1, ms1, ACT.Sqrt).then_inc(rs1_ready, 1)
                act.wait_ge(cT_ready, 1)
                nc.scalar.copy(krT[NOPE:QH, :], ps[7][NOPE:QH, S:2 * S]).then_inc(cT_evac, 1)
                for c in range(2):
                    A(cqT[:, c, :], ps[6][:, S * c:S * c + S], ACT.Identity, scale=gq[:, c:c + 1])
                A(ckvT, ps[7][:, 0:S], ACT.Identity, scale=gkv[:, 0:1]).then_inc(cT_evac, 1)
                for what, i in proj1:
                    if what == "T":
                        g, t = divmod(i, T)
                        act.wait_ge(qrT_ready, i + 1)
                        nc.scalar.copy(qT1[0:QH, 4 * g:4 * g + 4, P * t:P * t + P],
                                       ps[4 + i % 2][0:QH, :].rearrange("p (b s) -> p b s", b=4)
                                       ).then_inc(qT_evac, 1)
                    elif what != "q":
                        b = ps[mm1.index((what, i)) % 4]
                        act.wait_ge(kvmm_ready, kv_list.index((what, i)) + 1)
                        if what == "v":
                            n, t = divmod(i, T)
                            nc.scalar.copy(vh[:, t, 512 * n:512 * n + 512], b[:, :]).then_inc(kv_evac, 1)
                        else:
                            nc.scalar.copy(kT1[0:NOPE, 2 * i:2 * i + 2, :].rearrange("p h s -> p (h s)"),
                                           b[0:NOPE, :]).then_inc(kv_evac, 1)

            def route(l):
                act.wait_ge(gmax_ready[l], 1)
                A(lgg[:, 1], lgg[:, 1], ACT.Exp).then_inc(gexp[l], 1)
                act.wait_ge(emax_ready[l], 1)
                A(ex2, ex2, ACT.Exp).then_inc(eexp[l], 1)

            def experts(l):
                act.wait_ge(bounds_ready[l], 1)
                with act.Fori(0, QUARTS // 2) as i:
                    for half in range(2):
                        q = 2 * i + half
                        first = act.value_load(bounds[0:1, l, bass.ds(q, 1)], min_val=0, max_val=8 * QUARTS)
                        end = act.value_load(bounds[0:1, l, bass.ds(q + 1, 1)], min_val=1, max_val=8 * QUARTS)
                        with act.Fori(first, end) as job:
                            act.wait_ge(xg_ready[l][0], job + 1)
                            nc.scalar.copy(xgT[:, 0:4, :].rearrange("p c s -> p (c s)"), ps[4][:, :]
                                           ).then_inc(xgT_a[l], 1)
                            act.wait_ge(a_done[l], job + 1)
                            A(sil, ps[6][:, 0:FF], ACT.Silu).then_inc(silu_done[l], 1)
                            act.wait_ge(hidT_ready[l], job + 1)
                            nc.scalar.copy(hidT[:, :, :].rearrange("p c s -> p (c s)"), ps[7][:, 0:256]
                                           ).then_inc(hidT_sb[l], 1)
                            act.wait_ge(b_done[l], job + 1)
                            nc.scalar.copy(ysb[:, 0:512], ps[4][:, :]).then_inc(y_a[l], 1)
                jobs = act.value_load(bounds[0:1, l, QUARTS:QUARTS + 1], min_val=1, max_val=8 * QUARTS)
                act.wait_ge(comb_done[l], jobs)
                for n in range(2):
                    nc.scalar.copy(xs[:, 0, 512 * n:512 * n + 512], ps[n][:, :]).then_inc(xr[2 * l + 2][0], 1)

            def small(dst, src, **kw):
                act.dma_start(dst, src, **kw).then_inc(smalls_loaded, 16)

            small(gcol[:, 0::2, :], attn_norm.rearrange("l (p c) -> p l c", c=C))
            small(gcol[:, 1::2, :], ffn_norm.rearrange("l (p c) -> p l c", c=C))
            small(rope[:, :, :], rope_tab.rearrange("(t p) f -> p t f", p=P))
            for k, v in enumerate((ev_lambda_q1, ev_lambda_k1, ev_lambda_q2, ev_lambda_k2)):
                small(lamv[:, k, :], v[0].partition_broadcast(P))
            small(gsub[:, :], ev_subln.rearrange("a p -> p a"), allow_slow_non_contiguous=True)
            small(gq[:, :], od_q_norm[0].rearrange("(c p) -> p c", p=P), allow_slow_non_contiguous=True)
            small(gkv[:, :], od_kv_norm.rearrange("a p -> p a"), allow_slow_non_contiguous=True)
            load_router(act, 0)
            for l in L2:
                small(br[:, l, 0:NG], moe_b_group[l].partition_broadcast(P))
                small(br[:, l, NG:], moe_b_expert[l].partition_broadcast(P))
            act.dma_start(gain[:, :], ffn_norm[0].partition_broadcast(P)).then_inc(gain_loaded, 16)

            square_sums(0)
            root(0)
            act.wait_ge(lam_sum, 1)
            A(lexp, lsum, ACT.Exp).then_inc(lam_exp, 1)
            project0()
            attention(0)
            act.wait_ge(mso_ready, 1)
            A(rso, mso, ACT.Sqrt).then_inc(rso_ready, 1)
            for b in range(2):
                act.wait_ge(onT_ready, b + 1)
                A(oT[:, 4 + 2 * b:6 + 2 * b, :].rearrange("p h s -> p (h s)"), ps[4 + b][:, :], ACT.Identity,
                  scale=gsub[:, 0:1]).then_inc(oT_evac[0], 1)
            square_sums(1)
            root(1)
            route(0)
            experts(0)
            square_sums(2)
            root(2)
            project1()
            attention(1)
            square_sums(3)
            root(3)
            route(1)
            experts(1)
            square_sums(4)
            root(4)

        @block.vector
        def _(dve):
            V = nc.vector
            links = [0]

            def link(ins):
                links[0] += 1
                ins.then_inc(chain, 1)
                dve.wait_ge(chain, links[0])

            def norm(n):
                if n == 0:
                    dve.wait_ge(smalls_loaded, 16 * 14)
                if n < 2 * LAYERS:
                    for t in range(T):
                        for h in range(2):
                            dve.wait_ge(xT_ready[n], 2 * t + h + 1)
                            V.tensor_tensor(hT[:, 4 * h:4 * h + 4, P * t:P * t + P],
                                            ps[2 * t + h][:, :].rearrange("p (c s) -> p c s", c=4),
                                            bc(gcol[:, n, 4 * h:4 * h + 4], [P, 4, P], [2]), ALU.mult
                                            ).then_inc(hT_ready[n], 1)
                dve.wait_ge(ss_ready[n], 2)
                link(V.tensor_scalar(ms, ss, 1.0 / D, EPS, ALU.mult, ALU.add))
                V.reciprocal(ms, ms).then_inc(rec_ready[n], 1)

            def rotate(dst, src, cos, sin, width, h):
                a = tmp_cos[:, 0:width].rearrange("p (n k h) -> p n k h", k=2, h=h)
                b = tmp_sin[:, 0:width].rearrange("p (n k h) -> p n k h", k=2, h=h)
                V.tensor_tensor(a, src, cos, ALU.mult)
                link(V.tensor_tensor(b, src, sin, ALU.mult))
                V.tensor_tensor(dst[:, :, 0, :], a[:, :, 0, :], b[:, :, 1, :], ALU.subtract)
                return V.tensor_tensor(dst[:, :, 1, :], a[:, :, 1, :], b[:, :, 0, :], ALU.add)

            def project0():
                dve.wait_ge(rstd_ready[0], 1)
                for t in range(T):
                    i = V.tensor_scalar(rope0[:, t, :, :].rearrange("p k h -> p (k h)"), rope[:, t, 0:2 * HALF],
                                        rstd[:, t:t + 1], None, ALU.mult)
                link(i)
                for r, i in enumerate(rope_items):
                    t = i % T
                    dve.wait_ge(z_ready, i + 1)
                    if r >= 2:
                        dve.wait_ge(zrT_ready, r - 1)
                    if r >= 1:
                        dve.wait_ge(z_roped, r)
                    src = ps[4 + i % 4][:, :].rearrange("p (m h) -> p m h", h=HALF)
                    a = tmp_cos.rearrange("p (m h) -> p m h", h=HALF)
                    b = tmp_sin.rearrange("p (m h) -> p m h", h=HALF)
                    V.tensor_tensor(a, src, bc(rope0[:, t, 0, :], [P, 16, HALF], [1]), ALU.mult)
                    link(V.tensor_tensor(b, src, bc(rope0[:, t, 1, :], [P, 16, HALF], [1]), ALU.mult))
                    d = rot[r % 2].rearrange("p (n k h) -> p n k h", k=2, h=HALF)
                    a = tmp_cos.rearrange("p (n k h) -> p n k h", k=2, h=HALF)
                    b = tmp_sin.rearrange("p (n k h) -> p n k h", k=2, h=HALF)
                    V.tensor_tensor(d[:, :, 0, :], a[:, :, 0, :], b[:, :, 1, :], ALU.subtract)
                    V.tensor_tensor(d[:, :, 1, :], a[:, :, 1, :], b[:, :, 0, :], ALU.add).then_inc(z_roped, 1)

            def attention(l):
                for s in range(NSTEP + 1):
                    if s < NSTEP:
                        k = s % 4
                        dve.wait_ge(s_ready[l], s + 1)
                        if s == 0:
                            if l == 0:
                                dve.wait_ge(zrT_ready, 8)
                            else:
                                dve.wait_ge(qrT_ready, 8)
                                dve.wait_ge(ss1_ready, 2)
                        if s >= 4:
                            u4 = unit(l, s - 4)
                            dve.wait_ge(pT_ready[l], (u4 if u4 is not None else unit(l, s - 3)) + 1)
                        V.tensor_tensor_reduce(prob[k][:, 0:P], ps[4 + s % 2][:, 0:P], mask[:, P:2 * P], 1.0, -3.0 * BIG,
                                               ALU.add, ALU.max, mx[:, k, 0:1])
                        link(V.tensor_tensor_reduce(prob[k][:, P:3 * P], ps[4 + s % 2][:, P:3 * P], mask[:, 0:2 * P],
                                                    1.0, -3.0 * BIG, ALU.add, ALU.max, mx[:, k, 1:2]))
                        V.tensor_scalar(nm[:, k, :], mx[:, k, :], -SCALE[l], None, ALU.mult).then_inc(m_ready[l], 1)
                    if s >= 1:
                        j = s - 1
                        k = j % 4
                        dve.wait_ge(e_ready[l], j + 1)
                        link(V.reciprocal(rs[:, k, :], sm[:, k, :]))
                        if diff(l, j) and j % 2:
                            link(V.tensor_scalar(rs[:, k, :], rs[:, k, :], nlam, None, ALU.mult))
                            k0 = (j - 1) % 4
                            V.scalar_tensor_tensor(prob[k0][:, 0:P], prob[k][:, 0:P], rs[:, k, 0:1],
                                                   prob[k0][:, 0:P], ALU.mult, ALU.add)
                            V.scalar_tensor_tensor(prob[k0][:, P:3 * P], prob[k][:, P:3 * P], rs[:, k, 1:2],
                                                   prob[k0][:, P:3 * P], ALU.mult, ALU.add).then_inc(p_ready[l], 1)
                        else:
                            V.tensor_scalar(prob[k][:, 0:P], prob[k][:, 0:P], rs[:, k, 0:1], None, ALU.mult)
                            i = V.tensor_scalar(prob[k][:, P:3 * P], prob[k][:, P:3 * P], rs[:, k, 1:2], None,
                                                ALU.mult)
                            if diff(l, j):
                                link(i)
                            else:
                                i.then_inc(p_ready[l], 1)

            def add_residual(l):
                for t in range(T):
                    for n in range(2):
                        dve.wait_ge(wo_ready[l], 2 * t + n + 1)
                        v = xs[:, t, 512 * n:512 * n + 512]
                        V.tensor_tensor(v, v, ps[WO_BANK[l][2 * t + n]][:, :], ALU.add).then_inc(xr[2 * l + 1][t], 1)

            def project1():
                dve.wait_ge(ss1_ready, 2)
                V.tensor_scalar(ms1[:, :, 0], ss1[:, :, 0], 1.0 / QR, EPS, ALU.mult, ALU.add)
                link(V.tensor_scalar(ms1[:, :, 1], ss1[:, :, 1], 1.0 / KR, EPS, ALU.mult, ALU.add))
                V.reciprocal(ms1, ms1).then_inc(ms1_ready, 1)
                link(V.memset(kr_in, 0.0))
                z = z1[:, :, QR + KR:].rearrange("p t (k h) -> p t k h", k=2)
                cos = bc(rope[:, :, 64:80], [P, T, 2, RR // 2], [2])
                sin = bc(rope[:, :, 80:96], [P, T, 2, RR // 2], [2])
                rotate(kr_in[:, :, NOPE:].rearrange("p t (k h) -> p t k h", k=2), z, cos, sin, T * RR, RR // 2)
                dve.wait_ge(rs1_ready, 1)
                for t in range(T):
                    V.tensor_scalar(z1[:, t, 0:QR], z1[:, t, 0:QR], rs1[:, t, 0:1], None, ALU.mult)
                    i = V.tensor_scalar(z1[:, t, QR:QR + KR], z1[:, t, QR:QR + KR], rs1[:, t, 1:2], None, ALU.mult)
                i.then_inc(zn_ready, 1)
                for i in range(8):
                    t = i % T
                    b = ps[mm1.index(("q", i)) % 4][:, 0:4 * QH].rearrange("p (h d) -> p h d", h=4)
                    d = rot[i % 2][:, 0:4 * QH].rearrange("p (h d) -> p h d", h=4)
                    dve.wait_ge(qmm_ready, i + 1)
                    if i >= 2:
                        dve.wait_ge(qrT_ready, i - 1)
                    if i >= 1:
                        dve.wait_ge(q_roped, i)
                    else:
                        dve.wait_ge(zn_ready, 1)
                    V.tensor_copy(d[:, :, 0:NOPE], b[:, :, 0:NOPE])
                    cos = bc(rope[:, t, 64:80], [P, 4, 2, RR // 2], [1, 1])
                    sin = bc(rope[:, t, 80:96], [P, 4, 2, RR // 2], [1, 1])
                    rotate(d[:, :, NOPE:].rearrange("p h (k e) -> p h k e", k=2),
                           b[:, :, NOPE:].rearrange("p h (k e) -> p h k e", k=2), cos, sin, 4 * RR, RR // 2
                           ).then_inc(q_roped, 1)

            def route(l):
                n = 2 * l + 1
                dve.wait_ge(rstd_ready[n], 1)
                dve.wait_ge(gain_loaded, 16 * (l + 1))
                for t in range(T):
                    V.scalar_tensor_tensor(hp[:, t, :].rearrange("s (c p) -> s p c", c=C),
                                           xs[:, t, :].rearrange("s (p c) -> s p c", c=C), rstd[:, t:t + 1],
                                           gain[:, :].rearrange("s (p c) -> s p c", c=C), ALU.mult, ALU.mult
                                           ).then_inc(hp_ready[l], 1)
                dve.wait_ge(lg_ready[l], 2)
                for t in range(T):
                    V.scalar_tensor_tensor(lgg[:, 0, t, :], ps[4][:, 64 * t:64 * t + NG], rstd[:, t:t + 1],
                                           br[:, l, 0:NG], ALU.mult, ALU.add)
                    i = V.scalar_tensor_tensor(lg[:, t, :], ps[4][:, 64 * t + NG:64 * t + NG + NE], rstd[:, t:t + 1],
                                               br[:, l, NG:], ALU.mult, ALU.add)
                link(i)
                G4 = [P, T, NG]
                E3 = [P, T, NE]
                link(V.tensor_reduce(gm, lgg[:, 0], AX.X, ALU.max))
                link(V.tensor_tensor(lgg[:, 1], lgg[:, 0], bc(gm, G4, [2]), ALU.subtract))
                link(V.tensor_scalar(lgg[:, 2], lgg[:, 1], 0.0, None, ALU.is_ge))
                link(V.tensor_tensor(lgg[:, 2], lgg[:, 2], bc(idxn[:, 0:NG], G4, [1]), ALU.mult))
                V.tensor_reduce(sel1, lgg[:, 2], AX.X, ALU.min).then_inc(gmax_ready[l], 1)
                dve.wait_ge(gmax_ready[l], 1)
                link(V.tensor_tensor(lgg[:, 2], bc(idxn[:, 0:NG], G4, [1]), bc(sel1, G4, [2]), ALU.is_equal))
                link(V.tensor_scalar(lgg[:, 0], lgg[:, 2], 1.0, BIG, ALU.subtract, ALU.mult))
                lge4 = lge.rearrange("p t (g e) -> p t g e", g=NG)
                link(V.tensor_tensor(lge4, lg.rearrange("p t (g e) -> p t g e", g=NG),
                                     bc(lgg[:, 0], [P, T, NG, EPG], [3]), ALU.add))
                def best(m, onehot):
                    link(V.tensor_reduce(m, lge, AX.X, ALU.max))
                    link(V.tensor_tensor(t0, lge, bc(m, E3, [2]), ALU.is_equal))
                    link(V.tensor_tensor(t0, t0, bc(idxn[:, :], E3, [1]), ALU.mult))
                    link(V.tensor_reduce(sel1, t0, AX.X, ALU.min))
                    link(V.tensor_tensor(onehot, bc(idxn[:, :], E3, [1]), bc(sel1, E3, [2]), ALU.is_equal))
                best(m1, oh1)
                link(V.scalar_tensor_tensor(lge, oh1, -3.0 * BIG, lge, ALU.mult, ALU.add))
                best(m2, oh2)
                V.tensor_tensor(routed, oh1, oh2, ALU.add).then_inc(routed_ready[l], 1)
                V.tensor_tensor(ex2, m2, m1, ALU.subtract).then_inc(emax_ready[l], 1)
                dve.wait_ge(gexp[l], 1)
                link(V.tensor_reduce(gs_, lgg[:, 1], AX.X, ALU.add))
                dve.wait_ge(eexp[l], 1)
                link(V.tensor_scalar(den, ex2, 1.0, None, ALU.add))
                link(V.tensor_tensor(den, den, gs_, ALU.mult))
                link(V.reciprocal(w1, den))
                link(V.tensor_tensor(w2, w1, ex2, ALU.mult))
                V.tensor_tensor(gate, oh1, bc(w1, E3, [2]), ALU.mult)
                link(V.tensor_tensor(t0, oh2, bc(w2, E3, [2]), ALU.mult))
                link(V.tensor_tensor(gate, gate, t0, ALU.add))
                dve.wait_ge(pos_ready[l], 1)
                link(V.tensor_reduce(cmax, ps[5][0:1, 2 * NE:3 * NE].rearrange("p (q e) -> p q e", e=LANES), AX.X,
                                     ALU.max))
                link(V.scalar_tensor_tensor(pos, ps[5][:, 0:2 * NE].rearrange("p (t e) -> p t e", t=T), 1.0, routed,
                                            ALU.add, ALU.mult))
                link(V.tensor_scalar(pos, pos, -1.0, None, ALU.add))
                link(V.tensor_tensor(cnt_ge[:, 0:QUARTS, 0:7], bc(cmax, [1, QUARTS, 7], [2]), thr[:, :, :], ALU.is_gt))
                link(V.tensor_reduce(rnd, cnt_ge[:, 0:QUARTS, 0:7], AX.X, ALU.add))
                link(V.tensor_scalar(rnd, rnd, 1.0, None, ALU.add))
                link(V.tensor_tensor(cnt_ge[:, :, :], before[:, :, :], bc(rnd, [1, QUARTS + 1, QUARTS], [1]), ALU.mult))
                link(V.tensor_reduce(bfl, cnt_ge[:, :, :], AX.X, ALU.add))
                V.tensor_copy(bounds[:, l, 0:QUARTS + 1], bfl).then_inc(bounds_ready[l], 1)

            def experts(l):
                dve.wait_ge(bounds_ready[l], 1)
                with dve.Fori(0, QUARTS // 2) as i:
                    for half in range(2):
                        q = 2 * i + half
                        first = dve.value_load(bounds[0:1, l, bass.ds(q, 1)], min_val=0, max_val=8 * QUARTS)
                        end = dve.value_load(bounds[0:1, l, bass.ds(q + 1, 1)], min_val=1, max_val=8 * QUARTS)
                        lanes = bass.ds(q * LANES, LANES)
                        with dve.Fori(first, end) as job:
                            for t in range(T):
                                m = V.tensor_tensor(pick[:, t], bc(idx[:, 0:SLOTS], [P, LANES, SLOTS], [1]),
                                                    bc(pos[:, t, lanes], [P, LANES, SLOTS], [2]), ALU.is_equal)
                            m.then_inc(pick_made[l], 1)
                            dve.wait_ge(pick_made[l], job + 1)
                            for t in range(T):
                                m = V.tensor_tensor(pickg[:, t], pick[:, t], bc(gate[:, t, lanes], [P, LANES, SLOTS], [2]),
                                                    ALU.mult)
                            m.then_inc(pick_ready[l], 1)
                            V.tensor_scalar(pos[:, :, lanes], pos[:, :, lanes], -float(SLOTS), None, ALU.add)
                            dve.wait_ge(xg_ready[l][1], job + 1)
                            V.tensor_copy(xgT[:, 4:8, :].rearrange("p c s -> p (c s)"), ps[5][:, :]).then_inc(xgT_d[l], 1)
                            dve.wait_ge(cT[l], job + 1)
                            V.tensor_copy(comb, ps[7][:, 256:512]).then_inc(comb_sb[l], 1)
                            dve.wait_ge(silu_done[l], job + 1)
                            V.tensor_tensor(hid[:, :, :].rearrange("s c f -> s f c"),
                                            sil.rearrange("s (f c) -> s f c", c=FC),
                                            ps[6][:, FF:2 * FF].rearrange("s (f c) -> s f c", c=FC), ALU.mult
                                            ).then_inc(hid_ready[l], 1)
                            dve.wait_ge(b_done[l], job + 1)
                            V.tensor_copy(ysb[:, 512:1024], ps[5][:, :]).then_inc(y_d[l], 1)
                            dve.wait_ge(y_d[l], job + 1)
                jobs = dve.value_load(bounds[0:1, l, QUARTS:QUARTS + 1], min_val=1, max_val=8 * QUARTS)
                dve.wait_ge(comb_done[l], jobs)
                for n in range(2):
                    V.tensor_copy(xs[:, 1, 512 * n:512 * n + 512], ps[2 + n][:, :]).then_inc(xr[2 * l + 2][1], 1)

            norm(0)
            for k in range(2):
                V.tensor_tensor_reduce(lamv[:, 2 * k, :], lamv[:, 2 * k, :], lamv[:, 2 * k + 1, :], 1.0, 0.0, ALU.mult,
                                       ALU.add, lsum[:, k:k + 1])
            V.tensor_scalar(gsub[:, :], gsub[:, :], 1.0 - LAM_INIT, None, ALU.mult).then_inc(lam_sum, 1)
            dve.wait_ge(lam_exp, 1)
            link(V.tensor_tensor(nlam, lexp[:, 1:2], lexp[:, 0:1], ALU.subtract))
            link(V.tensor_scalar(nlam, nlam, -LAM_INIT, None, ALU.add))
            dve.wait_ge(consts, 1)
            project0()
            attention(0)
            dve.wait_ge(sso_ready, 2)
            link(V.tensor_scalar(mso, sso, 1.0 / DV, EPS, ALU.mult, ALU.add))
            V.reciprocal(mso, mso).then_inc(mso_ready, 1)
            dve.wait_ge(rso_ready, 1)
            dve.wait_ge(pT_ready[0], 12)
            for b in range(2):
                V.tensor_tensor(on[:, 512 * b:512 * b + 512].rearrange("p (i d) -> p i d", i=4),
                                ps[2 + b][:, :].rearrange("p (i d) -> p i d", i=4),
                                bc(rso[:, 4 * b:4 * b + 4], [P, 4, DV], [2]), ALU.mult).then_inc(on_ready, 1)
            add_residual(0)
            norm(1)
            route(0)
            experts(0)
            norm(2)
            project1()
            attention(1)
            add_residual(1)
            norm(3)
            route(1)
            experts(1)
            norm(4)
            dve.wait_ge(rstd_ready[4], 1)
            dve.wait_ge(gain_loaded, 16 * 3)
            for t in range(T):
                V.scalar_tensor_tensor(xs[:, t, :], xs[:, t, :], rstd[:, t:t + 1], gain[:, :], ALU.mult, ALU.mult
                                       ).then_inc(y_out, 1)


_INS = ["x", "attn_norm", "ev_w_in", "ev_lambda_q1", "ev_lambda_k1", "ev_lambda_q2", "ev_lambda_k2", "ev_subln",
        "ev_w_out", "od_w_in", "od_q_norm", "od_kv_norm", "od_w_q_up", "od_w_kv_up", "od_w_out", "ffn_norm",
        "moe_w_group", "moe_b_group", "moe_w_expert", "moe_b_expert", "moe_w_gate", "moe_w_up", "moe_w_down",
        "final_norm"]


def kernel(**inputs):
    import numpy as np
    import concourse.bacc as bacc
    from concourse.bass_utils import run_bass_kernel_spmd

    seq = inputs["x"].shape[1]
    pos = np.arange(seq, dtype=np.float32)[:, None]
    cols = []
    for dim in (64, 32):
        inv = (1.0 / (10000.0 ** (np.arange(0, dim, 2, dtype=np.float32) / dim))).astype(np.float32)
        ang = pos * inv[None, :]
        cols += [np.cos(ang), np.sin(ang)]
    tab = np.concatenate(cols, axis=1).astype(np.float32)

    nc = bacc.Bacc("TRN2", target_bir_lowering=False, num_devices=1)
    arrays, args = {}, []
    for name in _INS:
        a = np.ascontiguousarray(inputs[name])
        arrays[f"in_{name}"] = a
        args.append(nc.dram_tensor(f"in_{name}", a.shape, mybir.dt.from_np(a.dtype), kind="ExternalInput").ap())
    arrays["rope_tab"] = tab
    args.append(nc.dram_tensor("rope_tab", tab.shape, F32, kind="ExternalInput").ap())
    args.append(nc.dram_tensor("out_y", tuple(inputs["x"].shape), F32, kind="ExternalOutput").ap())
    trunk(nc, *args)
    r = run_bass_kernel_spmd(nc, [arrays], core_ids=[0])
    return r.results[0]["out_y"]
```

```python
import math
from contextlib import ExitStack

import concourse.bass as bass
from concourse import mybir

F32 = mybir.dt.float32
I32 = mybir.dt.int32
U32 = mybir.dt.uint32
ALU = mybir.AluOpType
ACT = mybir.ActivationFunctionType
AX = mybir.AxisListType

P = 128
EPS = 1e-6
BIG = 1e30
SLOTS = 32
LANES = 4
SLOTS_W = 5


def trunk(nc, x, attn_norm, ev_w_in, ev_lambda_q1, ev_lambda_k1, ev_lambda_q2, ev_lambda_k2, ev_subln, ev_w_out,
          od_w_in, od_q_norm, od_kv_norm, od_w_q_up, od_w_kv_up, od_w_out, ffn_norm, moe_w_group, moe_b_group,
          moe_w_expert, moe_b_expert, moe_w_gate, moe_w_up, moe_w_down, final_norm, rope_tab, out):
    _, S, D = x.shape
    T = S // P
    C = D // P
    LAYERS = attn_norm.shape[0]
    NG = moe_w_group.shape[2]
    NE = moe_w_expert.shape[2]
    EPG = NE // NG
    FF = moe_w_gate.shape[3]
    FC = FF // P
    QUARTS = NE // LANES
    HD = ev_lambda_q1.shape[1]
    HALF = HD // 2
    DV = ev_subln.shape[1]
    DH = ev_w_in.shape[2] // 512
    QR, KR = od_q_norm.shape[1], od_kv_norm.shape[1]
    ODN = od_w_in.shape[2]
    RR = ODN - QR - KR
    NH1 = 16
    QH = od_w_q_up.shape[2] // NH1
    NOPE = QH - RR
    LAM_INIT = 0.8 - 0.6 * math.exp(-0.3 * 0)
    SCALE = [HD ** -0.5, QH ** -0.5]
    assert T == 2 and C == 8 and FC == 2 and DH == 6 and QH == 96 and NE * 8 == S

    ctx = ExitStack()
    with ctx:
        def sb(name, shape, dt=F32):
            return ctx.enter_context(nc.sbuf_tensor(name, shape, dt))

        def sem(name):
            return ctx.enter_context(nc.semaphore(name))

        ps = [ctx.enter_context(nc.psum_tensor(f"ps{i}", [P, 512], F32)) for i in range(8)]

        UNIT = 2 * 2 * C * FF
        assert UNIT == LANES * FC * D
        weights = sb("weights", [P, SLOTS_W, UNIT])
        w_gu = weights[:, :, :].rearrange("p s (e k c f) -> p s e k c f", e=2, k=2, c=C)
        w_dn = weights[:, :, :].rearrange("p s (e c n) -> p s e c n", e=LANES, c=FC)
        GU_AT = [[0, 1], [3, 4]]
        DN_AT = 2

        stream_raw = [weights[:, 3, UNIT // 2 * h:UNIT // 2 * (h + 1)] for h in range(2)]
        qk_raw = weights[:, 4, :]
        qT0 = qk_raw[:, 0:8 * S].rearrange("p (b s) -> p b s", b=8)
        kP0 = qk_raw[:, 8 * S:24 * S].rearrange("p (b r s) -> p b r s", b=8, r=2)
        qT1 = qk_raw[:, 0:NH1 * S].rearrange("p (h s) -> p h s", h=NH1)
        kT1 = qk_raw[:, NH1 * S:2 * NH1 * S].rearrange("p (h s) -> p h s", h=NH1)

        xs = sb("xs", [P, T, D])
        hT = sb("hT", [P, C, S])
        oT = hT
        vh = sb("vh", [P, T, D])
        hp = vh
        scr = sb("scr", [P, 3072])
        rot = [scr[:, 512 * i:512 * i + 512] for i in range(2)]
        tmp_cos, tmp_sin = scr[:, 1024:1536], scr[:, 1536:2048]
        prob = [scr[:, 384 * i:384 * i + 384] for i in range(4)]
        probT = [scr[:, 2048:2432], scr[:, 2432:2816], scr[:, 1536:1920]]
        junk = [scr[:, D * t:D * t + D] for t in range(T)]
        junk_late = [scr[:, 2 * D:3 * D], junk[1]]
        on = scr[:, 0:D]
        z1 = scr[:, 2048:2048 + T * ODN].rearrange("p (t n) -> p t n", t=T)
        xgT = scr[:, 0:C * P].rearrange("p (c s) -> p c s", c=C)
        ysb = scr[:, 0:D]
        hid = scr[:, 1024:1280].rearrange("p (c f) -> p c f", c=FC)
        hidT = scr[:, 1280:1536].rearrange("p (c s) -> p c s", c=FC)
        comb = scr[:, 1536:1792]
        pick = scr[:, 1792:2048].rearrange("p (t e s) -> p t e s", t=T, e=LANES)
        sil = scr[:, 1792:2048]
        pickg = scr[:, 2048:2304].rearrange("p (t e s) -> p t e s", t=T, e=LANES)
        kr_in = scr[:, 2880:3072].rearrange("p (t n) -> p t n", t=T)
        lamv = scr[:, 2816:3072].rearrange("p (k n) -> p k n", k=4)

        gain = sb("gain", [P, D])
        lat = gain
        cqT = lat[:, 0:2 * S].rearrange("p (c s) -> p c s", c=2)
        ckvT = lat[:, 2 * S:3 * S]
        krT = lat[:, 3 * S:4 * S]
        mask = sb("mask", [P, 2 * P])
        ident = sb("ident", [P, P])
        tri = sb("tri", [P, P])
        ones = sb("ones", [P, P])
        wr = sb("wr", [P, C, NG + NE])
        br = sb("br", [P, LAYERS, NG + NE])
        gcol = sb("gcol", [P, 2 * LAYERS, C])
        rope = sb("rope", [P, T, 96])
        rope0 = sb("rope0", [P, T, 2, HALF])
        SMALLS = 4 + 3 + 2 * LAYERS
        gsub = sb("gsub", [P, 1])
        gq = sb("gq", [P, 2])
        gkv = sb("gkv", [P, 1])
        idx = sb("idx", [P, NE])
        idx1 = sb("idx1", [P, NE])
        thr = sb("thr", [1, QUARTS, 8])
        before = sb("before", [1, QUARTS + 1, QUARTS])
        bounds = sb("bounds", [1, LAYERS, QUARTS + 2], I32)
        st = sb("st", [P, 144])
        ss, ms, rstd = st[:, 0:2], st[:, 2:4], st[:, 4:6]
        mx = st[:, 8:16].rearrange("p (u t) -> p u t", t=2)
        nm = st[:, 16:24].rearrange("p (u t) -> p u t", t=2)
        sm = st[:, 24:32].rearrange("p (u t) -> p u t", t=2)
        rs = st[:, 32:40].rearrange("p (u t) -> p u t", t=2)
        nlam = st[:, 40:41]
        lsum = st[:, 42:44]
        lexp = st[:, 44:46]
        sso, mso, rso = st[:, 48:56], st[:, 56:64], st[:, 64:72]
        ss1 = st[:, 72:76].rearrange("p (t k) -> p t k", t=T)
        ms1 = st[:, 76:80].rearrange("p (t k) -> p t k", t=T)
        rs1 = st[:, 80:84].rearrange("p (t k) -> p t k", t=T)
        cmax, rnd = st[0:1, 88:96], st[0:1, 96:104]
        gs_ = st[:, 118:120]
        ex2, den, w1, w2 = st[:, 126:128], st[:, 128:130], st[:, 130:132], st[:, 132:134]
        rt = scr[:, 1024:1024 + 6 * T * NE]
        lg, lge, routed, second = (rt[:, T * NE * k:T * NE * (k + 1)].rearrange("p (t e) -> p t e", t=T)
                                   for k in range(4))
        best = rt[:, 4 * T * NE:6 * T * NE].rearrange("p (t k e) -> p t k e", t=T, k=2)
        lgp = sb("lgp", [P, T, 8])[:, :, :]
        top = sb("top", [P, 2, T, 8])[:, :, :, :]
        where = sb("where", [P, 2, T, 8], U32)[:, :, :, :]
        lgg = sb("lgg", [P, T, NG])[:, :, :]
        other = sb("other", [P, T, NG])[:, :, :]
        pos = sb("pos", [P, T, NE])[:, :, :]
        gate = sb("gate", [P, T, NE])[:, :, :]
        exceeds = scr[0:1, 1024:1024 + 8 * QUARTS].rearrange("p (q m) -> p q m", m=8)
        cnt_ge = scr[0:1, 1408:1408 + (QUARTS + 1) * QUARTS].rearrange("p (k q) -> p k q", q=QUARTS)

        def bc(ap, shape, axis):
            for a in axis:
                ap = ap.unsqueeze(a)
            return ap.to_broadcast(shape)

        x_loaded = [sem("x0_loaded"), sem("x1_loaded")]
        smalls_loaded, w_in_first = sem("smalls_loaded"), [sem("w_in_first0"), sem("w_in_first1")]
        gcol_loaded = sem("gcol_loaded")
        stream_loaded = [sem("stream_loaded0"), sem("stream_loaded1")]
        gua_loaded = [sem("gate_up_01_loaded_even"), sem("gate_up_01_loaded_odd")]
        gub_loaded = [sem("gate_up_23_loaded_even"), sem("gate_up_23_loaded_odd")]
        dn_loaded = [sem("down_loaded_even"), sem("down_loaded_odd")]
        gain_loaded, wr_loaded, wr_ready = sem("gain_loaded"), sem("wr_loaded"), sem("wr_ready")
        early_loaded = sem("early_loaded")
        consts, kzero, ident_made = sem("consts"), sem("kzero"), sem("ident_made")
        pool_step = sem("pool_step")
        chain, achain = sem("dve_chain"), sem("act_chain")
        N5 = range(2 * LAYERS + 1)
        xr = [[sem(f"x_ready{n}_{t}") for t in range(T)] for n in N5]
        xT_ready = sem("xT_ready")
        hT_ready = sem("hT_ready")
        ss_ready = sem("ss_ready")
        rec_ready = sem("rec_ready")
        rstd_ready = sem("rstd_ready")
        xT_act = [sem(f"xT_act{l}") for l in range(LAYERS)]
        z_ready, z_roped, v_ready = sem("z_ready"), sem("z_roped"), sem("v_ready")
        zrT_ready, qk_evac = sem("zrT_ready"), sem("qk_evac")
        L2 = range(LAYERS)
        s_ready = sem("s_ready")
        m_ready = sem("m_ready")
        e_ready = sem("e_ready")
        p_ready = sem("p_ready")
        pT_ready = sem("pT_ready")
        pT_evac = sem("pT_evac")
        pv_done = sem("pv_done")
        oT_evac = sem("oT_evac")
        sso_ready, mso_ready, rso_ready = sem("sso_ready"), sem("mso_ready"), sem("rso_ready")
        on_ready, onT_ready, lam_sum, lam_exp = sem("on_ready"), sem("onT_ready"), sem("lam_sum"), sem("lam_exp")
        wo_ready = sem("wo_ready")
        z1_ready, z1_sb, ss1_ready = sem("z1_ready"), sem("z1_sb"), sem("ss1_ready")
        ms1_ready, rs1_ready, zn_ready = sem("ms1_ready"), sem("rs1_ready"), sem("zn_ready")
        cT_ready, cT_evac, kr_spread = sem("cT_ready"), sem("cT_evac"), sem("kr_spread")
        qmm_ready, kvmm_ready = sem("qmm_ready"), sem("kvmm_ready")
        q_roped, kv_evac, qrT_ready, qT_evac = sem("q_roped"), sem("kv_evac"), sem("qrT_ready"), sem("qT_evac")
        lg_ready = [sem(f"logits_ready{i}") for i in L2]
        gexp = [sem(f"group_exp{i}") for i in L2]
        eexp = [sem(f"expert_exp{i}") for i in L2]
        gmax_ready = [sem(f"group_max{i}") for i in L2]
        emax_ready = [sem(f"expert_max{i}") for i in L2]
        routed_ready = [sem(f"routed{i}") for i in L2]
        pos_ready = [sem(f"pos_ready{i}") for i in L2]
        hp_ready = [sem(f"hp_ready{i}") for i in L2]
        bounds_ready = [sem(f"bounds_ready{i}") for i in L2]
        pick_made = [sem(f"pick_made{i}") for i in L2]
        pick_ready = [sem(f"pick_ready{i}") for i in L2]
        xg_ready = [[sem(f"xg_ready{i}_{h}") for h in range(2)] for i in L2]
        xgT_a = [sem(f"xgT_act{i}") for i in L2]
        xgT_d = [sem(f"xgT_dve{i}") for i in L2]
        cT = [sem(f"comb_transposed{i}") for i in L2]
        comb_sb = [sem(f"comb_sb{i}") for i in L2]
        a_done = [sem(f"gate_up_done{i}") for i in L2]
        silu_done = [sem(f"silu_done{i}") for i in L2]
        hid_ready = [sem(f"hid_ready{i}") for i in L2]
        hidT_ready = [sem(f"hidT_ready{i}") for i in L2]
        hidT_sb = [sem(f"hidT_sb{i}") for i in L2]
        b_half = [sem(f"down_half{i}") for i in L2]
        b_done = [sem(f"down_done{i}") for i in L2]
        y_a = [sem(f"y_act{i}") for i in L2]
        y_d = [sem(f"y_dve{i}") for i in L2]
        comb0_done = [sem(f"comb_done_tile0_{i}") for i in L2]
        comb_done = [sem(f"comb_done{i}") for i in L2]
        y_out, stored = sem("y_out"), sem("stored")

        rope_items = [2 * n + t for n in (0, 1, 3, 4) for t in range(T)]
        v_items = [2 * n + t for n in (2, 5) for t in range(T)]
        proj0 = []
        for i in range(2 * DH + 2):
            if i < 2 * DH:
                proj0.append(("z", i))
            if i - 2 in rope_items:
                proj0.append(("T", rope_items.index(i - 2)))
        proj1, kv_list = [], []
        rest = [("v", j) for j in range(4)] + [("k", j) for j in range(8)]
        for r in range(8 + 2):
            if r < 8:
                proj1.append(("q", r))
            if r >= 2:
                proj1.append(("T", r - 2))
                proj1 += rest[:2] if r > 2 else rest[:1]
                rest = rest[2:] if r > 2 else rest[1:]
        proj1 += rest
        mm1 = [it for it in proj1 if it[0] != "T"]
        kv_list = [it for it in mm1 if it[0] != "q"]
        NSTEP = 16
        WARM_UP = 12

        def unit(layer, s):
            if not 0 <= s < NSTEP:
                return None
            if layer == 1 or s < 8:
                return s
            return 8 + (s - 9) // 2 if s % 2 else None

        def diff(layer, s):
            return layer == 0 and s >= 8

        def buffer_of(layer, u):
            return (u % 2, u - 1) if layer == 0 and u >= 8 else (u % 3, u - 2)

        WO_AT, WO_LOADS = [[0, 1], [1, 0]], [[3, 4], [6, 6]]
        FILL_FROM, FILLS = [12, 7], [7, 12]
        WO_BANK = [[0, 1, 6, 7], [2, 3, 6, 7]]

        x_dram = x[0].rearrange("(t p) d -> p t d", p=P)
        out_dram = out[0].rearrange("(t p) d -> p t d", p=P)
        gate_dram = moe_w_gate.rearrange("l e (p c) f -> l e p (c f)", c=C)
        up_dram = moe_w_up.rearrange("l e (p c) f -> l e p (c f)", c=C)
        down_dram = moe_w_down.rearrange("l e (p c) n -> l e p (c n)", c=FC)

        def jobs_of(eng, l, q):
            _, pair = nc.values_load_multi_w_load_instructions(
                bounds[0:1, l, bass.ds(q, 2)], engines=[eng.engine], min_val=0, max_val=8 * QUARTS)
            return pair

        def load_router(eng, l):
            eng.dma_start(wr[:, :, 0:NG], moe_w_group[l].rearrange("(p c) g -> p c g", c=C)).then_inc(wr_loaded, 16)
            eng.dma_start(wr[:, :, NG:], moe_w_expert[l].rearrange("(p c) g -> p c g", c=C)).then_inc(wr_loaded, 16)

        block = ctx.enter_context(nc.Block())

        @block.sync
        def _(sp):
            def load_stream(slot, dst, src):
                sp.dma_start(dst, src).then_inc(stream_loaded[slot], 16)

            def load_gu(l, q, part, parity, experts=range(2)):
                for e in experts:
                    for k, w in enumerate((gate_dram, up_dram)):
                        sp.dma_start(w_gu[:, GU_AT[parity][part], e, k].rearrange("p c f -> p (c f)"),
                                     w[l, q * LANES + 2 * part + e]).then_inc((gua_loaded, gub_loaded)[part][parity], 16)

            def load_down(l, q, parity):
                for e in range(LANES):
                    sp.dma_start(w_dn[:, DN_AT, e].rearrange("p c n -> p (c n)"), down_dram[l, q * LANES + e]
                                 ).then_inc(dn_loaded[parity], 16)

            w_in = ev_w_in[0].rearrange("(p c) n -> p c n", c=C)
            w_in_sb = [s.rearrange("p (c n) -> p c n", c=C) for s in stream_raw]

            def load_w_out(l, w, half, h):
                v = w[0].rearrange("(c p) n -> p c n", p=P)
                load_stream(h, stream_raw[h].rearrange("p (c n) -> p c n", c=C // 2), v[:, 4 * half:4 * half + 4, :])

            sp.dma_start(xs[:, 0, :], x_dram[:, 0, :]).then_inc(x_loaded[0], 16)
            for n in range(DH):
                if n >= 2:
                    sp.wait_ge(z_ready, 2 * (n - 1))
                if n == 0:
                    for h in range(2):
                        sp.dma_start(w_in_sb[0][:, 4 * h:4 * h + 4, :], w_in[:, 4 * h:4 * h + 4, 0:512]
                                     ).then_inc(w_in_first[h], 16)
                    sp.dma_start(xs[:, 1, :], x_dram[:, 1, :]).then_inc(x_loaded[1], 16)
                else:
                    load_stream(n % 2, w_in_sb[n % 2], w_in[:, :, 512 * n:512 * n + 512])
                if n == 1:
                    load_gu(0, 0, 0, 0, (0,))
                if n == 2:
                    load_gu(0, 0, 0, 0, (1,))
                    sp.dma_start(gain[:, :], ffn_norm[0].partition_broadcast(P)).then_inc(gain_loaded, 16)
                if n == 3:
                    load_gu(0, 0, 1, 0, (0,))
                if n == 4:
                    load_gu(0, 0, 1, 0, (1,))
            sp.wait_ge(z_ready, 2 * 5)
            load_w_out(0, ev_w_out, 0, 0)
            load_down(0, 0, 0)
            sp.wait_ge(z_ready, 2 * 6)
            load_w_out(0, ev_w_out, 1, 1)

            def jobs_before(l, q):
                return sp.value_load(bounds[0:1, l, bass.ds(q, 1)], min_val=1, max_val=8 * QUARTS)

            def experts(l):
                sp.wait_ge(s_ready, NSTEP * l + NSTEP)
                load_gu(l, 1, 1, 1)
                sp.wait_ge(wo_ready, 4 * l + 4)
                load_gu(l, 1, 0, 1)
                sp.wait_ge(bounds_ready[l], 1)
                with sp.Fori(0, QUARTS // 2 - 1) as i:
                    for half in range(2):
                        q = 2 * i + 2 + half
                        before_last = jobs_before(l, q - 1)
                        sp.wait_ge(a_done[l], before_last)
                        load_gu(l, q, 0, half)
                        sp.wait_ge(b_done[l], before_last)
                        load_down(l, q - 1, 1 - half)
                        load_gu(l, q, 1, half)
                sp.wait_ge(b_done[l], jobs_before(l, QUARTS - 1))
                load_down(l, QUARTS - 1, 1)

            experts(0)
            sp.wait_ge(a_done[0], jobs_before(0, QUARTS))
            load_stream(0, stream_raw[0][:, 0:C * ODN].rearrange("p (c n) -> p c n", c=C),
                        od_w_in[0].rearrange("(p c) n -> p c n", c=C))
            load_stream(1, stream_raw[1][:, 0:2 * QH * NH1].rearrange("p (c n) -> p c n", c=2),
                        od_w_q_up[0].rearrange("(c p) n -> p c n", p=P))
            load_gu(1, 0, 0, 0)
            load_gu(1, 0, 1, 0)
            sp.wait_ge(z1_ready, 2)
            load_stream(0, stream_raw[0][:, 0:P * NH1], od_w_kv_up[0])
            sp.wait_ge(b_done[0], jobs_before(0, QUARTS))
            load_down(1, 0, 0)
            sp.wait_ge(qmm_ready, 8)
            load_w_out(1, od_w_out, 0, 1)
            sp.wait_ge(kvmm_ready, len(kv_list))
            load_w_out(1, od_w_out, 1, 0)
            load_router(sp, 1)
            sp.wait_ge(kr_spread, 1)
            sp.dma_start(gain[:, :], ffn_norm[1].partition_broadcast(P)).then_inc(gain_loaded, 16)
            experts(1)
            sp.dma_start(gain[:, :], final_norm.partition_broadcast(P)).then_inc(gain_loaded, 16)
            for t in range(T):
                sp.wait_ge(y_out, t + 1)
                sp.dma_start(out_dram[:, t, :], xs[:, t, :]).then_inc(stored, 16)
            sp.wait_ge(stored, 16 * T)

        @block.gpsimd
        def _(pool):
            g = nc.gpsimd
            steps = [0]

            def then(ins):
                steps[0] += 1
                ins.then_inc(pool_step, 1)
                pool.wait_ge(pool_step, steps[0])

            then(g.memset(ident[:, :], 0.0))
            then(g.affine_select(out=ident[:, :], in_=ident[:, :], compare_op=ALU.not_equal, fill=1.0, base=0,
                                 pattern=[[-1, P]], channel_multiplier=1))
            g.nop().then_inc(ident_made, 1)
            then(g.memset(kP0[64:128, :, 0, :], 0.0))
            then(g.memset(kP0[0:64, :, 1, :], 0.0))
            g.nop().then_inc(kzero, 1)
            then(g.memset(mask[:, :], 0.0))
            then(g.affine_select(out=mask[:, P:2 * P], in_=mask[:, P:2 * P], compare_op=ALU.is_ge,
                                 fill=-BIG, base=0, pattern=[[-1, P]], channel_multiplier=1))
            then(g.memset(tri[:, :], 1.0))
            then(g.affine_select(out=tri[:, :], in_=tri[:, :], compare_op=ALU.is_gt, fill=0.0, base=0,
                                 pattern=[[1, P]], channel_multiplier=-1))
            then(g.memset(ones[:, :], 1.0))
            then(g.memset(before[:, :, :], 1.0))
            then(g.affine_select(out=before[:, :, :], in_=before[:, :, :], compare_op=ALU.is_gt, fill=0.0, base=0,
                                 pattern=[[1, QUARTS + 1], [-1, QUARTS]], channel_multiplier=0))
            then(g.iota(idx[:, :], pattern=[[1, NE]], base=0, channel_multiplier=0,
                        allow_small_or_imprecise_dtypes=True))
            then(g.iota(idx1[:, :], pattern=[[1, NE]], base=1, channel_multiplier=0,
                        allow_small_or_imprecise_dtypes=True))
            then(g.iota(thr[:, :, :], pattern=[[0, QUARTS], [SLOTS, 8]], base=0, channel_multiplier=0,
                        allow_small_or_imprecise_dtypes=True))
            then(g.memset(thr[:, :, 0:1], -1.0))
            g.nop().then_inc(consts, 1)

            def scale_router(l):
                pool.wait_ge(wr_loaded, 32 * (l + 1))
                pool.wait_ge(early_loaded, 16 * 2)
                g.tensor_tensor(wr[:, :, :], wr[:, :, :], bc(gcol[:, 2 * l + 1, :], [P, C, NG + NE], [2]), ALU.mult
                                ).then_inc(wr_ready, 1)

            scale_router(0)
            pool.wait_ge(cT_evac, 1)
            g.tensor_copy(kT1[NOPE:QH, :, :], bc(krT[NOPE:QH, :], [RR, NH1, S], [1])).then_inc(kr_spread, 1)
            pool.wait_ge(kr_spread, 1)
            scale_router(1)

        @block.tensor
        def _(pe):
            mm, tr = nc.tensor.matmul, nc.tensor.transpose

            def transpose_x(n, t):
                if n == 0:
                    pe.wait_ge(x_loaded[t], 16)
                else:
                    pe.wait_ge(xr[n][t], 2)
                v = xs[:, t, :].rearrange("s (p c) -> s c p", c=C)
                for h in range(2):
                    for j in range(4):
                        i = tr(ps[2 * t + h][:, P * j:P * j + P], v[:, 4 * h + j, :], ident[:, :])
                    i.then_inc(xT_ready, 1)

            def project0():
                w = [s.rearrange("p (c n) -> p c n", c=C) for s in stream_raw]
                for what, i in proj0:
                    if what == "z":
                        n, t = divmod(i, T)
                        if t == 0 and n >= 1:
                            pe.wait_ge(stream_loaded[n % 2], 16 * ((n + 1) // 2))
                        if n == 0:
                            transpose_x(0, t)
                            pe.wait_ge(hT_ready, 2 * t + 2)
                        if i >= 4 and i - 4 in rope_items:
                            pe.wait_ge(z_roped, rope_items.index(i - 4) + 1)
                        elif i >= 4:
                            pe.wait_ge(v_ready, v_items.index(i - 4) + 1)
                        for c in range(C):
                            if i == 0 and c % 4 == 0:
                                pe.wait_ge(w_in_first[c // 4], 16)
                            m = mm(ps[4 + i % 4][:, :], hT[:, c, P * t:P * t + P], w[n % 2][:, c, :],
                                   start=(c == 0), stop=(c == C - 1))
                        m.then_inc(z_ready, 1)
                    else:
                        pe.wait_ge(z_roped, i + 1)
                        if i >= 2:
                            pe.wait_ge(qk_evac, i - 1)
                        else:
                            pe.wait_ge(hT_ready, 4)
                        for j in range(4):
                            m = tr(ps[i % 2][:, P * j:P * j + P], rot[i % 2][:, P * j:P * j + P], ident[:, :])
                        m.then_inc(zrT_ready, 1)

            def attention(l):
                for s in range(NSTEP + 3):
                    if s < NSTEP:
                        if s == 0 and l == 0:
                            pe.wait_ge(v_ready, 4)
                            pe.wait_ge(z_roped, 8)
                            pe.wait_ge(qk_evac, 8)
                        if s == 0 and l == 1:
                            pe.wait_ge(kv_evac, len(kv_list))
                            pe.wait_ge(qT_evac, 8)
                            pe.wait_ge(kr_spread, 1)
                        if s >= 2:
                            pe.wait_ge(m_ready, NSTEP * l + s - 1)
                        if l == 0:
                            q, k, K = qT0[:, s // 2, :], kP0[:, s // 2, s % 2, :], P
                        else:
                            q, k, K = qT1[:, s, :], kT1[:, s, :], QH
                        mm(ps[4 + s % 2][:, 0:P], q[0:K, 0:P], k[0:K, 0:P], start=True, stop=True)
                        mm(ps[4 + s % 2][:, P:3 * P], q[0:K, P:S], k[0:K, 0:S], start=True, stop=True
                           ).then_inc(s_ready, 1)
                    out_products_between(l, s)
                    u = unit(l, s - 2)
                    if u is not None:
                        pe.wait_ge(p_ready, 12 * l + u + 1)
                        if u >= 2:
                            pe.wait_ge(pT_evac, 12 * l + u - 1)
                        src = prob[(s - 2 - diff(l, s - 2)) % 4]
                        for j in range(3):
                            m = tr(ps[6 + u % 2][:, P * j:P * j + P], src[:, P * j:P * j + P], ident[:, :])
                        m.then_inc(pT_ready, 1)
                    u = unit(l, s - 3)
                    if u is not None:
                        pT = probT[buffer_of(l, u)[0]]
                        if diff(l, s - 3):
                            pe.wait_ge(pT_evac, 12 * l + u + 1)
                            h = u - 8
                            o, a = ps[2 + h // 2], 256 * (h % 2)
                            v = vh[:, :, 512 + P * h:512 + P * h + P]
                            mm(o[:, a:a + P], pT[:, 0:P], v[:, 0, :], start=True, stop=True)
                            mm(o[:, a + P:a + 2 * P], pT[:, P:2 * P], v[:, 0, :], start=True, stop=False)
                            mm(o[:, a + P:a + 2 * P], pT[:, 2 * P:3 * P], v[:, 1, :], start=False, stop=True
                               ).then_inc(pv_done, 1)
                        elif u % 2:
                            pe.wait_ge(pT_evac, 12 * l + u + 1)
                            pair = u // 2
                            if pair >= 2:
                                pe.wait_ge(oT_evac, 6 * l + pair - 1)
                            for kt in range(T):
                                for r in range(2):
                                    head = 2 * pair + r
                                    o = ps[pair % 2][64 * r:64 * r + 64, :]
                                    v = vh[:, kt, 64 * head:64 * head + 64]
                                    pT = probT[buffer_of(l, head)[0]]
                                    if kt == 0:
                                        mm(o[:, 0:S], v, pT[:, 0:S], start=True, stop=False)
                                    else:
                                        mm(o[:, P:S], v, pT[:, 2 * P:3 * P], start=False, stop=True
                                           ).then_inc(pv_done, 1)

            def out_product(l, t, n, c):
                w = stream_raw[WO_AT[l][c // 4]].rearrange("p (c n) -> p c n", c=4)
                return mm(ps[WO_BANK[l][2 * t + n]][:, :], oT[:, c, P * t:P * t + P],
                          w[:, c % 4, 512 * n:512 * n + 512], start=(c == 0), stop=(c == C - 1),
                          skip_group_check=True)

            def out_loaded(l, half):
                pe.wait_ge(stream_loaded[WO_AT[l][half]], 16 * WO_LOADS[l][half])

            def out_products_between(l, s):
                if s - FILL_FROM[l] in range(FILLS[l]):
                    c, n = divmod(s - FILL_FROM[l], 2)
                    if n == 0:
                        if c % 4 == 0:
                            out_loaded(l, c // 4)
                        pe.wait_ge(oT_evac, 6 * l + (4 if l == 0 else c + 1))
                    out_product(l, 0, n, c)

            def rest_of_half0(l):
                for i in range(FILLS[l], 8):
                    out_product(l, 0, i % 2, i // 2)
                pe.wait_ge(pT_evac, 12 * l + (12 if l == 0 else 16))
                for n in range(2):
                    for c in range(4):
                        out_product(l, 1, n, c)

            def half1(l):
                if FILLS[l] < 9:
                    out_loaded(l, 1)
                pe.wait_ge(oT_evac, 6 * l + (6 if l == 0 else 8))
                for n in range(2):
                    for c in range(4, 8):
                        if 2 * c + n >= FILLS[l]:
                            m = out_product(l, 0, n, c)
                    m.then_inc(wo_ready, 1)
                for c in range(4, 8):
                    m = out_product(l, 1, 0, c)
                m.then_inc(wo_ready, 1)
                transpose_x(2 * l + 1, 0)
                for c in (4, 5):
                    out_product(l, 1, 1, c)
                router_product(l, 0)
                for c in (6, 7):
                    m = out_product(l, 1, 1, c)
                m.then_inc(wo_ready, 1)

            def router_product(l, t):
                if t == 0:
                    pe.wait_ge(wr_ready, l + 1)
                pe.wait_ge(hT_ready, 6 * l + 4 + t + 1)
                pe.wait_ge(xT_act[l], t + 1)
                for c in range(C):
                    m = mm(ps[4 + t][:, 0:NG + NE], hT[:, c, P * t:P * t + P], wr[:, c, :],
                           start=(c == 0), stop=(c == C - 1))
                m.then_inc(lg_ready[l], 1)

            def project1():
                pe.wait_ge(stream_loaded[0], 16 * 4)
                w = stream_raw[0][:, 0:C * ODN].rearrange("p (c n) -> p c n", c=C)
                for t in range(T):
                    pe.wait_ge(hT_ready, 6 + 2 * t + 2)
                    for c in range(C):
                        m = mm(ps[4 + t][:, 0:ODN], hT[:, c, P * t:P * t + P], w[:, c, :],
                               start=(c == 0), stop=(c == C - 1))
                    m.then_inc(z1_ready, 1)
                pe.wait_ge(zn_ready, 1)
                for t in range(T):
                    for c in range(2):
                        tr(ps[6][:, S * c + P * t:S * c + P * t + P], z1[:, t, P * c:P * c + P], ident[:, :])
                    tr(ps[7][:, P * t:P * t + P], z1[:, t, QR:QR + KR], ident[:, :])
                    m = tr(ps[7][0:QH, S + P * t:S + P * t + P], kr_in[:, t, :], ident[:, :])
                m.then_inc(cT_ready, 1)
                pe.wait_ge(cT_evac, 2)
                wq = stream_raw[1][:, 0:2 * QH * NH1].rearrange("p (c n) -> p c n", c=2)
                wkv = stream_raw[0][:, 0:P * NH1].rearrange("p (h k d) -> p h k d", h=NH1, k=2)
                done = {"q": 0, "kv": 0}
                for what, i in proj1:
                    if what == "T":
                        pe.wait_ge(q_roped, i + 1)
                        if i >= 2:
                            pe.wait_ge(qT_evac, i - 1)
                        for j in range(4):
                            m = tr(ps[4 + i % 2][0:QH, P * j:P * j + P], rot[i % 2][:, QH * j:QH * j + QH],
                                   ident[:, :])
                        m.then_inc(qrT_ready, 1)
                        continue
                    j = mm1.index((what, i))
                    if j >= 4:
                        w4, i4 = mm1[j - 4]
                        if w4 == "q":
                            pe.wait_ge(q_roped, i4 + 1)
                        else:
                            pe.wait_ge(kv_evac, kv_list.index((w4, i4)) + 1)
                    b = ps[j % 4]
                    if what == "q":
                        if i == 0:
                            pe.wait_ge(stream_loaded[1], 16 * 5)
                        g, t = divmod(i, T)
                        for c in range(2):
                            m = mm(b[:, 0:4 * QH], cqT[:, c, P * t:P * t + P], wq[:, c, 4 * QH * g:4 * QH * g + 4 * QH],
                                   start=(c == 0), stop=(c == 1))
                        m.then_inc(qmm_ready, 1)
                    elif what == "v":
                        if i == 0:
                            pe.wait_ge(stream_loaded[0], 16 * 5)
                        n, t = divmod(i, T)
                        mm(b[:, :], ckvT[:, P * t:P * t + P], wkv[:, 8 * n:8 * n + 8, 1, :], start=True, stop=True
                           ).then_inc(kvmm_ready, 1)
                    else:
                        for r in range(2):
                            m = mm(b[0:NOPE, S * r:S * r + S], wkv[:, 2 * i + r, 0, :], ckvT, start=True, stop=True)
                        m.then_inc(kvmm_ready, 1)

            def route(l):
                transpose_x(2 * l + 1, 1)
                router_product(l, 1)
                def residual(t):
                    for n in range(2):
                        mm(ps[2 * t + n][:, :], ident[:, :], xs[:, t, 512 * n:512 * n + 512], start=True, stop=False,
                           skip_group_check=True)

                residual(0)
                pe.wait_ge(routed_ready[l], 1)
                mm(ps[5][:, 0:NE], tri[:, :], routed[:, 0, :], start=True, stop=True)
                mm(ps[5][:, NE:2 * NE], ones[:, :], routed[:, 0, :], start=True, stop=False)
                mm(ps[5][:, NE:2 * NE], tri[:, :], routed[:, 1, :], start=False, stop=True)
                mm(ps[5][:, 2 * NE:3 * NE], ones[:, :], routed[:, 0, :], start=True, stop=False)
                mm(ps[5][:, 2 * NE:3 * NE], ones[:, :], routed[:, 1, :], start=False, stop=True
                   ).then_inc(pos_ready[l], 1)
                residual(1)

            def experts(l):
                pe.wait_ge(bounds_ready[l], 1)
                pe.wait_ge(hp_ready[l], 2)
                with pe.Fori(0, QUARTS // 2) as i:
                    for half in range(2):
                        q = 2 * i + half
                        first, end = jobs_of(pe, l, q)
                        gen = 16 * LANES * (QUARTS // 2 * l + 1) + i * (16 * LANES)
                        with pe.Fori(first, end) as job:
                            pe.wait_ge(pick_ready[l], job + 1)
                            for c in range(C):
                                for t in range(T):
                                    m = mm(ps[4 + c // 4][:, P * (c % 4):P * (c % 4) + P], hp[:, t, P * c:P * c + P],
                                           pick[:, t].rearrange("p e s -> p (e s)"), start=(t == 0), stop=(t == 1))
                                if c % 4 == 3:
                                    m.then_inc(xg_ready[l][c // 4], 1)
                            for t in range(T):
                                m = tr(ps[7][:, 256 + P * t:256 + P * t + P], pickg[:, t].rearrange("p e s -> p (e s)"),
                                       ident[:, :])
                            m.then_inc(cT[l], 1)
                            pe.wait_ge(gua_loaded[half], gen)
                            pe.wait_ge(gub_loaded[half], gen)
                            pe.wait_ge(xgT_a[l], job + 1)
                            for c in range(C):
                                if c == 4:
                                    pe.wait_ge(xgT_d[l], job + 1)
                                for e in range(LANES):
                                    m = mm(ps[6][SLOTS * e:SLOTS * e + SLOTS, :], xgT[:, c, SLOTS * e:SLOTS * e + SLOTS],
                                           w_gu[:, GU_AT[half][e // 2], e % 2, :, c, :], start=(c == 0),
                                           stop=(c == C - 1))
                            m.then_inc(a_done[l], 1)
                            pe.wait_ge(hid_ready[l], job + 1)
                            for c in range(FC):
                                m = tr(ps[7][:, P * c:P * c + P], hid[:, c, :], ident[:, :])
                            m.then_inc(hidT_ready[l], 1)
                            pe.wait_ge(dn_loaded[half], gen)
                            pe.wait_ge(hidT_sb[l], job + 1)
                            for n in range(2):
                                for c in range(FC):
                                    for e in range(LANES):
                                        m = mm(ps[4 + n][SLOTS * e:SLOTS * e + SLOTS, :],
                                               hidT[:, c, SLOTS * e:SLOTS * e + SLOTS],
                                               w_dn[:, DN_AT, e, c, 512 * n:512 * n + 512], start=(c == 0),
                                               stop=(c == FC - 1))
                                m.then_inc((b_half, b_done)[n][l], 1)
                            pe.wait_ge(comb_sb[l], job + 1)
                            for n in range(2):
                                pe.wait_ge((y_a, y_d)[n][l], job + 1)
                                for t in range(T):
                                    m = mm(ps[2 * t + n][:, :], comb[:, P * t:P * t + P],
                                           ysb[:, 512 * n:512 * n + 512], start=False, stop=False,
                                           skip_group_check=True)
                                    if n == 1:
                                        m.then_inc((comb0_done, comb_done)[t][l], 1)

            pe.wait_ge(ident_made, 1)
            for i in range(WARM_UP):
                mm(ps[7][:, 0:P], ident[:, :], ident[:, :], start=True, stop=True)
            project0()
            attention(0)
            rest_of_half0(0)
            pe.wait_ge(on_ready, 2)
            for b in range(2):
                for j in range(4):
                    m = tr(ps[4 + b][:, P * j:P * j + P], on[:, 512 * b + P * j:512 * b + P * j + P], ident[:, :])
                m.then_inc(onT_ready, 1)
            half1(0)
            route(0)
            experts(0)
            transpose_x(2, 0)
            transpose_x(2, 1)
            project1()
            attention(1)
            rest_of_half0(1)
            half1(1)
            route(1)
            experts(1)

        @block.scalar
        def _(act):
            A = nc.scalar.activation

            def square_sums(n):
                for t in range(T):
                    if n == 0:
                        act.wait_ge(x_loaded[t], 16)
                    else:
                        act.wait_ge(xr[n][t], 2)
                    A((junk_late if n in (2, 4) else junk)[t], xs[:, t, :], ACT.Square, accum_out=ss[:, t:t + 1]).then_inc(ss_ready, 1)
                    if n in (1, 3):
                        act.wait_ge(xT_ready, 4 * n + 2 * t + 2)
                        nc.scalar.copy(hT[:, 4:8, P * t:P * t + P],
                                       ps[2 * t + 1][:, :].rearrange("p (c s) -> p c s", c=4)
                                       ).then_inc(xT_act[n // 2], 1)
                    act.wait_ge(rec_ready, 2 * n + t + 1)
                    A(rstd[:, t:t + 1], ms[:, t:t + 1], ACT.Sqrt).then_inc(rstd_ready, 1)

            def project0():
                for what, i in proj0:
                    if what == "z" and i in v_items:
                        n, t = divmod(i, T)
                        act.wait_ge(z_ready, i + 1)
                        A(vh[:, t, 512 * (n // 5):512 * (n // 5) + 512], ps[4 + i % 4][:, :], ACT.Identity,
                          scale=rstd[:, t:t + 1]).then_inc(v_ready, 1)
                    elif what == "T":
                        n, t = divmod(rope_items[i], T)
                        act.wait_ge(zrT_ready, i + 1)
                        b0 = 4 * (n // 3)
                        src = ps[i % 2][:, :].rearrange("p (b s) -> p b s", b=4)
                        if n % 3 == 0:
                            nc.scalar.copy(qT0[:, b0:b0 + 4, P * t:P * t + P], src).then_inc(qk_evac, 1)
                        else:
                            act.wait_ge(kzero, 1)
                            nc.scalar.copy(kP0[0:64, b0:b0 + 4, 0, P * t:P * t + P], src[0:64])
                            nc.scalar.copy(kP0[64:128, b0:b0 + 4, 1, P * t:P * t + P], src[64:128]
                                           ).then_inc(qk_evac, 1)

            def attention(l):
                for s in range(NSTEP + 4):
                    if s < NSTEP:
                        act.wait_ge(m_ready, NSTEP * l + s + 1)
                        k = s % 4
                        A(prob[k][:, 0:P], prob[k][:, 0:P], ACT.Exp, bias=nm[:, k, 0:1], scale=SCALE[l],
                          accum_out=sm[:, k, 0:1])
                        A(prob[k][:, P:3 * P], prob[k][:, P:3 * P], ACT.Exp, bias=nm[:, k, 1:2], scale=SCALE[l],
                          accum_out=sm[:, k, 1:2]).then_inc(e_ready, 1)
                    u = unit(l, s - 2)
                    if u is not None:
                        act.wait_ge(pT_ready, 12 * l + u + 1)
                        buf, used = buffer_of(l, u)
                        if used >= 1:
                            act.wait_ge(pv_done, 12 * l + used)
                        nc.scalar.copy(probT[buf], ps[6 + u % 2][:, 0:3 * P]).then_inc(pT_evac, 1)
                    u = unit(l, s - 4)
                    if u is not None and diff(l, s - 4):
                        if u % 2:
                            b = (u - 8) // 2
                            act.wait_ge(pv_done, 12 * l + u + 1)
                            if b:
                                act.wait_ge(sso_ready, b)
                            for j in range(4):
                                m = A(tmp_sin[:, P * j:P * j + P], ps[2 + b][:, P * j:P * j + P], ACT.Square,
                                      accum_out=sso[:, 4 * b + j:4 * b + j + 1])
                            m.then_inc(sso_ready, 1)
                    elif u is not None and u % 2:
                        act.wait_ge(pv_done, 12 * l + u + 1)
                        nc.scalar.copy(oT[:, u // 2, :], ps[u // 2 % 2][:, 0:S]).then_inc(oT_evac, 1)

            def project1():
                act.wait_ge(rstd_ready, 2 * 2 + T)
                for t in range(T):
                    act.wait_ge(z1_ready, t + 1)
                    A(z1[:, t, :], ps[4 + t][:, 0:ODN], ACT.Identity, scale=rstd[:, t:t + 1]).then_inc(z1_sb, 1)
                    act.wait_ge(z1_sb, t + 1)
                    j1 = (tmp_cos, tmp_sin)[t]
                    A(j1[:, 0:QR], z1[:, t, 0:QR], ACT.Square, accum_out=ss1[:, t, 0:1])
                    A(j1[:, QR:QR + KR], z1[:, t, QR:QR + KR], ACT.Square, accum_out=ss1[:, t, 1:2]
                      ).then_inc(ss1_ready, 1)
                act.wait_ge(ms1_ready, 1)
                A(rs1, ms1, ACT.Sqrt).then_inc(rs1_ready, 1)
                act.wait_ge(cT_ready, 1)
                nc.scalar.copy(krT[NOPE:QH, :], ps[7][NOPE:QH, S:2 * S]).then_inc(cT_evac, 1)
                for c in range(2):
                    A(cqT[:, c, :], ps[6][:, S * c:S * c + S], ACT.Identity, scale=gq[:, c:c + 1])
                A(ckvT, ps[7][:, 0:S], ACT.Identity, scale=gkv[:, 0:1]).then_inc(cT_evac, 1)
                for what, i in proj1:
                    if what == "T":
                        g, t = divmod(i, T)
                        act.wait_ge(qrT_ready, i + 1)
                        nc.scalar.copy(qT1[0:QH, 4 * g:4 * g + 4, P * t:P * t + P],
                                       ps[4 + i % 2][0:QH, :].rearrange("p (b s) -> p b s", b=4)
                                       ).then_inc(qT_evac, 1)
                    elif what != "q":
                        b = ps[mm1.index((what, i)) % 4]
                        act.wait_ge(kvmm_ready, kv_list.index((what, i)) + 1)
                        if what == "v":
                            n, t = divmod(i, T)
                            nc.scalar.copy(vh[:, t, 512 * n:512 * n + 512], b[:, :]).then_inc(kv_evac, 1)
                        else:
                            nc.scalar.copy(kT1[0:NOPE, 2 * i:2 * i + 2, :].rearrange("p h s -> p (h s)"),
                                           b[0:NOPE, :]).then_inc(kv_evac, 1)

            def route(l):
                act.wait_ge(gmax_ready[l], 1)
                A(lgg[:, :], lgg[:, :], ACT.Exp).then_inc(gexp[l], 1)
                act.wait_ge(emax_ready[l], 1)
                A(ex2, ex2, ACT.Exp).then_inc(eexp[l], 1)

            def experts(l):
                act.wait_ge(bounds_ready[l], 1)
                with act.Fori(0, QUARTS // 2) as i:
                    for half in range(2):
                        q = 2 * i + half
                        first, end = jobs_of(act, l, q)
                        with act.Fori(first, end) as job:
                            act.wait_ge(xg_ready[l][0], job + 1)
                            nc.scalar.copy(xgT[:, 0:4, :].rearrange("p c s -> p (c s)"), ps[4][:, :]
                                           ).then_inc(xgT_a[l], 1)
                            act.wait_ge(a_done[l], job + 1)
                            A(sil, ps[6][:, 0:FF], ACT.Silu).then_inc(silu_done[l], 1)
                            act.wait_ge(hidT_ready[l], job + 1)
                            nc.scalar.copy(hidT[:, :, :].rearrange("p c s -> p (c s)"), ps[7][:, 0:256]
                                           ).then_inc(hidT_sb[l], 1)
                            act.wait_ge(b_half[l], job + 1)
                            nc.scalar.copy(ysb[:, 0:512], ps[4][:, :]).then_inc(y_a[l], 1)
                jobs = act.value_load(bounds[0:1, l, QUARTS:QUARTS + 1], min_val=1, max_val=8 * QUARTS)
                act.wait_ge(comb0_done[l], jobs)
                for n in range(2):
                    nc.scalar.copy(xs[:, 0, 512 * n:512 * n + 512], ps[n][:, :]).then_inc(xr[2 * l + 2][0], 1)

            def small(dst, src, **kw):
                act.dma_start(dst, src, **kw).then_inc(smalls_loaded, 16)

            act.dma_start(gcol[:, 0::2, :], attn_norm.rearrange("l (p c) -> p l c", c=C)).then_inc(gcol_loaded, 16)
            for dst, src in ((gcol[:, 1::2, :], ffn_norm.rearrange("l (p c) -> p l c", c=C)),
                             (rope[:, :, :], rope_tab.rearrange("(t p) f -> p t f", p=P))):
                act.dma_start(dst, src).then_inc(early_loaded, 16)
            load_router(act, 0)
            for k, v in enumerate((ev_lambda_q1, ev_lambda_k1, ev_lambda_q2, ev_lambda_k2)):
                small(lamv[:, k, :], v[0].partition_broadcast(P))
            small(gsub[:, :], ev_subln.rearrange("a p -> p a"), allow_slow_non_contiguous=True)
            small(gq[:, :], od_q_norm[0].rearrange("(c p) -> p c", p=P), allow_slow_non_contiguous=True)
            small(gkv[:, :], od_kv_norm.rearrange("a p -> p a"), allow_slow_non_contiguous=True)
            for l in L2:
                small(br[:, l, 0:NG], moe_b_group[l].partition_broadcast(P))
                small(br[:, l, NG:], moe_b_expert[l].partition_broadcast(P))

            square_sums(0)
            act.wait_ge(lam_sum, 1)
            A(lexp, lsum, ACT.Exp).then_inc(lam_exp, 1)
            project0()
            attention(0)
            act.wait_ge(mso_ready, 1)
            A(rso, mso, ACT.Sqrt).then_inc(rso_ready, 1)
            for b in range(2):
                act.wait_ge(onT_ready, b + 1)
                A(oT[:, 4 + 2 * b:6 + 2 * b, :].rearrange("p h s -> p (h s)"), ps[4 + b][:, :], ACT.Identity,
                  scale=gsub[:, 0:1]).then_inc(oT_evac, 1)
            square_sums(1)
            route(0)
            experts(0)
            square_sums(2)
            project1()
            attention(1)
            square_sums(3)
            route(1)
            experts(1)
            square_sums(4)

        @block.vector
        def _(dve):
            V = nc.vector
            links = [0]

            def link(ins):
                links[0] += 1
                ins.then_inc(chain, 1)
                dve.wait_ge(chain, links[0])

            def norm(n):
                if n == 0:
                    dve.wait_ge(gcol_loaded, 16)
                for t in range(T):
                    norm_tile(n, t)

            def norm_tile(n, t):
                if n in (0, 2):
                    for h in range(2):
                        dve.wait_ge(xT_ready, 4 * n + 2 * t + h + 1)
                        V.tensor_tensor(hT[:, 4 * h:4 * h + 4, P * t:P * t + P],
                                        ps[2 * t + h][:, :].rearrange("p (c s) -> p c s", c=4),
                                        bc(gcol[:, n, 4 * h:4 * h + 4], [P, 4, P], [2]), ALU.mult
                                        ).then_inc(hT_ready, 1)
                if n in (1, 3):
                    dve.wait_ge(xT_ready, 4 * n + 2 * t + 1)
                    V.tensor_copy(hT[:, 0:4, P * t:P * t + P],
                                  ps[2 * t][:, :].rearrange("p (c s) -> p c s", c=4)).then_inc(hT_ready, 1)
                dve.wait_ge(ss_ready, 2 * n + t + 1)
                link(V.tensor_scalar(ms[:, t:t + 1], ss[:, t:t + 1], 1.0 / D, EPS, ALU.mult, ALU.add))
                V.reciprocal(ms[:, t:t + 1], ms[:, t:t + 1]).then_inc(rec_ready, 1)

            def for_router(l, t):
                n = 2 * l + 1
                norm_tile(n, t)
                dve.wait_ge(rstd_ready, 2 * n + t + 1)
                if t == 0:
                    dve.wait_ge(gain_loaded, 16 * (l + 1))
                V.scalar_tensor_tensor(hp[:, t, :].rearrange("s (c p) -> s p c", c=C),
                                       xs[:, t, :].rearrange("s (p c) -> s p c", c=C), rstd[:, t:t + 1],
                                       gain[:, :].rearrange("s (p c) -> s p c", c=C), ALU.mult, ALU.mult
                                       ).then_inc(hp_ready[l], 1)

            def rotate(dst, src, cos, sin, width, h):
                a = tmp_cos[:, 0:width].rearrange("p (n k h) -> p n k h", k=2, h=h)
                b = tmp_sin[:, 0:width].rearrange("p (n k h) -> p n k h", k=2, h=h)
                V.tensor_tensor(a, src, cos, ALU.mult)
                link(V.tensor_tensor(b, src, sin, ALU.mult))
                V.tensor_tensor(dst[:, :, 0, :], a[:, :, 0, :], b[:, :, 1, :], ALU.subtract)
                return V.tensor_tensor(dst[:, :, 1, :], a[:, :, 1, :], b[:, :, 0, :], ALU.add)

            def project0():
                dve.wait_ge(rstd_ready, T)
                dve.wait_ge(early_loaded, 16 * 2)
                for t in range(T):
                    i = V.tensor_scalar(rope0[:, t, :, :].rearrange("p k h -> p (k h)"), rope[:, t, 0:2 * HALF],
                                        rstd[:, t:t + 1], None, ALU.mult)
                link(i)
                for r, i in enumerate(rope_items):
                    t = i % T
                    dve.wait_ge(z_ready, i + 1)
                    if r >= 2:
                        dve.wait_ge(zrT_ready, r - 1)
                    if r >= 1:
                        dve.wait_ge(z_roped, r)
                    src = ps[4 + i % 4][:, :].rearrange("p (m h) -> p m h", h=HALF)
                    a = tmp_cos.rearrange("p (m h) -> p m h", h=HALF)
                    b = tmp_sin.rearrange("p (m h) -> p m h", h=HALF)
                    V.tensor_tensor(a, src, bc(rope0[:, t, 0, :], [P, 16, HALF], [1]), ALU.mult)
                    link(V.tensor_tensor(b, src, bc(rope0[:, t, 1, :], [P, 16, HALF], [1]), ALU.mult))
                    d = rot[r % 2].rearrange("p (n k h) -> p n k h", k=2, h=HALF)
                    a = tmp_cos.rearrange("p (n k h) -> p n k h", k=2, h=HALF)
                    b = tmp_sin.rearrange("p (n k h) -> p n k h", k=2, h=HALF)
                    V.tensor_tensor(d[:, :, 0, :], a[:, :, 0, :], b[:, :, 1, :], ALU.subtract)
                    V.tensor_tensor(d[:, :, 1, :], a[:, :, 1, :], b[:, :, 0, :], ALU.add).then_inc(z_roped, 1)

            def attention(l):
                for s in range(NSTEP + 1):
                    if s < NSTEP:
                        k = s % 4
                        dve.wait_ge(s_ready, NSTEP * l + s + 1)
                        if s == 0:
                            if l == 0:
                                dve.wait_ge(zrT_ready, 8)
                            else:
                                dve.wait_ge(qrT_ready, 8)
                                dve.wait_ge(ss1_ready, 2)
                        if s >= 4:
                            u4 = unit(l, s - 4)
                            dve.wait_ge(pT_ready, 12 * l + (u4 if u4 is not None else unit(l, s - 3)) + 1)
                        V.tensor_tensor_reduce(prob[k][:, 0:P], ps[4 + s % 2][:, 0:P], mask[:, P:2 * P], 1.0, -3.0 * BIG,
                                               ALU.add, ALU.max, mx[:, k, 0:1])
                        link(V.tensor_tensor_reduce(prob[k][:, P:3 * P], ps[4 + s % 2][:, P:3 * P], mask[:, 0:2 * P],
                                                    1.0, -3.0 * BIG, ALU.add, ALU.max, mx[:, k, 1:2]))
                        V.tensor_scalar(nm[:, k, :], mx[:, k, :], -SCALE[l], None, ALU.mult).then_inc(m_ready, 1)
                    if s >= 1:
                        j = s - 1
                        k = j % 4
                        dve.wait_ge(e_ready, NSTEP * l + j + 1)
                        link(V.reciprocal(rs[:, k, :], sm[:, k, :]))
                        if diff(l, j) and j % 2:
                            link(V.tensor_scalar(rs[:, k, :], rs[:, k, :], nlam, None, ALU.mult))
                            k0 = (j - 1) % 4
                            V.scalar_tensor_tensor(prob[k0][:, 0:P], prob[k][:, 0:P], rs[:, k, 0:1],
                                                   prob[k0][:, 0:P], ALU.mult, ALU.add)
                            V.scalar_tensor_tensor(prob[k0][:, P:3 * P], prob[k][:, P:3 * P], rs[:, k, 1:2],
                                                   prob[k0][:, P:3 * P], ALU.mult, ALU.add).then_inc(p_ready, 1)
                        else:
                            V.tensor_scalar(prob[k][:, 0:P], prob[k][:, 0:P], rs[:, k, 0:1], None, ALU.mult)
                            i = V.tensor_scalar(prob[k][:, P:3 * P], prob[k][:, P:3 * P], rs[:, k, 1:2], None,
                                                ALU.mult)
                            if diff(l, j):
                                link(i)
                            else:
                                i.then_inc(p_ready, 1)

            def add_residual(l):
                for t in range(T):
                    for n in range(2):
                        dve.wait_ge(wo_ready, 4 * l + 2 * t + n + 1)
                        v = xs[:, t, 512 * n:512 * n + 512]
                        V.tensor_tensor(v, v, ps[WO_BANK[l][2 * t + n]][:, :], ALU.add).then_inc(xr[2 * l + 1][t], 1)
                        if (t, n) == (1, 0):
                            for_router(l, 0)
                for_router(l, 1)

            def project1():
                dve.wait_ge(ss1_ready, 2)
                V.tensor_scalar(ms1[:, :, 0], ss1[:, :, 0], 1.0 / QR, EPS, ALU.mult, ALU.add)
                link(V.tensor_scalar(ms1[:, :, 1], ss1[:, :, 1], 1.0 / KR, EPS, ALU.mult, ALU.add))
                V.reciprocal(ms1, ms1).then_inc(ms1_ready, 1)
                link(V.memset(kr_in, 0.0))
                z = z1[:, :, QR + KR:].rearrange("p t (k h) -> p t k h", k=2)
                cos = bc(rope[:, :, 64:80], [P, T, 2, RR // 2], [2])
                sin = bc(rope[:, :, 80:96], [P, T, 2, RR // 2], [2])
                rotate(kr_in[:, :, NOPE:].rearrange("p t (k h) -> p t k h", k=2), z, cos, sin, T * RR, RR // 2)
                dve.wait_ge(rs1_ready, 1)
                for t in range(T):
                    V.tensor_scalar(z1[:, t, 0:QR], z1[:, t, 0:QR], rs1[:, t, 0:1], None, ALU.mult)
                    i = V.tensor_scalar(z1[:, t, QR:QR + KR], z1[:, t, QR:QR + KR], rs1[:, t, 1:2], None, ALU.mult)
                i.then_inc(zn_ready, 1)
                for i in range(8):
                    t = i % T
                    b = ps[mm1.index(("q", i)) % 4][:, 0:4 * QH].rearrange("p (h d) -> p h d", h=4)
                    d = rot[i % 2][:, 0:4 * QH].rearrange("p (h d) -> p h d", h=4)
                    dve.wait_ge(qmm_ready, i + 1)
                    if i >= 2:
                        dve.wait_ge(qrT_ready, i - 1)
                    if i >= 1:
                        dve.wait_ge(q_roped, i)
                    else:
                        dve.wait_ge(zn_ready, 1)
                    V.tensor_copy(d[:, :, 0:NOPE], b[:, :, 0:NOPE])
                    cos = bc(rope[:, t, 64:80], [P, 4, 2, RR // 2], [1, 1])
                    sin = bc(rope[:, t, 80:96], [P, 4, 2, RR // 2], [1, 1])
                    rotate(d[:, :, NOPE:].rearrange("p h (k e) -> p h k e", k=2),
                           b[:, :, NOPE:].rearrange("p h (k e) -> p h k e", k=2), cos, sin, 4 * RR, RR // 2
                           ).then_inc(q_roped, 1)

            def route(l):
                for t in range(T):
                    dve.wait_ge(lg_ready[l], t + 1)
                    V.scalar_tensor_tensor(lgp[:, t, 0:NG], ps[4 + t][:, 0:NG], rstd[:, t:t + 1],
                                           br[:, l, 0:NG], ALU.mult, ALU.add)
                    i = V.scalar_tensor_tensor(lg[:, t, :], ps[4 + t][:, NG:NG + NE], rstd[:, t:t + 1],
                                               br[:, l, NG:], ALU.mult, ALU.add)
                link(i)
                for t in range(T):
                    i = V.max(top[:, 0, t, :], lgp[:, t, :])
                link(i)
                for t in range(T):
                    V.max_index(where[:, 0, t, :], top[:, 0, t, :], lgp[:, t, :])
                link(V.tensor_tensor(lgg, lgp[:, :, 0:NG], bc(top[:, 0, :, 0], [P, T, NG], [2]), ALU.subtract))
                V.tensor_tensor(other, bc(idx[:, 0:NG], [P, T, NG], [1]), where[:, 0, :, 0:1].to_broadcast([P, T, NG]),
                                ALU.not_equal).then_inc(gmax_ready[l], 1)
                dve.wait_ge(gmax_ready[l], 1)
                for t in range(T):
                    i = V.scalar_tensor_tensor(lge[:, t, :].rearrange("p (g e) -> p g e", g=NG),
                                               bc(other[:, t, :], [P, NG, EPG], [2]), -BIG,
                                               lg[:, t, :].rearrange("p (g e) -> p g e", g=NG), ALU.mult, ALU.add)
                link(i)
                for t in range(T):
                    i = V.max(top[:, 1, t, :], lge[:, t, :])
                link(i)
                for t in range(T):
                    i = V.max_index(where[:, 1, t, :], top[:, 1, t, :], lge[:, t, :])
                link(i)
                V.tensor_tensor(ex2, top[:, 1, :, 1], top[:, 1, :, 0], ALU.subtract).then_inc(emax_ready[l], 1)
                link(V.tensor_tensor(best, bc(idx[:, :], [P, T, 2, NE], [1, 1]), bc(where[:, 1, :, 0:2], [P, T, 2, NE], [3]),
                                     ALU.is_equal))
                V.tensor_tensor(routed, best[:, :, 0, :], best[:, :, 1, :], ALU.add).then_inc(routed_ready[l], 1)
                E3 = [P, T, NE]
                dve.wait_ge(gexp[l], 1)
                link(V.tensor_reduce(gs_, lgg, AX.X, ALU.add))
                dve.wait_ge(eexp[l], 1)
                link(V.tensor_scalar(den, ex2, 1.0, None, ALU.add))
                link(V.tensor_tensor(den, den, gs_, ALU.mult))
                link(V.reciprocal(w1, den))
                link(V.tensor_tensor(w2, w1, ex2, ALU.mult))
                V.tensor_tensor(gate, best[:, :, 0, :], bc(w1, E3, [2]), ALU.mult)
                link(V.tensor_tensor(second, best[:, :, 1, :], bc(w2, E3, [2]), ALU.mult))
                link(V.tensor_tensor(gate, gate, second, ALU.add))
                dve.wait_ge(pos_ready[l], 1)
                link(V.tensor_reduce(cmax, ps[5][0:1, 2 * NE:3 * NE].rearrange("p (q e) -> p q e", e=LANES), AX.X,
                                     ALU.max))
                link(V.tensor_tensor(exceeds, bc(cmax, [1, QUARTS, 8], [2]), thr[:, :, :], ALU.is_gt))
                link(V.tensor_reduce(rnd, exceeds, AX.X, ALU.add))
                link(V.tensor_tensor(cnt_ge[:, :, :], before[:, :, :], bc(rnd, [1, QUARTS + 1, QUARTS], [1]), ALU.mult))
                with nc.allow_low_precision(reason="sums of small whole numbers"):
                    V.tensor_reduce(bounds[:, l, 0:QUARTS + 1], cnt_ge[:, :, :], AX.X, ALU.add
                                    ).then_inc(bounds_ready[l], 1)
                link(V.scalar_tensor_tensor(pos, ps[5][:, 0:2 * NE].rearrange("p (t e) -> p t e", t=T), 1.0, routed,
                                            ALU.add, ALU.mult))

            def experts(l):
                dve.wait_ge(bounds_ready[l], 1)
                with dve.Fori(0, QUARTS // 2) as i:
                    for half in range(2):
                        q = 2 * i + half
                        first, end = jobs_of(dve, l, q)
                        lanes = bass.ds(q * LANES, LANES)
                        with dve.Fori(first, end) as job:
                            for t in range(T):
                                m = V.tensor_tensor(pick[:, t], bc(idx1[:, 0:SLOTS], [P, LANES, SLOTS], [1]),
                                                    bc(pos[:, t, lanes], [P, LANES, SLOTS], [2]), ALU.is_equal)
                            m.then_inc(pick_made[l], 1)
                            dve.wait_ge(pick_made[l], job + 1)
                            for t in range(T):
                                m = V.tensor_tensor(pickg[:, t], pick[:, t], bc(gate[:, t, lanes], [P, LANES, SLOTS], [2]),
                                                    ALU.mult)
                            m.then_inc(pick_ready[l], 1)
                            V.tensor_scalar(pos[:, :, lanes], pos[:, :, lanes], -float(SLOTS), None, ALU.add)
                            dve.wait_ge(xg_ready[l][1], job + 1)
                            V.tensor_copy(xgT[:, 4:8, :].rearrange("p c s -> p (c s)"), ps[5][:, :]).then_inc(xgT_d[l], 1)
                            dve.wait_ge(cT[l], job + 1)
                            V.tensor_copy(comb, ps[7][:, 256:512]).then_inc(comb_sb[l], 1)
                            dve.wait_ge(silu_done[l], job + 1)
                            V.tensor_tensor(hid[:, :, :].rearrange("s c f -> s f c"),
                                            sil.rearrange("s (f c) -> s f c", c=FC),
                                            ps[6][:, FF:2 * FF].rearrange("s (f c) -> s f c", c=FC), ALU.mult
                                            ).then_inc(hid_ready[l], 1)
                            dve.wait_ge(b_done[l], job + 1)
                            V.tensor_copy(ysb[:, 512:1024], ps[5][:, :]).then_inc(y_d[l], 1)
                            dve.wait_ge(y_d[l], job + 1)
                jobs = dve.value_load(bounds[0:1, l, QUARTS:QUARTS + 1], min_val=1, max_val=8 * QUARTS)
                dve.wait_ge(comb_done[l], jobs)
                for n in range(2):
                    V.tensor_copy(xs[:, 1, 512 * n:512 * n + 512], ps[2 + n][:, :]).then_inc(xr[2 * l + 2][1], 1)

            link(V.memset(lgp, -BIG))
            norm(0)
            dve.wait_ge(smalls_loaded, 16 * SMALLS)
            for k in range(2):
                V.tensor_tensor_reduce(lamv[:, 2 * k, :], lamv[:, 2 * k, :], lamv[:, 2 * k + 1, :], 1.0, 0.0, ALU.mult,
                                       ALU.add, lsum[:, k:k + 1])
            V.tensor_scalar(gsub[:, :], gsub[:, :], 1.0 - LAM_INIT, None, ALU.mult).then_inc(lam_sum, 1)
            dve.wait_ge(lam_exp, 1)
            link(V.tensor_tensor(nlam, lexp[:, 1:2], lexp[:, 0:1], ALU.subtract))
            link(V.tensor_scalar(nlam, nlam, -LAM_INIT, None, ALU.add))
            dve.wait_ge(consts, 1)
            project0()
            attention(0)
            dve.wait_ge(sso_ready, 2)
            link(V.tensor_scalar(mso, sso, 1.0 / DV, EPS, ALU.mult, ALU.add))
            V.reciprocal(mso, mso).then_inc(mso_ready, 1)
            dve.wait_ge(rso_ready, 1)
            dve.wait_ge(pT_ready, 12)
            for b in range(2):
                V.tensor_tensor(on[:, 512 * b:512 * b + 512].rearrange("p (i d) -> p i d", i=4),
                                ps[2 + b][:, :].rearrange("p (i d) -> p i d", i=4),
                                bc(rso[:, 4 * b:4 * b + 4], [P, 4, DV], [2]), ALU.mult).then_inc(on_ready, 1)
            add_residual(0)
            route(0)
            experts(0)
            norm(2)
            project1()
            attention(1)
            add_residual(1)
            route(1)
            experts(1)
            norm(4)
            dve.wait_ge(gain_loaded, 16 * 3)
            for t in range(T):
                dve.wait_ge(rstd_ready, 2 * 4 + t + 1)
                V.scalar_tensor_tensor(xs[:, t, :], xs[:, t, :], rstd[:, t:t + 1], gain[:, :], ALU.mult, ALU.mult
                                       ).then_inc(y_out, 1)


_INS = ["x", "attn_norm", "ev_w_in", "ev_lambda_q1", "ev_lambda_k1", "ev_lambda_q2", "ev_lambda_k2", "ev_subln",
        "ev_w_out", "od_w_in", "od_q_norm", "od_kv_norm", "od_w_q_up", "od_w_kv_up", "od_w_out", "ffn_norm",
        "moe_w_group", "moe_b_group", "moe_w_expert", "moe_b_expert", "moe_w_gate", "moe_w_up", "moe_w_down",
        "final_norm"]


def kernel(**inputs):
    import numpy as np
    import concourse.bacc as bacc
    from concourse.bass_utils import run_bass_kernel_spmd

    seq = inputs["x"].shape[1]
    pos = np.arange(seq, dtype=np.float32)[:, None]
    cols = []
    for dim in (64, 32):
        inv = (1.0 / (10000.0 ** (np.arange(0, dim, 2, dtype=np.float32) / dim))).astype(np.float32)
        ang = pos * inv[None, :]
        cols += [np.cos(ang), np.sin(ang)]
    tab = np.concatenate(cols, axis=1).astype(np.float32)

    nc = bacc.Bacc("TRN2", target_bir_lowering=False, num_devices=1)
    arrays, args = {}, []
    for name in _INS:
        a = np.ascontiguousarray(inputs[name])
        arrays[f"in_{name}"] = a
        args.append(nc.dram_tensor(f"in_{name}", a.shape, mybir.dt.from_np(a.dtype), kind="ExternalInput").ap())
    arrays["rope_tab"] = tab
    args.append(nc.dram_tensor("rope_tab", tab.shape, F32, kind="ExternalInput").ap())
    args.append(nc.dram_tensor("out_y", tuple(inputs["x"].shape), F32, kind="ExternalOutput").ap())
    trunk(nc, *args)
    r = run_bass_kernel_spmd(nc, [arrays], core_ids=[0])
    return r.results[0]["out_y"]
```

```python
import math
from contextlib import ExitStack

import concourse.bass as bass
from concourse import mybir

F32 = mybir.dt.float32
I32 = mybir.dt.int32
U32 = mybir.dt.uint32
ALU = mybir.AluOpType
ACT = mybir.ActivationFunctionType
AX = mybir.AxisListType

P = 128
EPS = 1e-6
BIG = 1e30
SLOTS = 32
LANES = 4
PLACES = 5


def trunk(nc, x, attn_norm, ev_w_in, ev_lambda_q1, ev_lambda_k1, ev_lambda_q2, ev_lambda_k2, ev_subln, ev_w_out,
          od_w_in, od_q_norm, od_kv_norm, od_w_q_up, od_w_kv_up, od_w_out, ffn_norm, moe_w_group, moe_b_group,
          moe_w_expert, moe_b_expert, moe_w_gate, moe_w_up, moe_w_down, final_norm, rope_tab, out):
    _, S, D = x.shape
    T = S // P
    C = D // P
    LAYERS = attn_norm.shape[0]
    NG = moe_w_group.shape[2]
    NE = moe_w_expert.shape[2]
    EPG = NE // NG
    FF = moe_w_gate.shape[3]
    FC = FF // P
    QUARTS = NE // LANES
    HD = ev_lambda_q1.shape[1]
    HALF = HD // 2
    DV = ev_subln.shape[1]
    DH = ev_w_in.shape[2] // 512
    QR, KR = od_q_norm.shape[1], od_kv_norm.shape[1]
    ODN = od_w_in.shape[2]
    RR = ODN - QR - KR
    NH1 = 16
    QH = od_w_q_up.shape[2] // NH1
    NOPE = QH - RR
    LAM_INIT = 0.8 - 0.6 * math.exp(-0.3 * 0)
    SCALE = [HD ** -0.5, QH ** -0.5]
    assert T == 2 and C == 8 and FC == 2 and DH == 6 and QH == 96 and NE * 8 == S

    ctx = ExitStack()
    with ctx:
        def sb(name, shape, dt=F32):
            return ctx.enter_context(nc.sbuf_tensor(name, shape, dt))

        def sem(name):
            return ctx.enter_context(nc.semaphore(name))

        ps = [ctx.enter_context(nc.psum_tensor(f"ps{i}", [P, 512], F32)) for i in range(8)]

        UNIT = 2 * 2 * C * FF
        MAX_ROUNDS = S // SLOTS
        assert UNIT == LANES * FC * D
        weights = sb("weights", [P, PLACES, UNIT])
        w_gu = weights[:, :, :].rearrange("p s (e k c f) -> p s e k c f", e=2, k=2, c=C)
        w_dn = weights[:, :, :].rearrange("p s (e c n) -> p s e c n", e=LANES, c=FC)
        GU_AT = [[0, 1], [3, 4]]
        DN_AT = 2

        stream_raw = [weights[:, 3, UNIT // 2 * h:UNIT // 2 * (h + 1)] for h in range(2)]
        qk_raw = weights[:, 4, :]
        kv_up_raw = weights[:, DN_AT, 0:P * NH1]
        qT0 = qk_raw[:, 0:8 * S].rearrange("p (b s) -> p b s", b=8)
        kP0 = qk_raw[:, 8 * S:24 * S].rearrange("p (b r s) -> p b r s", b=8, r=2)
        qT1 = qk_raw[:, 0:NH1 * S].rearrange("p (h s) -> p h s", h=NH1)
        kT1 = qk_raw[:, NH1 * S:2 * NH1 * S].rearrange("p (h s) -> p h s", h=NH1)

        xs = sb("xs", [P, T, D])
        hT = sb("hT", [P, C, S])
        oT = hT
        vh = sb("vh", [P, T, D])
        hp = vh
        scr = sb("scr", [P, 3072])
        rot = [scr[:, 512 * i:512 * i + 512] for i in range(2)]
        tmp_cos, tmp_sin = scr[:, 1024:1536], scr[:, 1536:2048]
        prob = [scr[:, 384 * i:384 * i + 384] for i in range(4)]
        probT = [scr[:, 2048:2432], scr[:, 2432:2816], scr[:, 1536:1920]]
        junk = [scr[:, D * t:D * t + D] for t in range(T)]
        junk_late = [scr[:, 2 * D:3 * D], junk[1]]
        junk_final = [scr[:, 512 * i:512 * i + 512] for i in (4, 5, 2, 0)]
        on = scr[:, 0:D]
        z1 = scr[:, 2048:2048 + T * ODN].rearrange("p (t n) -> p t n", t=T)
        xgT = scr[:, 0:C * P].rearrange("p (c s) -> p c s", c=C)
        ysb = scr[:, 0:D]
        hid = scr[:, 1024:1280].rearrange("p (c f) -> p c f", c=FC)
        hidT_kept = hT[:, :, :].rearrange("p c s -> p (c s)").rearrange("p (r n) -> p r n", r=MAX_ROUNDS)
        hidT = scr[:, 1280:1536].rearrange("p (c s) -> p c s", c=FC)
        comb = scr[:, 1536:1792]
        pick = scr[:, 1792:2048].rearrange("p (t e s) -> p t e s", t=T, e=LANES)
        sil = scr[:, 2368:2624]
        pickg = scr[:, 2048:2304].rearrange("p (t e s) -> p t e s", t=T, e=LANES)
        kr_in = scr[:, 2880:3072].rearrange("p (t n) -> p t n", t=T)
        lamv = scr[:, 2816:3072].rearrange("p (k n) -> p k n", k=4)

        gain = sb("gain", [P, D])
        lat = gain
        cqT = lat[:, 0:2 * S].rearrange("p (c s) -> p c s", c=2)
        ckvT = lat[:, 2 * S:3 * S]
        krT = lat[:, 3 * S:4 * S]
        mask = sb("mask", [P, 2 * P])
        ident = sb("ident", [P, P])
        tri = sb("tri", [P, P])
        ones = sb("ones", [P, P])
        wr = sb("wr", [P, C, NG + NE])
        br = sb("br", [P, LAYERS, NG + NE])
        gcol = sb("gcol", [P, 2 * LAYERS, C])
        rope = sb("rope", [P, T, 96])
        rope0 = sb("rope0", [P, T, 2, HALF])
        SMALLS = 4 + 3 + 2 * LAYERS
        gsub = sb("gsub", [P, 1])
        gq = sb("gq", [P, 2])
        gkv = sb("gkv", [P, 1])
        idx = sb("idx", [P, NE])
        idx1 = sb("idx1", [P, NE])
        thr = sb("thr", [1, QUARTS, 8])
        before = sb("before", [1, QUARTS + 1, QUARTS])
        bounds = sb("bounds", [1, LAYERS, QUARTS + 2], I32)
        st = sb("st", [P, 144])
        ss, ms, rstd = st[:, 0:2], st[:, 2:4], st[:, 4:6]
        mx = st[:, 8:16].rearrange("p (u t) -> p u t", t=2)
        nm = st[:, 16:24].rearrange("p (u t) -> p u t", t=2)
        sm = st[:, 24:32].rearrange("p (u t) -> p u t", t=2)
        rs = st[:, 32:40].rearrange("p (u t) -> p u t", t=2)
        nlam = st[:, 40:41]
        lsum = st[:, 42:44]
        lexp = st[:, 44:46]
        sso, mso, rso = st[:, 48:56], st[:, 56:64], st[:, 64:72]
        ss1 = st[:, 72:76].rearrange("p (t k) -> p t k", t=T)
        ms1 = st[:, 76:80].rearrange("p (t k) -> p t k", t=T)
        rs1 = st[:, 80:84].rearrange("p (t k) -> p t k", t=T)
        spare = st[:, 104:105]
        ssf = st[:, 106:110].rearrange("p (t n) -> p t n", t=T)
        cmax, rnd = st[0:1, 88:96], st[0:1, 96:104]
        gs_ = st[:, 118:120]
        ex2, den, w1, w2 = st[:, 126:128], st[:, 128:130], st[:, 130:132], st[:, 132:134]
        rt = scr[:, 1024:1024 + 6 * T * NE]
        lg, lge, routed, second = (rt[:, T * NE * k:T * NE * (k + 1)].rearrange("p (t e) -> p t e", t=T)
                                   for k in range(4))
        best = rt[:, 4 * T * NE:6 * T * NE].rearrange("p (t k e) -> p t k e", t=T, k=2)
        lgp = sb("lgp", [P, T, 8])[:, :, :]
        top = sb("top", [P, 2, T, 8])[:, :, :, :]
        where = sb("where", [P, 2, T, 8], U32)[:, :, :, :]
        lgg = sb("lgg", [P, T, NG])[:, :, :]
        other = sb("other", [P, T, NG])[:, :, :]
        pos = sb("pos", [P, T, NE])[:, :, :]
        pos_d = scr[:, 2304:2304 + T * NE].rearrange("p (t e) -> p t e", t=T)
        gate = sb("gate", [P, T, NE])[:, :, :]
        exceeds = scr[0:1, 1024:1024 + 8 * QUARTS].rearrange("p (q m) -> p q m", m=8)
        cnt_ge = scr[0:1, 1408:1408 + (QUARTS + 1) * QUARTS].rearrange("p (k q) -> p k q", q=QUARTS)

        def bc(ap, shape, axis):
            for a in axis:
                ap = ap.unsqueeze(a)
            return ap.to_broadcast(shape)

        x_loaded = [sem("x0_loaded"), sem("x1_loaded")]
        smalls_loaded, w_in_first = sem("smalls_loaded"), [sem("w_in_first0"), sem("w_in_first1")]
        gcol_loaded = sem("gcol_loaded")
        stream_loaded = [sem("stream_loaded0"), sem("stream_loaded1")]
        gua_loaded = [sem("gate_up_01_loaded_even"), sem("gate_up_01_loaded_odd")]
        gub_loaded = [sem("gate_up_23_loaded_even"), sem("gate_up_23_loaded_odd")]
        dn_loaded = [[sem(f"down_loaded_{x}_{n}") for n in range(2)] for x in ("even", "odd")]
        gain_loaded, wr_loaded, wr_ready = sem("gain_loaded"), sem("wr_loaded"), sem("wr_ready")
        early_loaded = sem("early_loaded")
        consts, kzero, ident_made = sem("consts"), sem("kzero"), sem("ident_made")
        pool_step = sem("pool_step")
        chain = sem("dve_chain")
        N4 = range(2 * LAYERS)
        xr = [[sem(f"x_ready{n}_{t}") for t in range(T)] for n in N4]
        xT_ready = sem("xT_ready")
        hT_ready = sem("hT_ready")
        ss_ready = sem("ss_ready")
        rec_ready = sem("rec_ready")
        rstd_ready = sem("rstd_ready")
        xT_act = [sem(f"xT_act{l}") for l in range(LAYERS)]
        z_ready, z_roped, v_ready = sem("z_ready"), sem("z_roped"), sem("v_ready")
        zrT_ready, qk_evac = sem("zrT_ready"), sem("qk_evac")
        L2 = range(LAYERS)
        s_ready = sem("s_ready")
        m_ready = sem("m_ready")
        e_ready = sem("e_ready")
        p_ready = sem("p_ready")
        pT_ready = sem("pT_ready")
        pT_evac = sem("pT_evac")
        pv_done = sem("pv_done")
        oT_evac = sem("oT_evac")
        sso_ready, mso_ready, rso_ready = sem("sso_ready"), sem("mso_ready"), sem("rso_ready")
        on_ready, onT_ready, lam_sum, lam_exp = sem("on_ready"), sem("onT_ready"), sem("lam_sum"), sem("lam_exp")
        wo_ready = sem("wo_ready")
        z1_ready, z1_sb, ss1_ready = sem("z1_ready"), sem("z1_sb"), sem("ss1_ready")
        ms1_ready, rs1_ready, zn_ready = sem("ms1_ready"), sem("rs1_ready"), sem("zn_ready")
        cT_ready, cT_evac, kr_spread = sem("cT_ready"), sem("cT_evac"), sem("kr_spread")
        kr_evac, kv_up_loaded = sem("kr_evac"), sem("kv_up_loaded")
        qmm_ready, kvmm_ready = sem("qmm_ready"), sem("kvmm_ready")
        q_roped, kv_evac, qrT_ready, qT_evac = sem("q_roped"), sem("kv_evac"), sem("qrT_ready"), sem("qT_evac")
        lg_ready = [sem(f"logits_ready{i}") for i in L2]
        gexp = [sem(f"group_exp{i}") for i in L2]
        eexp = [sem(f"expert_exp{i}") for i in L2]
        gmax_ready = [sem(f"group_max{i}") for i in L2]
        emax_ready = [sem(f"expert_max{i}") for i in L2]
        routed_ready = [sem(f"routed{i}") for i in L2]
        pos_ready = [sem(f"pos_ready{i}") for i in L2]
        hp_ready = [sem(f"hp_ready{i}") for i in L2]
        pos_down = [sem(f"pos_counted_down{i}") for i in L2]
        pos_set, pos_copied = sem("pos_set"), sem("pos_copied")
        bounds_ready = [sem(f"bounds_ready{i}") for i in L2]
        pick_made = [sem(f"pick_made{i}") for i in L2]
        pick_ready = [sem(f"pick_ready{i}") for i in L2]
        pickg_ready = [sem(f"pick_times_gate{i}") for i in L2]
        hid_kept = [sem(f"hidT_kept{i}") for i in L2]
        xg_ready = [[sem(f"xg_ready{i}_{h}") for h in range(2)] for i in L2]
        xgT_a = [sem(f"xgT_act{i}") for i in L2]
        xgT_d = [sem(f"xgT_dve{i}") for i in L2]
        cT = [sem(f"comb_transposed{i}") for i in L2]
        comb_sb = [sem(f"comb_sb{i}") for i in L2]
        a_done = [sem(f"gate_up_done{i}") for i in L2]
        silu_done = [sem(f"silu_done{i}") for i in L2]
        hid_ready = [sem(f"hid_ready{i}") for i in L2]
        hidT_ready = [sem(f"hidT_ready{i}") for i in L2]
        hidT_sb = [sem(f"hidT_sb{i}") for i in L2]
        b_half = [sem(f"down_half{i}") for i in L2]
        b_done = [sem(f"down_done{i}") for i in L2]
        y_a = [sem(f"y_act{i}") for i in L2]
        y_d = [sem(f"y_dve{i}") for i in L2]
        comb0_done = [sem(f"comb_done_tile0_{i}") for i in L2]
        comb_done = [sem(f"comb_done{i}") for i in L2]
        sq_done, gained = sem("final_squares"), sem("times_final_gain")
        y_out, stored = [sem("y_out0"), sem("y_out1")], sem("stored")

        rope_items = [2 * n + t for n in (0, 1, 3, 4) for t in range(T)]
        v_items = [2 * n + t for n in (2, 5) for t in range(T)]
        proj0 = []
        for i in range(2 * DH - 2):
            proj0.append(("z", i))
            if i - 2 in rope_items:
                proj0.append(("T", rope_items.index(i - 2)))
        proj0 += [("T", 6), ("v", range(0, 4)), ("T", 7)]

        def value_products_at(s):
            return range(4 + 2 * s, 6 + 2 * s) if s < 2 else range(6 + s, 7 + s) if s < 10 else range(0)

        proj1 = []
        beside = {1: [("v", 0)], 2: [("v", 2)], 3: [("k", 0)], 4: [("k", 1)], 6: [("k", 2), ("k", 3)]}
        for r in range(8):
            proj1.append(("q", r))
            if r >= 2:
                proj1.append(("T", r - 2))
            if r == 2:
                proj1.append(("latents", 1))
            proj1 += beside.get(r - 1, [])
        proj1 += [("T", 6), ("T", 7)]
        late = [("v", 1), ("v", 3)] + [("k", j) for j in range(4, 8)]
        mm1 = [it for it in proj1 if it[0] in "qkv"]
        kv_list = [it for it in mm1 if it[0] != "q"]
        kv_early = len(kv_list)
        kv_list += late
        NSTEP = 16

        def unit(layer, s):
            if not 0 <= s < NSTEP:
                return None
            if layer == 1 or s < 8:
                return s
            return 8 + (s - 9) // 2 if s % 2 else None

        def diff(layer, s):
            return layer == 0 and s >= 8

        def buffer_of(layer, u):
            return (u % 2, u - 1) if layer == 0 and u >= 8 else (u % 3, u - 2)

        WO_AT, WO_LOADS = [[0, 1], [1, 0]], [[3, 4], [6, 5]]
        FILL_FROM, FILLS = [13, 7], [6, 12]
        WO_BANK = [[0, 1, 6, 7], [2, 3, 6, 7]]

        x_dram = x[0].rearrange("(t p) d -> p t d", p=P)
        out_dram = out[0].rearrange("(t p) d -> p t d", p=P)
        gate_dram = moe_w_gate.rearrange("l e (p c) f -> l e p (c f)", c=C)
        up_dram = moe_w_up.rearrange("l e (p c) f -> l e p (c f)", c=C)
        down_dram = moe_w_down.rearrange("l e (p c) n -> l e p c n", c=FC)

        def jobs_of(eng, l, q):
            _, pair = nc.values_load_multi_w_load_instructions(
                bounds[0:1, l, bass.ds(q, 2)], engines=[eng.engine], min_val=0, max_val=8 * QUARTS)
            return pair

        def load_router(eng, l):
            eng.dma_start(wr[:, :, 0:NG], moe_w_group[l].rearrange("(p c) g -> p c g", c=C)).then_inc(wr_loaded, 16)
            eng.dma_start(wr[:, :, NG:], moe_w_expert[l].rearrange("(p c) g -> p c g", c=C)).then_inc(wr_loaded, 16)

        block = ctx.enter_context(nc.Block())

        @block.sync
        def _(sp):
            def load_stream(slot, dst, src):
                sp.dma_start(dst, src).then_inc(stream_loaded[slot], 16)

            def load_gu(l, q, part, parity, experts=range(2)):
                for e in experts:
                    for k, w in enumerate((gate_dram, up_dram)):
                        sp.dma_start(w_gu[:, GU_AT[parity][part], e, k].rearrange("p c f -> p (c f)"),
                                     w[l, q * LANES + 2 * part + e]).then_inc((gua_loaded, gub_loaded)[part][parity], 16)

            def load_down(l, q, parity):
                for n in range(2):
                    for e in range(LANES):
                        sp.dma_start(w_dn[:, DN_AT, e, :, 512 * n:512 * n + 512],
                                     down_dram[l, q * LANES + e, :, :, 512 * n:512 * n + 512]
                                     ).then_inc(dn_loaded[parity][n], 16)

            w_in = ev_w_in[0].rearrange("(p c) n -> p c n", c=C)
            w_in_sb = [s.rearrange("p (c n) -> p c n", c=C) for s in stream_raw]

            def load_w_out(l, w, half, h):
                v = w[0].rearrange("(c p) n -> p c n", p=P)
                load_stream(h, stream_raw[h].rearrange("p (c n) -> p c n", c=C // 2), v[:, 4 * half:4 * half + 4, :])

            sp.dma_start(xs[:, 0, :], x_dram[:, 0, :]).then_inc(x_loaded[0], 16)
            for n in range(DH):
                if n >= 2:
                    sp.wait_ge(z_ready, 2 * (n - 1))
                if n == 0:
                    for h in range(2):
                        sp.dma_start(w_in_sb[0][:, 4 * h:4 * h + 4, :], w_in[:, 4 * h:4 * h + 4, 0:512]
                                     ).then_inc(w_in_first[h], 16)
                    sp.dma_start(xs[:, 1, :], x_dram[:, 1, :]).then_inc(x_loaded[1], 16)
                else:
                    load_stream(n % 2, w_in_sb[n % 2], w_in[:, :, 512 * n:512 * n + 512])
                if n == 1:
                    load_gu(0, 0, 0, 0, (0,))
                if n == 2:
                    load_gu(0, 0, 0, 0, (1,))
                    sp.dma_start(gain[:, :], ffn_norm[0].partition_broadcast(P)).then_inc(gain_loaded, 16)
                if n == 3:
                    load_gu(0, 0, 1, 0, (0,))
                if n == 4:
                    load_gu(0, 0, 1, 0, (1,))
            sp.wait_ge(z_ready, 2 * 5)
            load_w_out(0, ev_w_out, 0, 0)
            load_down(0, 0, 0)
            sp.wait_ge(z_ready, 2 * 6)
            load_w_out(0, ev_w_out, 1, 1)

            def jobs_before(l, q):
                return sp.value_load(bounds[0:1, l, bass.ds(q, 1)], min_val=1, max_val=8 * QUARTS)

            def experts(l):
                sp.wait_ge(s_ready, NSTEP * l + NSTEP)
                load_gu(l, 1, 1, 1)
                sp.wait_ge(wo_ready, 4 * l + 4)
                load_gu(l, 1, 0, 1)
                sp.wait_ge(bounds_ready[l], 1)
                with sp.Fori(0, QUARTS // 2 - 2) as i:
                    for half in range(2):
                        q = 2 * i + 2 + half
                        before_last = jobs_before(l, q - 1)
                        sp.wait_ge(a_done[l], before_last)
                        load_gu(l, q, 0, half)
                        load_gu(l, q, 1, half)
                        sp.wait_ge(b_done[l], before_last)
                        load_down(l, q - 1, 1 - half)
                for q in (QUARTS - 2, QUARTS - 1):
                    before_last = jobs_before(l, q - 1)
                    sp.wait_ge(a_done[l], before_last)
                    load_gu(l, q, 0, q % 2)
                    sp.wait_ge(b_done[l], before_last)
                    load_down(l, q - 1, 1 - q % 2)
                    load_gu(l, q, 1, q % 2)
                sp.wait_ge(b_done[l], jobs_before(l, QUARTS - 1))
                load_down(l, QUARTS - 1, 1)

            experts(0)
            sp.wait_ge(a_done[0], jobs_before(0, QUARTS))
            load_stream(0, stream_raw[0][:, 0:C * ODN].rearrange("p (c n) -> p c n", c=C),
                        od_w_in[0].rearrange("(p c) n -> p c n", c=C))
            load_stream(1, stream_raw[1][:, 0:2 * QH * NH1].rearrange("p (c n) -> p c n", c=2),
                        od_w_q_up[0].rearrange("(c p) n -> p c n", p=P))
            sp.wait_ge(b_done[0], jobs_before(0, QUARTS))
            sp.dma_start(kv_up_raw, od_w_kv_up[0]).then_inc(kv_up_loaded, 16)
            load_gu(1, 0, 0, 0)
            load_gu(1, 0, 1, 0)
            sp.wait_ge(z1_ready, 2)
            load_w_out(1, od_w_out, 1, 0)
            sp.wait_ge(qmm_ready, 8)
            load_w_out(1, od_w_out, 0, 1)
            sp.wait_ge(kvmm_ready, len(kv_list))
            load_down(1, 0, 0)
            load_router(sp, 1)
            sp.wait_ge(kr_spread, 1)
            sp.dma_start(gain[:, :], ffn_norm[1].partition_broadcast(P)).then_inc(gain_loaded, 16)
            experts(1)
            sp.dma_start(gain[:, :], final_norm.partition_broadcast(P)).then_inc(gain_loaded, 16)
            for t in range(T):
                sp.wait_ge(y_out[t], 1)
                sp.dma_start(out_dram[:, t, :], xs[:, t, :]).then_inc(stored, 16)
            sp.wait_ge(stored, 16 * T)

        @block.gpsimd
        def _(pool):
            g = nc.gpsimd
            steps = [0]

            def then(ins):
                steps[0] += 1
                ins.then_inc(pool_step, 1)
                pool.wait_ge(pool_step, steps[0])

            then(g.memset(ident[:, :], 0.0))
            then(g.affine_select(out=ident[:, :], in_=ident[:, :], compare_op=ALU.not_equal, fill=1.0, base=0,
                                 pattern=[[-1, P]], channel_multiplier=1))
            g.nop().then_inc(ident_made, 1)
            then(g.memset(kP0[64:128, :, 0, :], 0.0))
            then(g.memset(kP0[0:64, :, 1, :], 0.0))
            g.nop().then_inc(kzero, 1)
            then(g.memset(mask[:, :], 0.0))
            then(g.affine_select(out=mask[:, P:2 * P], in_=mask[:, P:2 * P], compare_op=ALU.is_ge,
                                 fill=-BIG, base=0, pattern=[[-1, P]], channel_multiplier=1))
            then(g.memset(tri[:, :], 1.0))
            then(g.affine_select(out=tri[:, :], in_=tri[:, :], compare_op=ALU.is_gt, fill=0.0, base=0,
                                 pattern=[[1, P]], channel_multiplier=-1))
            then(g.memset(ones[:, :], 1.0))
            then(g.memset(before[:, :, :], 1.0))
            then(g.affine_select(out=before[:, :, :], in_=before[:, :, :], compare_op=ALU.is_gt, fill=0.0, base=0,
                                 pattern=[[1, QUARTS + 1], [-1, QUARTS]], channel_multiplier=0))
            then(g.iota(idx[:, :], pattern=[[1, NE]], base=0, channel_multiplier=0,
                        allow_small_or_imprecise_dtypes=True))
            then(g.iota(idx1[:, :], pattern=[[1, NE]], base=1, channel_multiplier=0,
                        allow_small_or_imprecise_dtypes=True))
            then(g.iota(thr[:, :, :], pattern=[[0, QUARTS], [SLOTS, 8]], base=0, channel_multiplier=0,
                        allow_small_or_imprecise_dtypes=True))
            then(g.memset(thr[:, :, 0:1], -1.0))
            g.nop().then_inc(consts, 1)

            def scale_router(l):
                pool.wait_ge(wr_loaded, 32 * (l + 1))
                pool.wait_ge(early_loaded, 16 * 2)
                g.tensor_tensor(wr[:, :, :], wr[:, :, :], bc(gcol[:, 2 * l + 1, :], [P, C, NG + NE], [2]), ALU.mult
                                ).then_inc(wr_ready, 1)

            scale_router(0)
            pool.wait_ge(kr_evac, 2)
            g.tensor_copy(kT1[NOPE:QH, :, :], bc(krT[NOPE:QH, :], [RR, NH1, S], [1])).then_inc(kr_spread, 1)
            pool.wait_ge(kr_spread, 1)
            scale_router(1)

        @block.tensor
        def _(pe):
            mm, tr = nc.tensor.matmul, nc.tensor.transpose

            def keep_clock(products, bank=6):
                for i in range(products):
                    mm(ps[bank][:, :], ident[:, :], xs[:, 0, 0:512], start=True, stop=True)

            def transpose_x(n, t):
                if n == 0:
                    pe.wait_ge(x_loaded[t], 16)
                else:
                    pe.wait_ge(xr[n][t], 2)
                v = xs[:, t, :].rearrange("s (p c) -> s c p", c=C)
                for h in range(2):
                    for j in range(4):
                        i = tr(ps[2 * t + h][:, P * j:P * j + P], v[:, 4 * h + j, :], ident[:, :])
                    i.then_inc(xT_ready, 1)

            def project0():
                w = [s.rearrange("p (c n) -> p c n", c=C) for s in stream_raw]
                for what, i in proj0:
                    if what == "z":
                        n, t = divmod(i, T)
                        if t == 0 and n >= 1:
                            pe.wait_ge(stream_loaded[n % 2], 16 * ((n + 1) // 2))
                        if i == 0:
                            transpose_x(0, 0)
                        if n == 0:
                            pe.wait_ge(hT_ready, 2 * t + 2)
                        if i >= 4 and i - 4 in rope_items:
                            pe.wait_ge(z_roped, rope_items.index(i - 4) + 1)
                        elif i >= 4:
                            pe.wait_ge(v_ready, v_items.index(i - 4) + 1)
                        for c in range(C):
                            if i == 0 and c % 4 == 0:
                                pe.wait_ge(w_in_first[c // 4], 16)
                            if i == 0 and c == 6:
                                transpose_x(0, 1)
                            m = mm(ps[4 + i % 4][:, :], hT[:, c, P * t:P * t + P], w[n % 2][:, c, :],
                                   start=(c == 0), stop=(c == C - 1), skip_group_check=True)
                        m.then_inc(z_ready, 1)
                    elif what == "v":
                        pe.wait_ge(stream_loaded[1], 16 * 3)
                        value_products(i)
                    else:
                        pe.wait_ge(z_roped, i + 1)
                        if i >= 2:
                            pe.wait_ge(qk_evac, i - 1)
                        else:
                            pe.wait_ge(hT_ready, 4)
                        for j in range(4):
                            m = tr(ps[i % 2][:, P * j:P * j + P], rot[i % 2][:, P * j:P * j + P], ident[:, :])
                        m.then_inc(zrT_ready, 1)

            def value_products(which):
                w = stream_raw[1].rearrange("p (c n) -> p c n", c=C)
                for k in which:
                    c, t = divmod(k, T)
                    m = mm(ps[2 + t][:, :], hT[:, c, P * t:P * t + P], w[:, c, :], start=(c == 0), stop=(c == C - 1),
                           skip_group_check=True)
                    if c == C - 1:
                        m.then_inc(z_ready, 1)

            def attention(l):
                for s in range(NSTEP + 3):
                    if s < NSTEP:
                        if s == 0 and l == 0:
                            pe.wait_ge(v_ready, 2)
                            pe.wait_ge(z_roped, 8)
                            pe.wait_ge(qk_evac, 7)
                        if s == 8 and l == 0:
                            pe.wait_ge(qk_evac, 8)
                        if s == FILL_FROM[1] and l == 1:
                            pe.wait_ge(kv_evac, len(kv_list))
                        if s == 0 and l == 1:
                            pe.wait_ge(kv_evac, kv_early)
                            pe.wait_ge(qT_evac, 8)
                            pe.wait_ge(kr_spread, 1)
                        if s >= 2:
                            pe.wait_ge(m_ready, NSTEP * l + s - 1)
                        if l == 0:
                            q, k, K = qT0[:, s // 2, :], kP0[:, s // 2, s % 2, :], P
                        else:
                            q, k, K = qT1[:, s, :], kT1[:, s, :], QH
                        mm(ps[4 + s % 2][:, 0:P], q[0:K, 0:P], k[0:K, 0:P], start=True, stop=True)
                        mm(ps[4 + s % 2][:, P:3 * P], q[0:K, P:S], k[0:K, 0:S], start=True, stop=True
                           ).then_inc(s_ready, 1)
                    if l == 0:
                        value_products(value_products_at(s))
                    elif s < len(late):
                        if s >= 2:
                            pe.wait_ge(kv_evac, kv_early + s - 1)
                        key_value_product(*late[s], ps[2 + s % 2])
                    out_products_between(l, s)
                    u = unit(l, s - 2)
                    if u is not None:
                        pe.wait_ge(p_ready, 12 * l + u + 1)
                        if u >= 2:
                            pe.wait_ge(pT_evac, 12 * l + u - 1)
                        src = prob[(s - 2 - diff(l, s - 2)) % 4]
                        for j in range(3):
                            m = tr(ps[6 + u % 2][:, P * j:P * j + P], src[:, P * j:P * j + P], ident[:, :])
                        m.then_inc(pT_ready, 1)
                    u = unit(l, s - 3)
                    if u is not None:
                        pT = probT[buffer_of(l, u)[0]]
                        if diff(l, s - 3):
                            pe.wait_ge(v_ready, 4)
                            pe.wait_ge(pT_evac, 12 * l + u + 1)
                            h = u - 8
                            o, a = ps[2 + h // 2], 256 * (h % 2)
                            v = vh[:, :, 512 + P * h:512 + P * h + P]
                            mm(o[:, a:a + P], pT[:, 0:P], v[:, 0, :], start=True, stop=True)
                            mm(o[:, a + P:a + 2 * P], pT[:, P:2 * P], v[:, 0, :], start=True, stop=False)
                            mm(o[:, a + P:a + 2 * P], pT[:, 2 * P:3 * P], v[:, 1, :], start=False, stop=True
                               ).then_inc(pv_done, 1)
                        elif u % 2:
                            pe.wait_ge(pT_evac, 12 * l + u + 1)
                            pair = u // 2
                            if pair >= 2:
                                pe.wait_ge(oT_evac, 6 * l + pair - 1)
                            for kt in range(T):
                                for r in range(2):
                                    head = 2 * pair + r
                                    o = ps[pair % 2][64 * r:64 * r + 64, :]
                                    v = vh[:, kt, 64 * head:64 * head + 64]
                                    pT = probT[buffer_of(l, head)[0]]
                                    if kt == 0:
                                        mm(o[:, 0:S], v, pT[:, 0:S], start=True, stop=False)
                                    else:
                                        mm(o[:, P:S], v, pT[:, 2 * P:3 * P], start=False, stop=True
                                           ).then_inc(pv_done, 1)

            def out_product(l, t, n, c):
                w = stream_raw[WO_AT[l][c // 4]].rearrange("p (c n) -> p c n", c=4)
                return mm(ps[WO_BANK[l][2 * t + n]][:, :], oT[:, c, P * t:P * t + P],
                          w[:, c % 4, 512 * n:512 * n + 512], start=(c == 0), stop=(c == C - 1),
                          skip_group_check=True)

            def out_loaded(l, half):
                pe.wait_ge(stream_loaded[WO_AT[l][half]], 16 * WO_LOADS[l][half])

            def out_products_between(l, s):
                if s - FILL_FROM[l] in range(FILLS[l]):
                    c, n = divmod(s - FILL_FROM[l], 2)
                    if n == 0:
                        if c % 4 == 0:
                            out_loaded(l, c // 4)
                        pe.wait_ge(oT_evac, 6 * l + (4 if l == 0 else c + 1))
                    out_product(l, 0, n, c)

            def transpose_differential():
                pe.wait_ge(on_ready, 2)
                for b in range(2):
                    for j in range(4):
                        m = tr(ps[4 + b][:, P * j:P * j + P], on[:, 512 * b + P * j:512 * b + P * j + P], ident[:, :])
                    m.then_inc(onT_ready, 1)

            def rest_of_half0(l):
                for i in range(FILLS[l], 8):
                    out_product(l, 0, i % 2, i // 2)
                pe.wait_ge(pT_evac, 12 * l + (12 if l == 0 else 16))
                for n in range(2):
                    if l == 0 and n == 1:
                        transpose_differential()
                    for c in range(4):
                        out_product(l, 1, n, c)

            def half1(l):
                if FILLS[l] < 9:
                    out_loaded(l, 1)
                pe.wait_ge(oT_evac, 6 * l + (6 if l == 0 else 8))
                for n in range(2):
                    for c in range(4, 8):
                        if 2 * c + n >= FILLS[l]:
                            m = out_product(l, 0, n, c)
                    m.then_inc(wo_ready, 1)
                for c in range(4, 8):
                    m = out_product(l, 1, 0, c)
                m.then_inc(wo_ready, 1)
                transpose_x(2 * l + 1, 0)
                for c in (4, 5):
                    out_product(l, 1, 1, c)
                router_product(l, 0)
                for c in (6, 7):
                    m = out_product(l, 1, 1, c)
                m.then_inc(wo_ready, 1)
                residual(0, 0)

            def residual(t, n):
                mm(ps[2 * t + n][:, :], ident[:, :], xs[:, t, 512 * n:512 * n + 512], start=True, stop=False,
                   skip_group_check=True)

            def router_product(l, t):
                if t == 0:
                    pe.wait_ge(wr_ready, l + 1)
                pe.wait_ge(hT_ready, 6 * l + 4 + t + 1)
                pe.wait_ge(xT_act[l], t + 1)
                for c in range(C):
                    m = mm(ps[4 + t][:, 0:NG + NE], hT[:, c, P * t:P * t + P], wr[:, c, :],
                           start=(c == 0), stop=(c == C - 1))
                m.then_inc(lg_ready[l], 1)

            def transpose_latents(t):
                pe.wait_ge(zn_ready, t + 1)
                for c in range(2):
                    tr(ps[6][:, S * c + P * t:S * c + P * t + P], z1[:, t, P * c:P * c + P], ident[:, :])
                tr(ps[7][:, P * t:P * t + P], z1[:, t, QR:QR + KR], ident[:, :])
                tr(ps[7][0:QH, S + P * t:S + P * t + P], kr_in[:, t, :], ident[:, :]).then_inc(cT_ready, 1)

            def project1():
                pe.wait_ge(stream_loaded[0], 16 * 4)
                w = stream_raw[0][:, 0:C * ODN].rearrange("p (c n) -> p c n", c=C)
                for t in range(T):
                    pe.wait_ge(hT_ready, 6 + 2 * t + 2)
                    for c in range(C):
                        if t == 1 and c == 6:
                            transpose_latents(0)
                        m = mm(ps[4 + t][:, 0:ODN], hT[:, c, P * t:P * t + P], w[:, c, :],
                               start=(c == 0), stop=(c == C - 1), skip_group_check=True)
                    m.then_inc(z1_ready, 1)
                pe.wait_ge(cT_evac, 1)
                wq = stream_raw[1][:, 0:2 * QH * NH1].rearrange("p (c n) -> p c n", c=2)
                for what, i in proj1:
                    if what == "latents":
                        transpose_latents(1)
                        continue
                    if what == "T":
                        pe.wait_ge(q_roped, i + 1)
                        if i >= 2:
                            pe.wait_ge(qT_evac, i - 1)
                        for j in range(4):
                            m = tr(ps[4 + i % 2][0:QH, P * j:P * j + P], rot[i % 2][:, QH * j:QH * j + QH],
                                   ident[:, :])
                        m.then_inc(qrT_ready, 1)
                        continue
                    j = mm1.index((what, i))
                    if j >= 4:
                        w4, i4 = mm1[j - 4]
                        if w4 == "q":
                            pe.wait_ge(q_roped, i4 + 1)
                        else:
                            pe.wait_ge(kv_evac, kv_list.index((w4, i4)) + 1)
                    b = ps[j % 4]
                    if what == "q":
                        if i == 0:
                            pe.wait_ge(stream_loaded[1], 16 * 5)
                        t, g = divmod(i, 4)
                        if i == 4:
                            pe.wait_ge(cT_evac, 2)
                        for c in range(2):
                            m = mm(b[:, 0:4 * QH], cqT[:, c, P * t:P * t + P], wq[:, c, 4 * QH * g:4 * QH * g + 4 * QH],
                                   start=(c == 0), stop=(c == 1))
                        m.then_inc(qmm_ready, 1)
                    else:
                        if (what, i) == kv_list[0]:
                            pe.wait_ge(kv_up_loaded, 16)
                        if (what, i) == kv_list[1]:
                            pe.wait_ge(cT_evac, 2)
                        key_value_product(what, i, b)

            def key_value_product(what, i, b):
                wkv = kv_up_raw.rearrange("p (h k d) -> p h k d", h=NH1, k=2)
                if what == "v":
                    t, n = divmod(i, 2)
                    m = mm(b[:, :], ckvT[:, P * t:P * t + P], wkv[:, 8 * n:8 * n + 8, 1, :], start=True, stop=True)
                else:
                    for r in range(2):
                        m = mm(b[0:NOPE, S * r:S * r + S], wkv[:, 2 * i + r, 0, :], ckvT, start=True, stop=True)
                m.then_inc(kvmm_ready, 1)

            def route(l):
                transpose_x(2 * l + 1, 1)
                residual(0, 1)
                router_product(l, 1)
                residual(1, 0)
                residual(1, 1)
                pe.wait_ge(routed_ready[l], 1)
                mm(ps[5][:, 0:NE], tri[:, :], routed[:, 0, :], start=True, stop=True)
                mm(ps[5][:, NE:2 * NE], ones[:, :], routed[:, 0, :], start=True, stop=False)
                mm(ps[5][:, NE:2 * NE], tri[:, :], routed[:, 1, :], start=False, stop=True)
                mm(ps[5][:, 2 * NE:3 * NE], ones[:, :], routed[:, 0, :], start=True, stop=False)
                mm(ps[5][:, 2 * NE:3 * NE], ones[:, :], routed[:, 1, :], start=False, stop=True
                   ).then_inc(pos_ready[l], 1)
                keep_clock(3)

            def experts(l):
                pe.wait_ge(bounds_ready[l], 1)
                pe.wait_ge(hp_ready[l], 2)
                with pe.Fori(0, QUARTS // 2) as i:
                    for half in range(2):
                        q = 2 * i + half
                        first, end = jobs_of(pe, l, q)
                        gen = 16 * 4 * (QUARTS // 2 * l + 1) + i * (16 * 4)
                        with pe.Fori(first, end) as job:
                            pe.wait_ge(pick_ready[l], job + q + 1)
                            for c in range(C):
                                for t in range(T):
                                    m = mm(ps[4 + c // 4][:, P * (c % 4):P * (c % 4) + P], hp[:, t, P * c:P * c + P],
                                           pick[:, t].rearrange("p e s -> p (e s)"), start=(t == 0), stop=(t == 1))
                                if c % 4 == 3:
                                    m.then_inc(xg_ready[l][c // 4], 1)
                            pe.wait_ge(gua_loaded[half], gen)
                            pe.wait_ge(gub_loaded[half], gen)
                            pe.wait_ge(xgT_a[l], job + 1)
                            for c in range(C):
                                if c == 4:
                                    pe.wait_ge(xgT_d[l], job + 1)
                                for e in range(LANES):
                                    m = mm(ps[6][SLOTS * e:SLOTS * e + SLOTS, :], xgT[:, c, SLOTS * e:SLOTS * e + SLOTS],
                                           w_gu[:, GU_AT[half][e // 2], e % 2, :, c, :], start=(c == 0),
                                           stop=(c == C - 1))
                            m.then_inc(a_done[l], 1)
                            keep_clock(1, 5)
                            pe.wait_ge(hid_ready[l], job + 1)
                            for c in range(FC):
                                m = tr(ps[7][:, P * c:P * c + P], hid[:, c, :], ident[:, :])
                            m.then_inc(hidT_ready[l], 1)
                            keep_clock(1, 5)
                        with pe.Fori(first, end) as job:
                            pe.wait_ge(hidT_sb[l], job + 1)
                            for n in range(2):
                                pe.wait_ge(dn_loaded[half][n], gen)
                                for c in range(FC):
                                    for e in range(LANES):
                                        m = mm(ps[4 + n][SLOTS * e:SLOTS * e + SLOTS, :],
                                               hidT[:, c, SLOTS * e:SLOTS * e + SLOTS],
                                               w_dn[:, DN_AT, e, c, 512 * n:512 * n + 512], start=(c == 0),
                                               stop=(c == FC - 1))
                                m.then_inc((b_half, b_done)[n][l], 1)
                                if n == 0:
                                    pe.wait_ge(pickg_ready[l], job + 1)
                                    for t in range(T):
                                        m = tr(ps[6][:, P * t:P * t + P], pickg[:, t].rearrange("p e s -> p (e s)"),
                                               ident[:, :])
                                    m.then_inc(cT[l], 1)
                            pe.wait_ge(comb_sb[l], job + 1)
                            for n in range(2):
                                pe.wait_ge((y_a, y_d)[n][l], job + 1)
                                for t in range(T):
                                    m = mm(ps[2 * t + n][:, :], comb[:, P * t:P * t + P],
                                           ysb[:, 512 * n:512 * n + 512], start=False, stop=False,
                                           skip_group_check=True)
                                    if n == 1:
                                        m.then_inc((comb0_done, comb_done)[t][l], 1)

            pe.wait_ge(x_loaded[0], 16)
            pe.wait_ge(ident_made, 1)
            project0()
            attention(0)
            rest_of_half0(0)
            half1(0)
            route(0)
            experts(0)
            transpose_x(2, 0)
            transpose_x(2, 1)
            project1()
            attention(1)
            rest_of_half0(1)
            half1(1)
            route(1)
            experts(1)

        @block.scalar
        def _(act):
            A = nc.scalar.activation

            def square_sums(n):
                for t in range(T):
                    if n == 0:
                        act.wait_ge(x_loaded[t], 16)
                    else:
                        act.wait_ge(xr[n][t], 2)
                    A((junk_late if n == 2 else junk)[t], xs[:, t, :], ACT.Square, accum_out=ss[:, t:t + 1]).then_inc(ss_ready, 1)
                    if n in (1, 3):
                        act.wait_ge(xT_ready, 4 * n + 2 * t + 2)
                        nc.scalar.copy(hT[:, 4:8, P * t:P * t + P],
                                       ps[2 * t + 1][:, :].rearrange("p (c s) -> p c s", c=4)
                                       ).then_inc(xT_act[n // 2], 1)
                    act.wait_ge(rec_ready, 2 * n + t + 1)
                    A(rstd[:, t:t + 1], ms[:, t:t + 1], ACT.Sqrt).then_inc(rstd_ready, 1)

            def project0():
                for what, i in proj0:
                    if what == "z" and i in v_items:
                        n, t = divmod(i, T)
                        act.wait_ge(z_ready, i + 1)
                        A(vh[:, t, 0:512], ps[4 + i % 4][:, :], ACT.Identity, scale=rstd[:, t:t + 1]
                          ).then_inc(v_ready, 1)
                    elif what == "T":
                        n, t = divmod(rope_items[i], T)
                        act.wait_ge(zrT_ready, i + 1)
                        b0 = 4 * (n // 3)
                        src = ps[i % 2][:, :].rearrange("p (b s) -> p b s", b=4)
                        if n % 3 == 0:
                            nc.scalar.copy(qT0[:, b0:b0 + 4, P * t:P * t + P], src).then_inc(qk_evac, 1)
                        else:
                            act.wait_ge(kzero, 1)
                            nc.scalar.copy(kP0[0:64, b0:b0 + 4, 0, P * t:P * t + P], src[0:64])
                            nc.scalar.copy(kP0[64:128, b0:b0 + 4, 1, P * t:P * t + P], src[64:128]
                                           ).then_inc(qk_evac, 1)

            def attention(l):
                for s in range(NSTEP + 4):
                    if s < NSTEP:
                        act.wait_ge(m_ready, NSTEP * l + s + 1)
                        k = s % 4
                        A(prob[k][:, 0:P], prob[k][:, 0:P], ACT.Exp, bias=nm[:, k, 0:1], scale=SCALE[l],
                          accum_out=sm[:, k, 0:1])
                        A(prob[k][:, P:3 * P], prob[k][:, P:3 * P], ACT.Exp, bias=nm[:, k, 1:2], scale=SCALE[l],
                          accum_out=sm[:, k, 1:2]).then_inc(e_ready, 1)
                    u = unit(l, s - 2)
                    if u is not None:
                        act.wait_ge(pT_ready, 12 * l + u + 1)
                        buf, used = buffer_of(l, u)
                        if used >= 1:
                            act.wait_ge(pv_done, 12 * l + used)
                        nc.scalar.copy(probT[buf], ps[6 + u % 2][:, 0:3 * P]).then_inc(pT_evac, 1)
                    if l == 1 and s < len(late):
                        key_value_out(*late[s], ps[2 + s % 2])
                    if l == 0 and s in (9, 10):
                        t = s - 9
                        act.wait_ge(z_ready, 11 + t)
                        A(vh[:, t, 512:D], ps[2 + t][:, :], ACT.Identity, scale=rstd[:, t:t + 1]).then_inc(v_ready, 1)
                    u = unit(l, s - 4)
                    if u is not None and diff(l, s - 4):
                        if u % 2:
                            b = (u - 8) // 2
                            act.wait_ge(pv_done, 12 * l + u + 1)
                            if b:
                                act.wait_ge(sso_ready, b)
                            for j in range(4):
                                m = A(tmp_sin[:, P * j:P * j + P], ps[2 + b][:, P * j:P * j + P], ACT.Square,
                                      accum_out=sso[:, 4 * b + j:4 * b + j + 1])
                            m.then_inc(sso_ready, 1)
                    elif u is not None and u % 2:
                        act.wait_ge(pv_done, 12 * l + u + 1)
                        nc.scalar.copy(oT[:, u // 2, :], ps[u // 2 % 2][:, 0:S]).then_inc(oT_evac, 1)

            def project1():
                act.wait_ge(rstd_ready, 2 * 2 + T)

                def latents(t):
                    act.wait_ge(z1_ready, t + 1)
                    A(z1[:, t, :], ps[4 + t][:, 0:ODN], ACT.Identity, scale=rstd[:, t:t + 1]).then_inc(z1_sb, 1)
                    act.wait_ge(z1_sb, t + 1)
                    A(rot[t][:, 0:QR], z1[:, t, 0:QR], ACT.Square, accum_out=ss1[:, t, 0:1])
                    A(rot[t][:, QR:QR + KR], z1[:, t, QR:QR + KR], ACT.Square, accum_out=ss1[:, t, 1:2]
                      ).then_inc(ss1_ready, 1)

                def latent_root(t):
                    act.wait_ge(ms1_ready, t + 1)
                    A(rs1[:, t, :], ms1[:, t, :], ACT.Sqrt).then_inc(rs1_ready, 1)

                def latents_out(t):
                    act.wait_ge(cT_ready, t + 1)
                    for c in range(2):
                        A(cqT[:, c, P * t:P * t + P], ps[6][:, S * c + P * t:S * c + P * t + P], ACT.Identity,
                          scale=gq[:, c:c + 1])
                    A(ckvT[:, P * t:P * t + P], ps[7][:, P * t:P * t + P], ACT.Identity, scale=gkv[:, 0:1]
                      ).then_inc(cT_evac, 1)
                    nc.scalar.copy(krT[NOPE:QH, P * t:P * t + P], ps[7][NOPE:QH, S + P * t:S + P * t + P]
                                   ).then_inc(kr_evac, 1)

                latents(0)
                latent_root(0)
                latents_out(0)
                latents(1)
                latent_root(1)
                for what, i in proj1:
                    if what == "latents":
                        latents_out(1)
                    elif what == "T":
                        t, g = divmod(i, 4)
                        act.wait_ge(qrT_ready, i + 1)
                        nc.scalar.copy(qT1[0:QH, 4 * g:4 * g + 4, P * t:P * t + P],
                                       ps[4 + i % 2][0:QH, :].rearrange("p (b s) -> p b s", b=4)
                                       ).then_inc(qT_evac, 1)
                    elif what != "q":
                        key_value_out(what, i, ps[mm1.index((what, i)) % 4])

            def key_value_out(what, i, b):
                act.wait_ge(kvmm_ready, kv_list.index((what, i)) + 1)
                if what == "v":
                    t, n = divmod(i, 2)
                    nc.scalar.copy(vh[:, t, 512 * n:512 * n + 512], b[:, :]).then_inc(kv_evac, 1)
                else:
                    nc.scalar.copy(kT1[0:NOPE, 2 * i:2 * i + 2, :].rearrange("p h s -> p (h s)"), b[0:NOPE, :]
                                   ).then_inc(kv_evac, 1)

            def route(l):
                act.wait_ge(gmax_ready[l], 1)
                A(lgg[:, :], lgg[:, :], ACT.Exp).then_inc(gexp[l], 1)
                act.wait_ge(emax_ready[l], 1)
                A(ex2, ex2, ACT.Exp).then_inc(eexp[l], 1)
                act.wait_ge(pos_set, l + 1)
                nc.scalar.copy(pos_d, pos).then_inc(pos_copied, 1)

            def experts(l):
                act.wait_ge(bounds_ready[l], 1)
                with act.Fori(0, QUARTS // 2) as i:
                    for half in range(2):
                        q = 2 * i + half
                        first, end = jobs_of(act, l, q)
                        with act.Fori(first, end) as job:
                            act.wait_ge(xg_ready[l][0], job + 1)
                            nc.scalar.copy(xgT[:, 0:4, :].rearrange("p c s -> p (c s)"), ps[4][:, :]
                                           ).then_inc(xgT_a[l], 1)
                            act.wait_ge(a_done[l], job + 1)
                            A(sil, ps[6][:, 0:FF], ACT.Silu).then_inc(silu_done[l], 1)
                            act.wait_ge(hidT_ready[l], job + 1)
                            nc.scalar.copy(hidT_kept[:, bass.ds(act.snap(job % MAX_ROUNDS), 1), :], ps[7][:, 0:256]
                                           ).then_inc(hid_kept[l], 1)
                        with act.Fori(first, end) as job:
                            act.wait_ge(hid_kept[l], job + 1)
                            nc.scalar.copy(hidT[:, :, :].rearrange("p c s -> p (c s)"),
                                           hidT_kept[:, bass.ds(act.snap(job % MAX_ROUNDS), 1), :]
                                           ).then_inc(hidT_sb[l], 1)
                            act.wait_ge(b_half[l], job + 1)
                            nc.scalar.copy(ysb[:, 0:512], ps[4][:, :]).then_inc(y_a[l], 1)
                            act.wait_ge(b_done[l], job + 1)
                A(spare, ones[:, 0:1], ACT.Sqrt)
                jobs = act.value_load(bounds[0:1, l, QUARTS:QUARTS + 1], min_val=1, max_val=8 * QUARTS)
                act.wait_ge(comb0_done[l], jobs)
                if l == LAYERS - 1:
                    final_squares(jobs)
                    return
                for t in range(T):
                    if t == 1:
                        act.wait_ge(comb_done[l], jobs)
                    nc.scalar.copy(xs[:, t, 0:512], ps[2 * t][:, :]).then_inc(xr[2 * l + 2][t], 1)

            def final_squares(jobs):
                for t in range(T):
                    if t == 1:
                        act.wait_ge(comb_done[LAYERS - 1], jobs)
                    for n in range(2):
                        A(junk_final[2 * t + n], ps[2 * t + n][:, :], ACT.Square, accum_out=ssf[:, t, n:n + 1]
                          ).then_inc(sq_done, 1)
                for t in range(T):
                    act.wait_ge(rec_ready, 2 * 2 * LAYERS + t + 1)
                    A(rstd[:, t:t + 1], ms[:, t:t + 1], ACT.Sqrt).then_inc(rstd_ready, 1)
                    if t == 0:
                        act.wait_ge(gained, 2)
                        act.wait_ge(rstd_ready, 2 * 2 * LAYERS + 1)
                        A(xs[:, 0, :], xs[:, 0, :], ACT.Identity, scale=rstd[:, 0:1]).then_inc(y_out[0], 1)

            def small(dst, src, **kw):
                act.dma_start(dst, src, **kw).then_inc(smalls_loaded, 16)

            act.dma_start(gcol[:, 0::2, :], attn_norm.rearrange("l (p c) -> p l c", c=C)).then_inc(gcol_loaded, 16)
            for dst, src in ((gcol[:, 1::2, :], ffn_norm.rearrange("l (p c) -> p l c", c=C)),
                             (rope[:, :, :], rope_tab.rearrange("(t p) f -> p t f", p=P))):
                act.dma_start(dst, src).then_inc(early_loaded, 16)
            load_router(act, 0)
            for k, v in enumerate((ev_lambda_q1, ev_lambda_k1, ev_lambda_q2, ev_lambda_k2)):
                small(lamv[:, k, :], v[0].partition_broadcast(P))
            small(gsub[:, :], ev_subln.rearrange("a p -> p a"), allow_slow_non_contiguous=True)
            small(gq[:, :], od_q_norm[0].rearrange("(c p) -> p c", p=P), allow_slow_non_contiguous=True)
            small(gkv[:, :], od_kv_norm.rearrange("a p -> p a"), allow_slow_non_contiguous=True)
            for l in L2:
                small(br[:, l, 0:NG], moe_b_group[l].partition_broadcast(P))
                small(br[:, l, NG:], moe_b_expert[l].partition_broadcast(P))

            square_sums(0)
            act.wait_ge(lam_sum, 1)
            A(lexp, lsum, ACT.Exp).then_inc(lam_exp, 1)
            project0()
            attention(0)
            act.wait_ge(mso_ready, 1)
            A(rso, mso, ACT.Sqrt).then_inc(rso_ready, 1)
            for b in range(2):
                act.wait_ge(onT_ready, b + 1)
                A(oT[:, 4 + 2 * b:6 + 2 * b, :].rearrange("p h s -> p (h s)"), ps[4 + b][:, :], ACT.Identity,
                  scale=gsub[:, 0:1]).then_inc(oT_evac, 1)
            square_sums(1)
            route(0)
            experts(0)
            square_sums(2)
            project1()
            attention(1)
            square_sums(3)
            route(1)
            experts(1)

        @block.vector
        def _(dve):
            V = nc.vector
            links = [0]

            def link(ins):
                links[0] += 1
                ins.then_inc(chain, 1)
                dve.wait_ge(chain, links[0])

            def norm(n):
                if n == 0:
                    dve.wait_ge(gcol_loaded, 16)
                for t in range(T):
                    norm_tile(n, t)

            def norm_tile(n, t):
                if n in (0, 2):
                    for h in range(2):
                        dve.wait_ge(xT_ready, 4 * n + 2 * t + h + 1)
                        V.tensor_tensor(hT[:, 4 * h:4 * h + 4, P * t:P * t + P],
                                        ps[2 * t + h][:, :].rearrange("p (c s) -> p c s", c=4),
                                        bc(gcol[:, n, 4 * h:4 * h + 4], [P, 4, P], [2]), ALU.mult
                                        ).then_inc(hT_ready, 1)
                if n in (1, 3):
                    dve.wait_ge(xT_ready, 4 * n + 2 * t + 1)
                    V.tensor_copy(hT[:, 0:4, P * t:P * t + P],
                                  ps[2 * t][:, :].rearrange("p (c s) -> p c s", c=4)).then_inc(hT_ready, 1)
                dve.wait_ge(ss_ready, 2 * n + t + 1)
                link(V.tensor_scalar(ms[:, t:t + 1], ss[:, t:t + 1], 1.0 / D, EPS, ALU.mult, ALU.add))
                V.reciprocal(ms[:, t:t + 1], ms[:, t:t + 1]).then_inc(rec_ready, 1)

            def for_router(l, t):
                n = 2 * l + 1
                norm_tile(n, t)
                dve.wait_ge(rstd_ready, 2 * n + t + 1)
                if t == 0:
                    dve.wait_ge(gain_loaded, 16 * (l + 1))
                V.scalar_tensor_tensor(hp[:, t, :].rearrange("s (c p) -> s p c", c=C),
                                       xs[:, t, :].rearrange("s (p c) -> s p c", c=C), rstd[:, t:t + 1],
                                       gain[:, :].rearrange("s (p c) -> s p c", c=C), ALU.mult, ALU.mult
                                       ).then_inc(hp_ready[l], 1)

            def rotate(dst, src, cos, sin, width, h):
                a = tmp_cos[:, 0:width].rearrange("p (n k h) -> p n k h", k=2, h=h)
                b = tmp_sin[:, 0:width].rearrange("p (n k h) -> p n k h", k=2, h=h)
                V.tensor_tensor(a, src, cos, ALU.mult)
                link(V.tensor_tensor(b, src, sin, ALU.mult))
                V.tensor_tensor(dst[:, :, 0, :], a[:, :, 0, :], b[:, :, 1, :], ALU.subtract)
                return V.tensor_tensor(dst[:, :, 1, :], a[:, :, 1, :], b[:, :, 0, :], ALU.add)

            def project0():
                dve.wait_ge(rstd_ready, T)
                dve.wait_ge(early_loaded, 16 * 2)
                for t in range(T):
                    i = V.tensor_scalar(rope0[:, t, :, :].rearrange("p k h -> p (k h)"), rope[:, t, 0:2 * HALF],
                                        rstd[:, t:t + 1], None, ALU.mult)
                link(i)
                for r, i in enumerate(rope_items):
                    t = i % T
                    dve.wait_ge(z_ready, i + 1)
                    if r >= 2:
                        dve.wait_ge(zrT_ready, r - 1)
                    if r >= 1:
                        dve.wait_ge(z_roped, r)
                    src = ps[4 + i % 4][:, :].rearrange("p (m h) -> p m h", h=HALF)
                    a = tmp_cos.rearrange("p (m h) -> p m h", h=HALF)
                    b = tmp_sin.rearrange("p (m h) -> p m h", h=HALF)
                    V.tensor_tensor(a, src, bc(rope0[:, t, 0, :], [P, 16, HALF], [1]), ALU.mult)
                    link(V.tensor_tensor(b, src, bc(rope0[:, t, 1, :], [P, 16, HALF], [1]), ALU.mult))
                    d = rot[r % 2].rearrange("p (n k h) -> p n k h", k=2, h=HALF)
                    a = tmp_cos.rearrange("p (n k h) -> p n k h", k=2, h=HALF)
                    b = tmp_sin.rearrange("p (n k h) -> p n k h", k=2, h=HALF)
                    V.tensor_tensor(d[:, :, 0, :], a[:, :, 0, :], b[:, :, 1, :], ALU.subtract)
                    V.tensor_tensor(d[:, :, 1, :], a[:, :, 1, :], b[:, :, 0, :], ALU.add).then_inc(z_roped, 1)

            def attention(l):
                for s in range(NSTEP + 1):
                    if s < NSTEP:
                        k = s % 4
                        dve.wait_ge(s_ready, NSTEP * l + s + 1)
                        if s == 0:
                            if l == 0:
                                dve.wait_ge(zrT_ready, 8)
                            else:
                                dve.wait_ge(qrT_ready, 8)
                                dve.wait_ge(ss1_ready, 2)
                        if s >= 4:
                            u4 = unit(l, s - 4)
                            dve.wait_ge(pT_ready, 12 * l + (u4 if u4 is not None else unit(l, s - 3)) + 1)
                        V.tensor_tensor_reduce(prob[k][:, 0:P], ps[4 + s % 2][:, 0:P], mask[:, P:2 * P], 1.0, -3.0 * BIG,
                                               ALU.add, ALU.max, mx[:, k, 0:1])
                        link(V.tensor_tensor_reduce(prob[k][:, P:3 * P], ps[4 + s % 2][:, P:3 * P], mask[:, 0:2 * P],
                                                    1.0, -3.0 * BIG, ALU.add, ALU.max, mx[:, k, 1:2]))
                        V.tensor_scalar(nm[:, k, :], mx[:, k, :], -SCALE[l], None, ALU.mult).then_inc(m_ready, 1)
                    if s >= 1:
                        j = s - 1
                        k = j % 4
                        dve.wait_ge(e_ready, NSTEP * l + j + 1)
                        link(V.reciprocal(rs[:, k, :], sm[:, k, :]))
                        if diff(l, j) and j % 2:
                            link(V.tensor_scalar(rs[:, k, :], rs[:, k, :], nlam, None, ALU.mult))
                            k0 = (j - 1) % 4
                            V.scalar_tensor_tensor(prob[k0][:, 0:P], prob[k][:, 0:P], rs[:, k, 0:1],
                                                   prob[k0][:, 0:P], ALU.mult, ALU.add)
                            V.scalar_tensor_tensor(prob[k0][:, P:3 * P], prob[k][:, P:3 * P], rs[:, k, 1:2],
                                                   prob[k0][:, P:3 * P], ALU.mult, ALU.add).then_inc(p_ready, 1)
                        else:
                            V.tensor_scalar(prob[k][:, 0:P], prob[k][:, 0:P], rs[:, k, 0:1], None, ALU.mult)
                            i = V.tensor_scalar(prob[k][:, P:3 * P], prob[k][:, P:3 * P], rs[:, k, 1:2], None,
                                                ALU.mult)
                            if diff(l, j):
                                link(i)
                            else:
                                i.then_inc(p_ready, 1)

            def add_residual(l):
                for t in range(T):
                    for n in range(2):
                        dve.wait_ge(wo_ready, 4 * l + 2 * t + n + 1)
                        v = xs[:, t, 512 * n:512 * n + 512]
                        V.tensor_tensor(v, v, ps[WO_BANK[l][2 * t + n]][:, :], ALU.add).then_inc(xr[2 * l + 1][t], 1)
                        if (t, n) == (1, 0):
                            for_router(l, 0)
                for_router(l, 1)

            def project1():
                for t in range(T):
                    dve.wait_ge(ss1_ready, t + 1)
                    V.tensor_scalar(ms1[:, t, 0:1], ss1[:, t, 0:1], 1.0 / QR, EPS, ALU.mult, ALU.add)
                    link(V.tensor_scalar(ms1[:, t, 1:2], ss1[:, t, 1:2], 1.0 / KR, EPS, ALU.mult, ALU.add))
                    V.reciprocal(ms1[:, t, :], ms1[:, t, :]).then_inc(ms1_ready, 1)
                    link(V.memset(kr_in[:, t, :], 0.0))
                    z = z1[:, t, QR + KR:].rearrange("p (n k h) -> p n k h", n=1, k=2)
                    cos = bc(rope[:, t, 64:80], [P, 1, 2, RR // 2], [1, 1])
                    sin = bc(rope[:, t, 80:96], [P, 1, 2, RR // 2], [1, 1])
                    link(rotate(kr_in[:, t, NOPE:].rearrange("p (n k h) -> p n k h", n=1, k=2), z, cos, sin, RR,
                                RR // 2))
                    dve.wait_ge(rs1_ready, t + 1)
                    V.tensor_scalar(z1[:, t, 0:QR], z1[:, t, 0:QR], rs1[:, t, 0:1], None, ALU.mult)
                    V.tensor_scalar(z1[:, t, QR:QR + KR], z1[:, t, QR:QR + KR], rs1[:, t, 1:2], None, ALU.mult
                                    ).then_inc(zn_ready, 1)
                for i in range(8):
                    t = i // 4
                    b = ps[mm1.index(("q", i)) % 4][:, 0:4 * QH].rearrange("p (h d) -> p h d", h=4)
                    d = rot[i % 2][:, 0:4 * QH].rearrange("p (h d) -> p h d", h=4)
                    dve.wait_ge(qmm_ready, i + 1)
                    if i >= 2:
                        dve.wait_ge(qrT_ready, i - 1)
                    if i >= 1:
                        dve.wait_ge(q_roped, i)
                    else:
                        dve.wait_ge(zn_ready, 2)
                    V.tensor_copy(d[:, :, 0:NOPE], b[:, :, 0:NOPE])
                    cos = bc(rope[:, t, 64:80], [P, 4, 2, RR // 2], [1, 1])
                    sin = bc(rope[:, t, 80:96], [P, 4, 2, RR // 2], [1, 1])
                    rotate(d[:, :, NOPE:].rearrange("p h (k e) -> p h k e", k=2),
                           b[:, :, NOPE:].rearrange("p h (k e) -> p h k e", k=2), cos, sin, 4 * RR, RR // 2
                           ).then_inc(q_roped, 1)

            def route(l):
                for t in range(T):
                    dve.wait_ge(lg_ready[l], t + 1)
                    V.scalar_tensor_tensor(lgp[:, t, 0:NG], ps[4 + t][:, 0:NG], rstd[:, t:t + 1],
                                           br[:, l, 0:NG], ALU.mult, ALU.add)
                    i = V.scalar_tensor_tensor(lg[:, t, :], ps[4 + t][:, NG:NG + NE], rstd[:, t:t + 1],
                                               br[:, l, NG:], ALU.mult, ALU.add)
                link(i)
                for t in range(T):
                    i = V.max(top[:, 0, t, :], lgp[:, t, :])
                link(i)
                for t in range(T):
                    V.max_index(where[:, 0, t, :], top[:, 0, t, :], lgp[:, t, :])
                link(V.tensor_tensor(lgg, lgp[:, :, 0:NG], bc(top[:, 0, :, 0], [P, T, NG], [2]), ALU.subtract))
                V.tensor_tensor(other, bc(idx[:, 0:NG], [P, T, NG], [1]), where[:, 0, :, 0:1].to_broadcast([P, T, NG]),
                                ALU.not_equal).then_inc(gmax_ready[l], 1)
                dve.wait_ge(gmax_ready[l], 1)
                for t in range(T):
                    i = V.scalar_tensor_tensor(lge[:, t, :].rearrange("p (g e) -> p g e", g=NG),
                                               bc(other[:, t, :], [P, NG, EPG], [2]), -BIG,
                                               lg[:, t, :].rearrange("p (g e) -> p g e", g=NG), ALU.mult, ALU.add)
                link(i)
                for t in range(T):
                    i = V.max(top[:, 1, t, :], lge[:, t, :])
                link(i)
                for t in range(T):
                    i = V.max_index(where[:, 1, t, :], top[:, 1, t, :], lge[:, t, :])
                link(i)
                V.tensor_tensor(ex2, top[:, 1, :, 1], top[:, 1, :, 0], ALU.subtract).then_inc(emax_ready[l], 1)
                link(V.tensor_tensor(best, bc(idx[:, :], [P, T, 2, NE], [1, 1]), bc(where[:, 1, :, 0:2], [P, T, 2, NE], [3]),
                                     ALU.is_equal))
                V.tensor_tensor(routed, best[:, :, 0, :], best[:, :, 1, :], ALU.add).then_inc(routed_ready[l], 1)
                E3 = [P, T, NE]
                dve.wait_ge(gexp[l], 1)
                link(V.tensor_reduce(gs_, lgg, AX.X, ALU.add))
                dve.wait_ge(eexp[l], 1)
                link(V.tensor_scalar(den, ex2, 1.0, None, ALU.add))
                link(V.tensor_tensor(den, den, gs_, ALU.mult))
                link(V.reciprocal(w1, den))
                link(V.tensor_tensor(w2, w1, ex2, ALU.mult))
                V.tensor_tensor(gate, best[:, :, 0, :], bc(w1, E3, [2]), ALU.mult)
                link(V.tensor_tensor(second, best[:, :, 1, :], bc(w2, E3, [2]), ALU.mult))
                link(V.tensor_tensor(gate, gate, second, ALU.add))
                dve.wait_ge(pos_ready[l], 1)
                link(V.tensor_reduce(cmax, ps[5][0:1, 2 * NE:3 * NE].rearrange("p (q e) -> p q e", e=LANES), AX.X,
                                     ALU.max))
                link(V.tensor_tensor(exceeds, bc(cmax, [1, QUARTS, 8], [2]), thr[:, :, :], ALU.is_gt))
                link(V.tensor_reduce(rnd, exceeds, AX.X, ALU.add))
                link(V.tensor_tensor(cnt_ge[:, :, :], before[:, :, :], bc(rnd, [1, QUARTS + 1, QUARTS], [1]), ALU.mult))
                with nc.allow_low_precision(reason="sums of small whole numbers"):
                    V.tensor_reduce(bounds[:, l, 0:QUARTS + 1], cnt_ge[:, :, :], AX.X, ALU.add
                                    ).then_inc(bounds_ready[l], 1)
                V.scalar_tensor_tensor(pos, ps[5][:, 0:2 * NE].rearrange("p (t e) -> p t e", t=T), 1.0, routed,
                                       ALU.add, ALU.mult).then_inc(pos_set, 1)
                dve.wait_ge(pos_set, l + 1)
                one_hot(pos, slice(0, LANES)).then_inc(pick_ready[l], 1)

            def one_hot(ranks, lanes):
                for t in range(T):
                    m = V.tensor_tensor(pick[:, t], bc(idx1[:, 0:SLOTS], [P, LANES, SLOTS], [1]),
                                        bc(ranks[:, t, lanes], [P, LANES, SLOTS], [2]), ALU.is_equal)
                return m

            def experts(l):
                dve.wait_ge(bounds_ready[l], 1)
                with dve.Fori(0, QUARTS // 2) as i:
                    for half in range(2):
                        q = 2 * i + half
                        first, end = jobs_of(dve, l, q)
                        lanes = bass.ds(q * LANES, LANES)
                        with dve.Fori(first, end) as job:
                            dve.wait_ge(xg_ready[l][1], job + 1)
                            V.tensor_copy(xgT[:, 4:8, :].rearrange("p c s -> p (c s)"), ps[5][:, :]).then_inc(xgT_d[l], 1)
                            dve.wait_ge(pos_copied, l + 1)
                            V.tensor_scalar(pos[:, :, lanes], pos[:, :, lanes], -float(SLOTS), None, ALU.add
                                            ).then_inc(pos_down[l], 1)
                            dve.wait_ge(pos_down[l], job + 1)
                            one_hot(pos, lanes).then_inc(pick_ready[l], 1)
                            dve.wait_ge(silu_done[l], job + 1)
                            V.tensor_tensor(hid[:, :, :].rearrange("s c f -> s f c"),
                                            sil.rearrange("s (f c) -> s f c", c=FC),
                                            ps[6][:, FF:2 * FF].rearrange("s (f c) -> s f c", c=FC), ALU.mult
                                            ).then_inc(hid_ready[l], 1)
                            dve.wait_ge(hid_ready[l], job + 1)
                        with dve.Fori(first, end) as job:
                            one_hot(pos_d, lanes).then_inc(pick_made[l], 1)
                            dve.wait_ge(pick_made[l], job + 1)
                            for t in range(T):
                                m = V.tensor_tensor(pickg[:, t], pick[:, t], bc(gate[:, t, lanes], [P, LANES, SLOTS], [2]),
                                                    ALU.mult)
                            m.then_inc(pickg_ready[l], 1)
                            V.tensor_scalar(pos_d[:, :, lanes], pos_d[:, :, lanes], -float(SLOTS), None, ALU.add)
                            dve.wait_ge(cT[l], job + 1)
                            V.tensor_copy(comb, ps[6][:, 0:256]).then_inc(comb_sb[l], 1)
                            dve.wait_ge(b_done[l], job + 1)
                            V.tensor_copy(ysb[:, 512:1024], ps[5][:, :]).then_inc(y_d[l], 1)
                            dve.wait_ge(y_d[l], job + 1)
                        following = (2 * i + 1) * LANES if half == 0 else dve.snap((2 * i + 2) % QUARTS) * LANES
                        one_hot(pos, bass.ds(following, LANES)).then_inc(pick_ready[l], 1)
                jobs = dve.value_load(bounds[0:1, l, QUARTS:QUARTS + 1], min_val=1, max_val=8 * QUARTS)
                if l == LAYERS - 1:
                    return
                for t in range(T):
                    dve.wait_ge((comb0_done, comb_done)[t][l], jobs)
                    V.tensor_copy(xs[:, t, 512:D], ps[2 * t + 1][:, :]).then_inc(xr[2 * l + 2][t], 1)

            link(V.memset(lgp, -BIG))
            norm(0)
            dve.wait_ge(smalls_loaded, 16 * SMALLS)
            for k in range(2):
                V.tensor_tensor_reduce(lamv[:, 2 * k, :], lamv[:, 2 * k, :], lamv[:, 2 * k + 1, :], 1.0, 0.0, ALU.mult,
                                       ALU.add, lsum[:, k:k + 1])
            V.tensor_scalar(gsub[:, :], gsub[:, :], 1.0 - LAM_INIT, None, ALU.mult).then_inc(lam_sum, 1)
            dve.wait_ge(lam_exp, 1)
            link(V.tensor_tensor(nlam, lexp[:, 1:2], lexp[:, 0:1], ALU.subtract))
            link(V.tensor_scalar(nlam, nlam, -LAM_INIT, None, ALU.add))
            dve.wait_ge(consts, 1)
            project0()
            attention(0)
            dve.wait_ge(sso_ready, 2)
            link(V.tensor_scalar(mso, sso, 1.0 / DV, EPS, ALU.mult, ALU.add))
            V.reciprocal(mso, mso).then_inc(mso_ready, 1)
            dve.wait_ge(rso_ready, 1)
            dve.wait_ge(pT_ready, 12)
            for b in range(2):
                V.tensor_tensor(on[:, 512 * b:512 * b + 512].rearrange("p (i d) -> p i d", i=4),
                                ps[2 + b][:, :].rearrange("p (i d) -> p i d", i=4),
                                bc(rso[:, 4 * b:4 * b + 4], [P, 4, DV], [2]), ALU.mult).then_inc(on_ready, 1)
            add_residual(0)
            route(0)
            experts(0)
            norm(2)
            project1()
            attention(1)
            add_residual(1)
            route(1)
            experts(1)
            dve.wait_ge(gain_loaded, 16 * 3)
            for t in range(T):
                for n in range(2):
                    dve.wait_ge(sq_done, 2 * t + n + 1)
                    V.tensor_tensor(xs[:, t, 512 * n:512 * n + 512], ps[2 * t + n][:, :], gain[:, 512 * n:512 * n + 512],
                                    ALU.mult).then_inc(gained, 1)
                    if n == 0:
                        dve.wait_ge(sq_done, 2 * t + 2)
                        link(V.tensor_tensor(ss[:, t:t + 1], ssf[:, t, 0:1], ssf[:, t, 1:2], ALU.add))
                        link(V.tensor_scalar(ms[:, t:t + 1], ss[:, t:t + 1], 1.0 / D, EPS, ALU.mult, ALU.add))
                        V.reciprocal(ms[:, t:t + 1], ms[:, t:t + 1]).then_inc(rec_ready, 1)
            dve.wait_ge(gained, 4)
            dve.wait_ge(rstd_ready, 2 * 2 * LAYERS + 2)
            V.tensor_scalar(xs[:, 1, :], xs[:, 1, :], rstd[:, 1:2], None, ALU.mult).then_inc(y_out[1], 1)


_INS = ["x", "attn_norm", "ev_w_in", "ev_lambda_q1", "ev_lambda_k1", "ev_lambda_q2", "ev_lambda_k2", "ev_subln",
        "ev_w_out", "od_w_in", "od_q_norm", "od_kv_norm", "od_w_q_up", "od_w_kv_up", "od_w_out", "ffn_norm",
        "moe_w_group", "moe_b_group", "moe_w_expert", "moe_b_expert", "moe_w_gate", "moe_w_up", "moe_w_down",
        "final_norm"]


def kernel(**inputs):
    import numpy as np
    import concourse.bacc as bacc
    from concourse.bass_utils import run_bass_kernel_spmd

    seq = inputs["x"].shape[1]
    pos = np.arange(seq, dtype=np.float32)[:, None]
    cols = []
    for dim in (64, 32):
        inv = (1.0 / (10000.0 ** (np.arange(0, dim, 2, dtype=np.float32) / dim))).astype(np.float32)
        ang = pos * inv[None, :]
        cols += [np.cos(ang), np.sin(ang)]
    tab = np.concatenate(cols, axis=1).astype(np.float32)

    nc = bacc.Bacc("TRN2", target_bir_lowering=False, num_devices=1)
    arrays, args = {}, []
    for name in _INS:
        a = np.ascontiguousarray(inputs[name])
        arrays[f"in_{name}"] = a
        args.append(nc.dram_tensor(f"in_{name}", a.shape, mybir.dt.from_np(a.dtype), kind="ExternalInput").ap())
    arrays["rope_tab"] = tab
    args.append(nc.dram_tensor("rope_tab", tab.shape, F32, kind="ExternalInput").ap())
    args.append(nc.dram_tensor("out_y", tuple(inputs["x"].shape), F32, kind="ExternalOutput").ap())
    trunk(nc, *args)
    r = run_bass_kernel_spmd(nc, [arrays], core_ids=[0])
    return r.results[0]["out_y"]
```
